# Optimizing a Trainium2 kernel written in Bass

```python
import jax, jax.numpy as jnp
from jax import lax
import numpy as np

D_MODEL = 1024
BATCH = 1
SEQ = 512
DEPTH = 1

GLA_HEADS = 4
GLA_DK = 128
GLA_DV = 128
GLA_RANK = 16
GLA_TAU = 16.0
GLA_CHUNK = 64
CONV_CH = D_MODEL // 2
CONV_K = 3
SWA_Q_HEADS = 8
SWA_KV_HEADS = 2
SWA_HEAD_DIM = 64
SWA_WINDOW = 128
D_FF = 2816
FFN_CONV_K = 3
N_BRANCH = 3
EPS = 1e-6

MIX_SIZES = (
    GLA_HEADS * GLA_DK,
    GLA_HEADS * GLA_DK,
    GLA_HEADS * GLA_DV,
    GLA_HEADS * GLA_DV,
    GLA_RANK,
    CONV_CH,
    CONV_CH,
    CONV_CH,
    SWA_Q_HEADS * SWA_HEAD_DIM,
    SWA_KV_HEADS * SWA_HEAD_DIM,
    SWA_KV_HEADS * SWA_HEAD_DIM,
    N_BRANCH * D_MODEL,
)
D_IN_TOTAL = sum(MIX_SIZES)


def rmsnorm(x, g):
    xf = x.astype(jnp.float32)
    y = xf * lax.rsqrt(jnp.mean(xf * xf, axis=-1, keepdims=True) + EPS)
    return (y * g.astype(jnp.float32)).astype(x.dtype)

def split_columns(z):
    out = []
    off = 0
    for n in MIX_SIZES:
        out.append(z[..., off:off + n])
        off += n
    return out

def causal_dwconv(u, w):
    K = w.shape[0]
    S = u.shape[1]
    up = jnp.pad(u, ((0, 0), (K - 1, 0), (0, 0)))
    y = up[:, 0:S] * w[0]
    for i in range(1, K):
        y = y + up[:, i:i + S] * w[i]
    return y

def alibi_slopes(n_heads):
    return jnp.exp2(-(8.0 / n_heads) * jnp.arange(1, n_heads + 1, dtype=jnp.float32))

def gla_chunked(q, k, v, log_a):
    f32 = jnp.float32
    Bsz, S, H, dk = q.shape
    dv = v.shape[-1]
    C = GLA_CHUNK
    N = S // C
    q = (q.astype(f32) * dk ** -0.5).reshape(Bsz, N, C, H, dk)
    k = k.astype(f32).reshape(Bsz, N, C, H, dk)
    v = v.astype(f32).reshape(Bsz, N, C, H, dv)
    b = jnp.cumsum(log_a.astype(f32).reshape(Bsz, N, C, H, dk), axis=2)
    b_ref = b[:, :, C // 2 - 1:C // 2]
    b_last = b[:, :, C - 1:]
    causal = jnp.tril(jnp.ones((C, C), dtype=bool))
    attn = jnp.einsum('bnihk,bnjhk->bnhij', q * jnp.exp(b - b_ref), k * jnp.exp(b_ref - b))
    attn = jnp.where(causal, attn, 0.0)
    o_intra = jnp.einsum('bnhij,bnjhv->bnihv', attn, v)
    kv = jnp.einsum('bnjhk,bnjhv->bnhkv', k * jnp.exp(b_last - b), v)
    decay = jnp.exp(b_last[:, :, 0])

    def step(state, inp):
        d, kv_n = inp
        return d[..., None] * state + kv_n, state

    s0 = jnp.zeros((Bsz, H, dk, dv), f32)
    _, s_prev = lax.scan(step, s0, (jnp.moveaxis(decay, 1, 0), jnp.moveaxis(kv, 1, 0)))
    s_prev = jnp.moveaxis(s_prev, 0, 1)
    o_inter = jnp.einsum('bnihk,bnhkv->bnihv', q * jnp.exp(b), s_prev)
    return (o_intra + o_inter).reshape(Bsz, S, H, dv)

def swa_sink_attention(q, k, v, sinks, slopes):
    f32 = jnp.float32
    Bsz, S, Hq, hd = q.shape
    Hkv = k.shape[2]
    G = Hq // Hkv
    W = SWA_WINDOW
    Nb = S // W
    qb = (q.astype(f32) * hd ** -0.5).reshape(Bsz, Nb, W, Hkv, G, hd)

    def windows(t):
        tp = jnp.pad(t.astype(f32), ((0, 0), (W, 0), (0, 0), (0, 0))).reshape(Bsz, Nb + 1, W, Hkv, hd)
        return jnp.concatenate([tp[:, :-1], tp[:, 1:]], axis=2)

    kw = windows(k)
    vw = windows(v)
    scores = jnp.einsum('bnqhgd,bnkhd->bnhgqk', qb, kw)
    iq = jnp.arange(W)[:, None]
    jk = jnp.arange(2 * W)[None, :]
    dist = W + iq - jk
    blk = jnp.arange(Nb)[:, None, None]
    valid = (dist >= 0) & (dist < W) & (blk * W - W + jk >= 0)
    alibi = -slopes.reshape(Hkv, G)[:, :, None, None] * dist.astype(f32)
    logits = jnp.where(valid[None, :, None, None], scores + alibi, -jnp.inf)
    sink = sinks.astype(f32).reshape(Hkv, G)[None, None, :, :, None]
    m = jnp.maximum(logits.max(axis=-1), sink)
    p = jnp.exp(logits - m[..., None])
    denom = p.sum(axis=-1) + jnp.exp(sink - m)
    o = jnp.einsum('bnhgqk,bnkhd->bnqhgd', p, vw) / jnp.moveaxis(denom, 4, 2)[..., None]
    return o.reshape(Bsz, S, Hq * hd)

def first_inputs(seed: int = 0) -> dict:
    key = jax.random.key(seed)
    ks = jax.random.split(key, 17)
    f32 = jnp.float32

    def nrm(k, shape, scale):
        return jax.random.normal(k, shape, f32) * scale

    return {
        'x': nrm(ks[0], (BATCH, SEQ, D_MODEL), 1.0),
        'g_mix': 1.0 + nrm(ks[1], (DEPTH, D_MODEL), 0.02),
        'w_in': nrm(ks[2], (DEPTH, D_MODEL, D_IN_TOTAL), D_MODEL ** -0.5),
        'gla_w_alpha': nrm(ks[3], (DEPTH, GLA_RANK, GLA_HEADS * GLA_DK), GLA_RANK ** -0.5),
        'gla_b_alpha': nrm(ks[4], (DEPTH, GLA_HEADS * GLA_DK), 0.02),
        'gla_norm_g': 1.0 + nrm(ks[5], (DEPTH, GLA_HEADS * GLA_DV), 0.02),
        'conv_w': nrm(ks[6], (DEPTH, CONV_K, CONV_CH), CONV_K ** -0.5),
        'swa_sinks': nrm(ks[7], (DEPTH, SWA_Q_HEADS), 0.5),
        'w_gla_o': nrm(ks[8], (DEPTH, GLA_HEADS * GLA_DV, D_MODEL), (GLA_HEADS * GLA_DV) ** -0.5),
        'w_conv_o': nrm(ks[9], (DEPTH, CONV_CH, D_MODEL), CONV_CH ** -0.5),
        'w_swa_o': nrm(ks[10], (DEPTH, SWA_Q_HEADS * SWA_HEAD_DIM, D_MODEL), (SWA_Q_HEADS * SWA_HEAD_DIM) ** -0.5),
        'w_o': nrm(ks[11], (DEPTH, D_MODEL, D_MODEL), D_MODEL ** -0.5),
        'g_ffn': 1.0 + nrm(ks[12], (DEPTH, D_MODEL), 0.02),
        'w_up': nrm(ks[13], (DEPTH, D_MODEL, 2 * D_FF), D_MODEL ** -0.5),
        'ffn_conv_w': nrm(ks[14], (DEPTH, FFN_CONV_K, 2 * D_FF), FFN_CONV_K ** -0.5),
        'w_down': nrm(ks[15], (DEPTH, D_FF, D_MODEL), D_FF ** -0.5),
        'g_final': 1.0 + nrm(ks[16], (D_MODEL,), 0.02),
    }

def first_block(x, g_mix, w_in, gla_w_alpha, gla_b_alpha, gla_norm_g, conv_w, swa_sinks, w_gla_o, w_conv_o, w_swa_o, w_o, g_ffn, w_up, ffn_conv_w, w_down, g_final):
    f32 = jnp.float32
    Bsz, S, _ = x.shape
    slopes = alibi_slopes(SWA_Q_HEADS)
    h = x
    for l in range(DEPTH):
        u = rmsnorm(h, g_mix[l])
        z = u @ w_in[l]
        gq, gk, gv, gr, ga, cx, cb, cc, sq, sk, sv, gates = split_columns(z)

        log_a = jax.nn.log_sigmoid((ga @ gla_w_alpha[l] + gla_b_alpha[l]).astype(f32)) / GLA_TAU
        o = gla_chunked(gq.reshape(Bsz, S, GLA_HEADS, GLA_DK),
                        gk.reshape(Bsz, S, GLA_HEADS, GLA_DK),
                        gv.reshape(Bsz, S, GLA_HEADS, GLA_DV),
                        log_a.reshape(Bsz, S, GLA_HEADS, GLA_DK))
        o = o * lax.rsqrt(jnp.mean(o * o, axis=-1, keepdims=True) + EPS)
        o = o.reshape(Bsz, S, GLA_HEADS * GLA_DV) * gla_norm_g[l].astype(f32)
        y_gla = (o * jax.nn.silu(gr.astype(f32))).astype(x.dtype) @ w_gla_o[l]

        y_conv = (cb * causal_dwconv(cc * cx, conv_w[l])) @ w_conv_o[l]

        o = swa_sink_attention(sq.reshape(Bsz, S, SWA_Q_HEADS, SWA_HEAD_DIM),
                               sk.reshape(Bsz, S, SWA_KV_HEADS, SWA_HEAD_DIM),
                               sv.reshape(Bsz, S, SWA_KV_HEADS, SWA_HEAD_DIM),
                               swa_sinks[l], slopes)
        y_swa = o.astype(x.dtype) @ w_swa_o[l]

        gt = jax.nn.sigmoid(gates)
        merged = (gt[..., :D_MODEL] * y_gla
                  + gt[..., D_MODEL:2 * D_MODEL] * y_conv
                  + gt[..., 2 * D_MODEL:] * y_swa)
        h = h + merged @ w_o[l]

        u = rmsnorm(h, g_ffn[l])
        hid = causal_dwconv(u @ w_up[l], ffn_conv_w[l])
        h = h + (jax.nn.silu(hid[..., :D_FF]) * hid[..., D_FF:]) @ w_down[l]
    return rmsnorm(h, g_final)


DEPTH_2 = 2

ATTN_HEADS = 8
ATTN_HEAD_DIM = 64
ATTN_WIDTH = ATTN_HEADS * ATTN_HEAD_DIM
IDX_HEADS = 4
IDX_HEAD_DIM = 64
MAX_TOPK = 256
Q_BLOCK = 128
HGRN_HEADS = 4
HGRN_KEY_DIM = 128
HGRN_VAL_DIM = 128
HGRN_F_WIDTH = HGRN_HEADS * HGRN_KEY_DIM
HGRN_WIDTH = HGRN_HEADS * HGRN_VAL_DIM
HGRN_CHUNK = 64
D_FF_2 = -(-8 * D_MODEL // (3 * 256)) * 256
ROPE_THETA = 10000.0
IN_WIDTHS = (ATTN_WIDTH, ATTN_WIDTH, ATTN_WIDTH,
             IDX_HEADS * IDX_HEAD_DIM, IDX_HEAD_DIM, IDX_HEADS,
             HGRN_F_WIDTH, HGRN_F_WIDTH, HGRN_WIDTH, HGRN_WIDTH,
             D_MODEL, D_MODEL)
D_IN = sum(IN_WIDTHS)


def rmsnorm_2(x, g):
    xf = x.astype(jnp.float32)
    xf = xf * lax.rsqrt(jnp.mean(xf * xf, axis=-1, keepdims=True) + EPS)
    return xf.astype(x.dtype) * g

def rope_tables(positions, dim):
    inv = ROPE_THETA ** (-jnp.arange(0, dim, 2, dtype=jnp.float32) / dim)
    ang = positions.astype(jnp.float32)[..., None] * inv
    return jnp.cos(ang)[:, :, None, :], jnp.sin(ang)[:, :, None, :]

def apply_rope(x, cos, sin):
    half = x.shape[-1] // 2
    x1 = x[..., :half].astype(jnp.float32)
    x2 = x[..., half:].astype(jnp.float32)
    return jnp.concatenate([x1 * cos - x2 * sin, x2 * cos + x1 * sin], axis=-1).astype(x.dtype)

def dsa_attention(q, k, v, qi, ki, wi):
    B, T, H, Dh = q.shape
    topk = min(MAX_TOPK, T // 4)
    nb = T // Q_BLOCK
    scale = Dh ** -0.5
    key_pos = jnp.arange(T)
    ki32 = ki.astype(jnp.float32)
    gather = jax.vmap(lambda a, i: a[i])

    def to_blocks(a):
        return a.reshape((B, nb, Q_BLOCK) + a.shape[2:]).swapaxes(0, 1)

    def block_fn(args):
        qb, qib, wib, start = args
        qpos = start + jnp.arange(Q_BLOCK)
        visible = key_pos[None, :] <= qpos[:, None]
        rel = jax.nn.relu(jnp.einsum('bqhd,bsd->bqhs', qib.astype(jnp.float32), ki32))
        score = jnp.einsum('bqh,bqhs->bqs', wib.astype(jnp.float32), rel)
        score = jnp.where(visible[None], score, -jnp.inf)
        _, idx = lax.top_k(score, topk)
        k_sel = gather(k, idx).astype(jnp.float32)
        v_sel = gather(v, idx).astype(jnp.float32)
        logits = jnp.einsum('bqhd,bqkhd->bhqk', qb.astype(jnp.float32), k_sel) * scale
        valid = idx <= qpos[None, :, None]
        logits = jnp.where(valid[:, None], logits, -jnp.inf)
        p = jax.nn.softmax(logits, axis=-1)
        return jnp.einsum('bhqk,bqkhd->bqhd', p, v_sel).astype(q.dtype)

    starts = jnp.arange(nb) * Q_BLOCK
    out = lax.map(block_fn, (to_blocks(q), to_blocks(qi), to_blocks(wi), starts))
    return out.swapaxes(0, 1).reshape(B, T, H * Dh)

def hgrn2_chunked(q, k, v, log_f):
    B, T, H, dk = q.shape
    dv = v.shape[-1]
    C = HGRN_CHUNK
    nc = T // C

    def chunks(a):
        return a.reshape(B, nc, C, H, a.shape[-1]).transpose(1, 0, 3, 2, 4)

    b = jnp.cumsum(chunks(log_f), axis=3)
    causal = jnp.tril(jnp.ones((C, C), dtype=bool))

    def step(S, xs):
        qc, kc, vc, bc = xs
        inter = jnp.einsum('bhtd,bhde->bhte', qc * jnp.exp(bc), S)
        diff = bc[:, :, :, None, :] - bc[:, :, None, :, :]
        decay = jnp.exp(jnp.where(causal[:, :, None], diff, -jnp.inf))
        A = jnp.einsum('bhtd,bhsd,bhtsd->bhts', qc, kc, decay)
        intra = jnp.einsum('bhts,bhse->bhte', A, vc)
        b_last = bc[:, :, -1:, :]
        S = jnp.exp(b_last[:, :, 0, :])[..., None] * S + jnp.einsum(
            'bhsd,bhse->bhde', kc * jnp.exp(b_last - bc), vc)
        return S, inter + intra

    S0 = jnp.zeros((B, H, dk, dv), jnp.float32)
    _, o = lax.scan(step, S0, (chunks(q), chunks(k), chunks(v), b))
    return o.transpose(1, 0, 3, 2, 4).reshape(B, T, H, dv)

def second_inputs(seed: int = 0) -> dict:
    key = jax.random.key(seed)
    ks = jax.random.split(key, 16)
    f32 = jnp.float32
    x = jax.random.normal(ks[0], (BATCH, SEQ, D_MODEL), f32)
    offset = jax.random.randint(ks[1], (BATCH, 1), 0, 4096, dtype=jnp.int32)
    positions = offset + jnp.arange(SEQ, dtype=jnp.int32)[None, :]
    res_scale = (2 * DEPTH_2) ** -0.5
    w_in = jax.random.normal(ks[2], (DEPTH_2, D_MODEL, D_IN), f32) * D_MODEL ** -0.5
    w_proj_attn = jax.random.normal(ks[3], (DEPTH_2, ATTN_WIDTH, D_MODEL), f32) * ATTN_WIDTH ** -0.5
    w_proj_hgrn = jax.random.normal(ks[4], (DEPTH_2, HGRN_WIDTH, D_MODEL), f32) * HGRN_WIDTH ** -0.5
    w_out = jax.random.normal(ks[5], (DEPTH_2, D_MODEL, D_MODEL), f32) * D_MODEL ** -0.5 * res_scale
    norm_mix = 1.0 + 0.02 * jax.random.normal(ks[6], (DEPTH_2, D_MODEL), f32)
    norm_ffn = 1.0 + 0.02 * jax.random.normal(ks[7], (DEPTH_2, D_MODEL), f32)
    q_norm = 1.0 + 0.02 * jax.random.normal(ks[8], (DEPTH_2, ATTN_HEAD_DIM), f32)
    k_norm = 1.0 + 0.02 * jax.random.normal(ks[9], (DEPTH_2, ATTN_HEAD_DIM), f32)
    hgrn_norm = 1.0 + 0.02 * jax.random.normal(ks[10], (DEPTH_2, HGRN_VAL_DIM), f32)
    hgrn_lower_bound = 0.5 * jax.random.normal(ks[11], (DEPTH_2, HGRN_F_WIDTH), f32)
    w_ffn_in = jax.random.normal(ks[12], (DEPTH_2, D_MODEL, 2 * D_FF_2), f32) * D_MODEL ** -0.5
    w_ffn_out = jax.random.normal(ks[13], (DEPTH_2, D_FF_2, D_MODEL), f32) * D_FF_2 ** -0.5 * res_scale
    return {"x": x, "positions": positions, "w_in": w_in, "w_proj_attn": w_proj_attn,
            "w_proj_hgrn": w_proj_hgrn, "w_out": w_out, "norm_mix": norm_mix, "norm_ffn": norm_ffn,
            "q_norm": q_norm, "k_norm": k_norm, "hgrn_norm": hgrn_norm,
            "hgrn_lower_bound": hgrn_lower_bound, "w_ffn_in": w_ffn_in, "w_ffn_out": w_ffn_out}

def second_block(x, positions, w_in, w_proj_attn, w_proj_hgrn, w_out, norm_mix, norm_ffn,
              q_norm, k_norm, hgrn_norm, hgrn_lower_bound, w_ffn_in, w_ffn_out):
    B, T, _ = x.shape
    cos, sin = rope_tables(positions, ATTN_HEAD_DIM)
    split_points = list(np.cumsum(IN_WIDTHS)[:-1])
    lb_all = jnp.cumsum(jax.nn.softmax(hgrn_lower_bound.astype(jnp.float32), axis=0), axis=0)
    lb_all = lb_all - lb_all[:1]
    for l in range(DEPTH_2):
        h = rmsnorm_2(x, norm_mix[l])
        proj = h @ w_in[l]
        aq, ak, av, iq, ik, iw, hq, hf, hi, hg, ga, gb = jnp.split(proj, split_points, axis=-1)
        aq = apply_rope(rmsnorm_2(aq.reshape(B, T, ATTN_HEADS, ATTN_HEAD_DIM), q_norm[l]), cos, sin)
        ak = apply_rope(rmsnorm_2(ak.reshape(B, T, ATTN_HEADS, ATTN_HEAD_DIM), k_norm[l]), cos, sin)
        av = av.reshape(B, T, ATTN_HEADS, ATTN_HEAD_DIM)
        iq = apply_rope(iq.reshape(B, T, IDX_HEADS, IDX_HEAD_DIM), cos, sin) * (IDX_HEAD_DIM ** -0.5)
        ik = apply_rope(ik[:, :, None, :], cos, sin)[:, :, 0, :]
        iw = iw * (IDX_HEADS ** -0.5)
        y_attn = dsa_attention(aq, ak, av, iq, ik, iw)
        lb = lb_all[l].reshape(HGRN_HEADS, HGRN_KEY_DIM)
        hf32 = hf.astype(jnp.float32).reshape(B, T, HGRN_HEADS, HGRN_KEY_DIM)
        log_f = jnp.logaddexp(jnp.log(lb), jnp.log1p(-lb) + jax.nn.log_sigmoid(hf32))
        k_in = -jnp.expm1(log_f)
        q_h = jax.nn.silu(hq.astype(jnp.float32)).reshape(B, T, HGRN_HEADS, HGRN_KEY_DIM)
        v_h = hi.astype(jnp.float32).reshape(B, T, HGRN_HEADS, HGRN_VAL_DIM)
        o = hgrn2_chunked(q_h, k_in, v_h, log_f).astype(x.dtype)
        o = rmsnorm_2(o, hgrn_norm[l]) * jax.nn.silu(hg.reshape(B, T, HGRN_HEADS, HGRN_VAL_DIM))
        y_hgrn = o.reshape(B, T, HGRN_WIDTH)
        merged = jax.nn.sigmoid(ga) * (y_attn @ w_proj_attn[l]) + jax.nn.sigmoid(gb) * (y_hgrn @ w_proj_hgrn[l])
        x = x + merged @ w_out[l]
        h = rmsnorm_2(x, norm_ffn[l])
        g, u = jnp.split(h @ w_ffn_in[l], 2, axis=-1)
        x = x + (jax.nn.silu(g) * u) @ w_ffn_out[l]
    return x


def setup_inputs(seed=0):
    out = dict(first_inputs(seed))
    for name, value in second_inputs(seed + 1).items():
        if name != "x":
            out[name + "_2"] = value
    return out


def reference(
    x, g_mix, w_in, gla_w_alpha, gla_b_alpha, gla_norm_g, conv_w, swa_sinks, w_gla_o, w_conv_o,
    w_swa_o, w_o, g_ffn, w_up, ffn_conv_w, w_down, g_final, positions_2, w_in_2, w_proj_attn_2,
    w_proj_hgrn_2, w_out_2, norm_mix_2, norm_ffn_2, q_norm_2, k_norm_2, hgrn_norm_2,
    hgrn_lower_bound_2, w_ffn_in_2, w_ffn_out_2,
):
    x = first_block(
        x, g_mix, w_in, gla_w_alpha, gla_b_alpha, gla_norm_g, conv_w, swa_sinks, w_gla_o,
        w_conv_o, w_swa_o, w_o, g_ffn, w_up, ffn_conv_w, w_down, g_final,
    )
    return second_block(
        x, positions_2, w_in_2, w_proj_attn_2, w_proj_hgrn_2, w_out_2, norm_mix_2, norm_ffn_2,
        q_norm_2, k_norm_2, hgrn_norm_2, hgrn_lower_bound_2, w_ffn_in_2, w_ffn_out_2,
    )


_drawn_inputs = setup_inputs


def setup_inputs(seed=0):
    import zlib

    import numpy as np

    out = dict(_drawn_inputs(seed))
    spreads = {}
    factors = {'gla_b_alpha': 8.0,
     'gla_norm_g': 7.172,
     'swa_sinks': 8.0,
     'g_ffn': 3.686,
     'norm_mix_2': 5.458,
     'norm_ffn_2': 4.767,
     'q_norm_2': 8.0,
     'k_norm_2': 8.0,
     'hgrn_norm_2': 8.0,
     'hgrn_lower_bound_2': 6.152}
    for name, (base, spread) in spreads.items():
        noise = np.random.default_rng([zlib.crc32(name.encode()), seed]).standard_normal(out[name].shape)
        drawn = base * np.exp(spread * noise) if base else spread * noise
        out[name] = __import__('jax').numpy.asarray(drawn.astype(out[name].dtype))
    for name, factor in factors.items():
        out[name] = (out[name] * factor).astype(out[name].dtype)
    return out
```

```python
from contextlib import ExitStack

import concourse.bass as bass
from concourse import mybir
import numpy as np

F32 = mybir.dt.float32
F32R = mybir.dt.float32r
I32 = mybir.dt.int32
U8 = mybir.dt.uint8
ALU = mybir.AluOpType
ACT = mybir.ActivationFunctionType
AX = mybir.AxisListType.X

P = 128
T = 512
NT = T // P
D = 1024
DC = D // P
EPS = 1e-6
H = 4
MIX = 512
MC = MIX // P
RANK = 16
GLA_TAU = 16.0
D_FF = 2816
FC = D_FF // P
FFN_PAIRS = FC // 2
THIRDS = (4, 4, 3)
AH = 8
HD = 64
LAYERS = 2
TOPK = 128
LEVELS = 7
NEG = -1.0e30
TAKEN = -3.0e38
FAR = 1.0e30

C_GQ, C_GK, C_GV, C_GR, C_GA = 0, 512, 1024, 1536, 2048
C_CX = C_GA + RANK
C_CB, C_CC = C_CX + 512, C_CX + 1024
C_SQ = C_CC + 512
C_SK = C_SQ + 512
C_SV = C_SK + 128
C_GATE = C_SV + 128
C_AQ, C_AK, C_AV, C_IQ, C_IK, C_IW = 0, 512, 1024, 1536, 1792, 1856
C_HQ = C_IW + 4
C_HF, C_HI, C_HG = C_HQ + 512, C_HQ + 1024, C_HQ + 1536
C_G2 = C_HG + 512

V_GMIX, V_GFFN, V_GFIN = 0, 8, 16
V_NMIX, V_NFFN = 24, 40
V_GLAN, V_GLAB = 56, 60
V_CONV = 64
V_HN = 76
V_LB = 78
V_QN, V_KN = 86, 88
N_VEC = 90

K_ID, K_BLK, K_ROT, K_CAUS, K_DIST, K_INV = 0, 128, 256, 384, 512, 768
N_CONST = 769
N_SUM = LEVELS + 2


class Semaphores:
    def __init__(self, sem):
        self.consts_in = sem("consts_in")
        self.x_in = sem("x_in")
        self.raw_in0 = sem("raw_in0")
        self.raw_in1 = sem("raw_in1")
        self.setup_done = sem("setup_done")
        self.trig_done = sem("trig_done")
        self.vec_T = sem("vec_T")
        self.vec_ready = sem("vec_ready")
        self.x_T = sem("x_T")
        self.x_copied = sem("x_copied")
        self.hi_done = sem("hi_done")
        self.lo_done = sem("lo_done")
        self.pair_full = sem("pair_full")
        self.pair_free0 = sem("pair_free0")
        self.pair_free1 = sem("pair_free1")
        self.n_square = sem("n_square")
        self.n_summed = sem("n_summed")
        self.n_root = sem("n_root")
        self.n_normed = sem("n_normed")
        self.n_hi = sem("n_hi")
        self.n_lo = sem("n_lo")
        self.alpha_done = sem("alpha_done")
        self.soft_done = sem("soft_done")
        self.decay_up = sem("decay_up")
        self.ln_done = sem("ln_done")
        self.lg_ready = sem("lg_ready")
        self.lg_T = sem("lg_T")
        self.lt_hi = sem("lt_hi")
        self.lt_lo = sem("lt_lo")
        self.sums_done = sem("sums_done")
        self.dec_done = sem("dec_done")
        self.kd_ready = sem("kd_ready")
        self.kd_T = sem("kd_T")
        self.kdt_done = sem("kdt_done")
        self.lev_ready = sem("lev_ready")
        self.att_done = sem("att_done")
        self.pairs_done = sem("pairs_done")
        self.out_done = sem("out_done")
        self.out_read = sem("out_read")
        self.kv_done = sem("kv_done")
        self.state_done = sem("state_done")
        self.g_square = sem("g_square")
        self.g_summed = sem("g_summed")
        self.g_root = sem("g_root")
        self.g_prod = sem("g_prod")
        self.b_hi = sem("b_hi")
        self.branch_ready = sem("branch_ready")
        self.q_ready = sem("q_ready")
        self.qk_done = sem("qk_done")
        self.logit_done = sem("logit_done")
        self.negmax = sem("negmax")
        self.prob_done = sem("prob_done")
        self.scaled = sem("scaled")
        self.pt_done = sem("pt_done")
        self.pt_read = sem("pt_read")
        self.pv_done = sem("pv_done")
        self.pv_read = sem("pv_read")
        self.r_square = sem("r_square")
        self.r_summed = sem("r_summed")
        self.r_root = sem("r_root")
        self.r_normed = sem("r_normed")
        self.r_turned = sem("r_turned")
        self.rope_done = sem("rope_done")
        self.i_scores = sem("i_scores")
        self.i_relu = sem("i_relu")
        self.i_scored = sem("i_scored")
        self.y_added = sem("y_added")
        self.m_hi = sem("m_hi")
        self.m_lo = sem("m_lo")
        self.f_tap = sem("f_tap")
        self.f_silu = sem("f_silu")
        self.f_mult = sem("f_mult")
        self.f_hi = sem("f_hi")
        self.f_lo = sem("f_lo")
        self.y_T = sem("y_T")
        self.y_out = sem("y_out")
        self.out_stored = sem("out_stored")
        self.act_chain = sem("act_chain")
        self.dve_chain = sem("dve_chain")


class Place:
    def __init__(self):
        self.p = self.q = self.hi = 0


def weight_panels(a):
    out = []

    def cols(w, c0, rows=None):
        r0, nk = rows or (0, w.shape[0] // P)
        v = w[r0 * P:(r0 + nk) * P, :].rearrange("(k p) n -> p k n", p=P)
        width = 256 if nk > 4 or rows else 512
        pairs = 2 if width == 512 or (w.shape[1] > 6000 and c0 == C_SK - HD) else 1
        out.append((v[:, :, c0:c0 + width], nk, width, pairs))

    def ffn(w_up, w_down):
        for step, third in FFN_STEPS:
            i0 = sum(THIRDS[:third])
            if step == "up":
                for i in range(i0, i0 + THIRDS[third]):
                    cols(w_up, 256 * i)
                    cols(w_up, D_FF + 256 * i)
            else:
                for m in range(DC // 2):
                    cols(w_down, 256 * m, (2 * i0, 2 * THIRDS[third]))

    w = a["w_in"][0]
    for c in (C_GK, C_GK + 256, C_GQ, C_GQ + 256, C_GA, C_GV, C_GV + 256, C_GR, C_GR + 256):
        cols(w, c)
    for j in range(2):
        for c in (C_CX, C_CC, C_CB):
            cols(w, c + 256 * j)
    for c in (C_SQ, C_SQ + 256, C_SK - HD, C_SV):
        cols(w, c)
    for j in range(2):
        for b, wy in enumerate(("w_gla_o", "w_conv_o", "w_swa_o")):
            cols(w, C_GATE + b * D + 512 * j)
            cols(w, C_GATE + b * D + 512 * j + 256)
            cols(a[wy][0], 512 * j)
    for m in range(4):
        cols(a["w_o"][0], 256 * m)
    ffn(a["w_up"][0], a["w_down"][0])
    for l in range(LAYERS):
        w = a["w_in_2"][l]
        for c in (C_HF, C_HF + 256, C_HQ, C_HQ + 256, C_HI, C_HI + 256, C_HG, C_HG + 256,
                  C_AQ, C_AQ + 256, C_AK, C_AK + 256, C_IQ, C_IK - HD, C_AV, C_AV + 256):
            cols(w, c)
        for j in range(2):
            for b, wy in enumerate(("w_proj_hgrn_2", "w_proj_attn_2")):
                gate = C_G2 + (1 - b) * D + 512 * j
                cols(w, gate)
                cols(w, gate + 256)
                cols(a[wy][l], 512 * j)
        for m in range(4):
            cols(a["w_out_2"][l], 256 * m)
        ffn(a["w_ffn_in_2"][l], a["w_ffn_out_2"][l])
    return out


FFN_STEPS = (("up", 0), ("up", 1), ("down", 0), ("up", 2), ("down", 1), ("down", 2))
SLOPES = [2.0 ** -(h + 1) for h in range(AH)]


def build_program(nc, a, out):
    panels = weight_panels(a)
    n_panels = len(panels)
    ctx = ExitStack()
    with ctx:
        def sb(name, shape, dt=F32):
            return ctx.enter_context(nc.sbuf_tensor(name, shape, dt))

        xT = sb("xT", [P, DC, T])
        uh = sb("uh", [P, DC, T], F32R)
        ul = sb("ul", [P, DC, T], F32R)
        raw = [sb(f"raw{i}", [P, 2048]) for i in range(2)]
        wh = [sb(f"wh{i}", [P, 2048], F32R) for i in range(2)]
        wl = [sb(f"wl{i}", [P, 2048], F32R) for i in range(2)]
        tmp = [sb(f"tmp{i}", [P, 2, T]) for i in range(4)]
        const = sb("const", [P, N_CONST])
        summask = sb("summask", [P, N_SUM * P], F32R)
        pairmask = sb("pairmask", [P, LEVELS + 1, P], U8)
        ones = sb("ones", [P, P])
        vec = sb("vec", [P, N_VEC])
        fconv = sb("fconv", [P, 3, 2 * FC])
        small = sb("small", [P, 64])
        cosT = sb("cosT", [P, T])
        sinT = sb("sinT", [P, T])
        walpha = sb("walpha", [RANK, MIX])
        sinks = sb("sinks", [P, AH])
        iw = sb("iw", [P, NT, 4])
        ident, blk, rot = const[:, K_ID:K_ID + P], const[:, K_BLK:K_BLK + P], const[:, K_ROT:K_ROT + P]
        causal = const[:, K_CAUS:K_CAUS + P]
        dist = const[:, K_DIST:K_DIST + 2 * P]
        psum = ctx.enter_context(nc.psum_tensor("psum", [P, 8, T], F32))
        pair = [psum[:, 0:2, :], psum[:, 2:4, :]]
        X = [psum[:, 4 + b, :] for b in range(4)]
        X4 = psum[:, 4:8, :]

        arena = (nc.sbuf_base + 63) // 64 * 64

        def at(name, kib, shape, dt=F32):
            return nc.alloc_sbuf_tensor_at(name, shape, dt, offset=arena + int(kib * 1024))

        brh = [at(f"brh{b}", 16 * b, [P, MC, T], F32R) for b in range(3)]
        brl = [at(f"brl{b}", 16 * b + 8, [P, MC, T], F32R) for b in range(3)]
        gk = at("gk", 0, [P, H, T])
        lg = at("lg", 8, [P, H, T])
        gq = at("gq", 16, [P, H, T])
        gv = at("gv", 24, [P, NT, MIX])
        dec = at("dec", 32, [P, H, N_SUM, P])
        lth = at("lth", 50, [P, H, P], F32R)
        ltl = at("ltl", 52, [P, H, P], F32R)
        attT = at("attT", 54, [P, H, P])
        kdt = at("kdt", 56, [P, H, P])
        state = at("state", 58, [P, H, P])
        gaT = at("gaT", 60, [RANK, T])
        sq = at("sq", 48, [P, MC, T])
        sk = at("sk", 56, [P, 2, T])
        sv = at("sv", 60, [P, NT, P])
        aq = at("aq", 32, [P, MC, T])
        ak = at("ak", 40, [P, MC, T])
        av = at("av", 48, [P, NT, MIX])
        iq = at("iq", 56, [P, 2, T])
        ik = at("ik", 60, [P, T])
        score = at("score", 62, [P, T])
        bias = at("bias", 64, [P, NT, T])
        logit = [tmp[0][:, i, :] for i in range(2)]
        prob = [tmp[1][:, i, :] for i in range(2)]
        probT = [tmp[2][:, i, :] for i in range(2)]
        top8 = at("top8", 78, [P, 8])
        stat = at("stat", 78.5, [P, 16])
        merged = at("merged", 48, [P, DC, T])
        fh = [at(f"fh{i}", 32 * i, [P, 8, T], F32R) for i in range(2)]
        fl = [at(f"fl{i}", 32 * i + 16, [P, 8, T], F32R) for i in range(2)]
        xtok = at("xtok", 32, [P, NT, D])
        vrow = at("vrow", 48, [N_VEC, P])
        crow = at("crow", 49, [2 * FC, 3, P])
        mrow = at("mrow", 51, [P, (N_SUM + LEVELS + 1) * P])
        posi = at("posi", 60, [P, T], I32)
        assert arena + 79 * 1024 <= nc.sbuf_usable_end, (arena, nc.sbuf_usable_end)

        S = Semaphores(lambda name: ctx.enter_context(nc.semaphore(name)))
        raw_in = [S.raw_in0, S.raw_in1]
        pair_free = [S.pair_free0, S.pair_free1]
        pairs_after = np.cumsum([x[3] for x in panels]).tolist()
        block = ctx.enter_context(nc.Block())

        class Turns:
            def __init__(self):
                self.at = {}

            def up(self, sem, by=1):
                self.at[sem.name] = self.at.get(sem.name, 0) + by
                return self.at[sem.name]

        def wview(t, p):
            nk, width = panels[p][1:3]
            return t[p % 2][:, 0:nk * width].rearrange("p (k n) -> p k n", k=nk)

        @block.sync
        def _(sp):
            sp.dma_start(xtok[:], a["x"][0].rearrange("(n p) d -> p n d", p=P)).then_inc(S.x_in, 16)
            loads = [(const[:], a["c_const"]), (mrow[:], a["c_masks"]),
                     (crow[:], a["ffn_conv_w"][0].rearrange("k (c p) -> c k p", p=P)),
                     (walpha[:], a["gla_w_alpha"][0]),
                     (sinks[:], a["swa_sinks"].partition_broadcast(P)),
                     (posi[:], a["positions_2"].partition_broadcast(P))]

            def rows(r, src):
                src = src.rearrange("a (c p) -> (a c) p", p=P)
                loads.append((vrow[r:r + src.shape[0], :], src))

            rows(V_GMIX, a["g_mix"])
            rows(V_GFFN, a["g_ffn"])
            loads.append((vrow[V_GFIN:V_GFIN + DC, :], a["g_final"].rearrange("(c p) -> c p", p=P)))
            rows(V_NMIX, a["norm_mix_2"])
            rows(V_NFFN, a["norm_ffn_2"])
            rows(V_GLAN, a["gla_norm_g"])
            rows(V_GLAB, a["gla_b_alpha"])
            rows(V_CONV, a["conv_w"][0])
            rows(V_HN, a["hgrn_norm_2"])
            rows(V_LB, a["hgrn_lower_bound_2"])
            for r, src in ((V_QN, a["q_norm_2"]), (V_KN, a["k_norm_2"])):
                for half in range(2):
                    loads.append((vrow[r:r + LAYERS, HD * half:HD * (half + 1)], src))
            assert len(loads) == N_LOADS
            for dst, src in loads:
                sp.dma_start(dst, src).then_inc(S.consts_in, 16)
            for p, (src, nk, width, _) in enumerate(panels):
                if p >= 2:
                    sp.wait_ge(S.lo_done, p - 1)
                sp.dma_start(wview(raw, p), src).then_inc(raw_in[p % 2], 16)
            for n in range(NT):
                sp.wait_ge(S.y_out, 2 * n + 2)
                sp.dma_start(out[0, n * P:(n + 1) * P, :], xtok[:, n, :]).then_inc(S.out_stored, 16)
            sp.wait_ge(S.out_stored, 16 * NT)

        @block.gpsimd
        def _(pool):
            for p in range(n_panels):
                nk, width = panels[p][1:3]
                pool.wait_ge(S.hi_done, p + 1)
                w = slice(0, nk * width)
                nc.gpsimd.tensor_tensor(wl[p % 2][:, w], raw[p % 2][:, w], wh[p % 2][:, w].bitcast(F32),
                                        ALU.subtract).then_inc(S.lo_done, 1)

        @block.tensor
        def _(pe):
            t = Turns()
            n = Place()

            def panel():
                pe.wait_ge(S.lo_done, n.p + 1)
                n.p += 1
                return wview(wh, n.p - 1), wview(wl, n.p - 1)

            def new_pair():
                if n.q >= 2:
                    pe.wait_ge(pair_free[n.q % 2], n.q // 2)
                n.q += 1
                return pair[(n.q - 1) % 2]

            def products(dst, hs, ls, rh, rl):
                todo = [(x, y) for h, l, r, q in zip(hs, ls, rh, rl) for x, y in ((h, r), (h, q), (l, r))]
                for i, (x, y) in enumerate(todo):
                    mm = nc.tensor.matmul(dst, x, y, start=(i == 0), stop=(i == len(todo) - 1))
                return mm

            def project(xh, xl, offsets=(0, P), w=None):
                h, l = w or panel()
                dst = new_pair()
                ks = range(h.shape[1])
                for i, off in enumerate(offsets):
                    mm = products(dst[:, i, :], [h[:, k, off:off + P] for k in ks], [l[:, k, off:off + P] for k in ks],
                                  [xh[:, k, :] for k in ks], [xl[:, k, :] for k in ks])
                mm.then_inc(S.pair_full, 1)
                return h, l

            def project_tokens(width=256):
                h, l = panel()
                dst = new_pair()
                ks = range(DC)
                for m in range(NT):
                    tok = slice(m * P, (m + 1) * P)
                    mm = products(dst[:, m // 2, 256 * (m % 2):256 * (m % 2) + width],
                                  [uh[:, k, tok] for k in ks], [ul[:, k, tok] for k in ks],
                                  [h[:, k, 0:width] for k in ks], [l[:, k, 0:width] for k in ks])
                mm.then_inc(S.pair_full, 1)

            def norm(split=True):
                for c in range(DC):
                    pe.wait_ge(S.n_square, t.up(S.n_square))
                    nc.tensor.matmul(X[0], ones[:], tmp[c // 2 % 2][:, c % 2, :], start=(c == 0),
                                            stop=(c == DC - 1)).then_inc(S.n_summed, 1)
                if split:
                    pe.wait_ge(S.n_lo, t.up(S.n_lo, DC))

            def core(logs=0):
                pe.wait_ge(S.lg_ready, t.up(S.lg_ready))
                pe.wait_ge(pair_free[(n.q - 1) % 2], (n.q - 1) // 2 + 1)
                if logs:
                    pe.wait_ge(S.ln_done, t.up(S.ln_done, logs))
                for m in range(NT):
                    tok = slice(m * P, (m + 1) * P)
                    if m > 0:
                        pe.wait_ge(S.out_read, t.up(S.out_read))
                    for h in range(H):
                        mm = nc.tensor.transpose(X[0][:, h * P:(h + 1) * P], lg[:, h, tok], ident)
                    mm.then_inc(S.lg_T, 1)
                    pe.wait_ge(S.lt_lo, t.up(S.lt_lo))
                    if m > 0:
                        pe.wait_ge(S.state_done, t.up(S.state_done))
                    for h in range(H):
                        if h > 0:
                            pe.wait_ge(S.dec_done, t.up(S.dec_done))
                        for b in range(3):
                            cols = slice(3 * P * b, 3 * P * (b + 1))
                            for part in (lth, ltl):
                                mm = nc.tensor.matmul(X[1 + b][:, 0:3 * P], part[:, h, :], summask[:, cols],
                                                      start=(part is lth), stop=(part is ltl))
                        mm.then_inc(S.sums_done, 1)
                    pe.wait_ge(S.dec_done, t.up(S.dec_done))
                    pe.wait_ge(S.kd_ready, t.up(S.kd_ready))
                    for h in range(H):
                        mm = nc.tensor.transpose(X[0][:, h * P:(h + 1) * P], dec[:, h, LEVELS + 1, :], ident)
                    mm.then_inc(S.kd_T, 1)
                    for l in range(LEVELS + 1):
                        if l < LEVELS:
                            pe.wait_ge(S.lev_ready, t.up(S.lev_ready))
                        if l > 2:
                            pe.wait_ge(S.pairs_done, t.up(S.pairs_done))
                        for h in range(H):
                            lhs, rhs = (dec[:, h, l, :], dec[:, h, l, :]) if l < LEVELS else (gk[:, h, tok], gq[:, h, tok])
                            mm = nc.tensor.matmul(X[1 + l % 3][:, h * P:(h + 1) * P], lhs, rhs, start=True, stop=True)
                        mm.then_inc(S.att_done, 1)
                    pe.wait_ge(S.pairs_done, t.up(S.pairs_done, 3))
                    pe.wait_ge(S.kdt_done, t.up(S.kdt_done))
                    for h in range(H):
                        v = gv[:, m, h * P:(h + 1) * P]
                        mm = nc.tensor.matmul(X[0][:, h * P:(h + 1) * P], v, attT[:, h, :], start=True, stop=(m == 0))
                        if m > 0:
                            mm = nc.tensor.matmul(X[0][:, h * P:(h + 1) * P], state[:, h, :], dec[:, h, LEVELS, :],
                                                  start=False, stop=True)
                    mm.then_inc(S.out_done, 1)
                    if m < NT - 1:
                        for h in range(H):
                            mm = nc.tensor.matmul(X[1][:, h * P:(h + 1) * P], kdt[:, h, :], gv[:, m, h * P:(h + 1) * P],
                                                  start=True, stop=True)
                        mm.then_inc(S.kv_done, 1)
                pe.wait_ge(S.out_read, t.up(S.out_read))

            def core_post():
                for j in range(2):
                    project(uh, ul)
                    pe.wait_ge(S.g_square, t.up(S.g_square))
                    for i in range(2):
                        mm = nc.tensor.matmul(X[i], ones[:], tmp[1][:, i, :], start=True, stop=True)
                    mm.then_inc(S.g_summed, 1)

            def attention(heads, q, kof, vof, blocks):
                steps = [(m, h) for m in range(NT) for h in range(heads)]

                def qk(i):
                    m, h = steps[i]
                    half = slice(HD * (h % 2), HD * (h % 2 + 1))
                    if i >= 2:
                        pe.wait_ge(S.logit_done, t.up(S.logit_done))
                    b0, b1 = blocks(m)
                    nc.tensor.matmul(X[i % 2][:, 0:(b1 - b0) * P], q[half, h // 2, m * P:(m + 1) * P],
                                            kof(h)[:, b0 * P:b1 * P], start=True, stop=True).then_inc(S.qk_done, 1)

                qk(0)
                for i, (m, h) in enumerate(steps):
                    if i + 1 < len(steps):
                        qk(i + 1)
                    b0, b1 = blocks(m)
                    pe.wait_ge(S.scaled, t.up(S.scaled))
                    for b in range(b1 - b0):
                        mm = nc.tensor.transpose(X[2][:, b * P:(b + 1) * P], prob[i % 2][:, b * P:(b + 1) * P], ident)
                    mm.then_inc(S.pt_done, 1)
                    pe.wait_ge(S.pt_read, t.up(S.pt_read))
                    if h % 2 == 0 and i >= 2:
                        pe.wait_ge(S.pv_read, t.up(S.pv_read))
                    for b in range(b0, b1):
                        mm = nc.tensor.matmul(X[3][HD * (h % 2):HD * (h % 2 + 1), 0:P], vof(h, b),
                                              probT[i % 2][:, (b - b0) * P:(b - b0 + 1) * P],
                                              start=(b == b0), stop=(b == b1 - 1))
                    mm.then_inc(S.pv_done, 1)
                pe.wait_ge(S.pv_read, t.up(S.pv_read))
                pe.wait_ge(S.logit_done, t.up(S.logit_done, 2))

            def index():
                for m in range(1, NT):
                    for h in range(4):
                        i = 4 * (m - 1) + h
                        if i >= 2:
                            pe.wait_ge(S.i_relu, t.up(S.i_relu))
                        half = slice(HD * (h % 2), HD * (h % 2 + 1))
                        nc.tensor.matmul(X[i % 2][:, 0:(m + 1) * P], iq[half, h // 2, m * P:(m + 1) * P],
                                                ik[half, 0:(m + 1) * P], start=True, stop=True).then_inc(S.i_scores, 1)
                pe.wait_ge(S.i_relu, t.up(S.i_relu, 2))

            def merge(branches):
                for j in range(2):
                    for b in branches:
                        project(uh, ul)
                        project(uh, ul)
                        w = panel()
                        if j == 0:
                            pe.wait_ge(S.branch_ready, t.up(S.branch_ready))
                        for off in (0, 256):
                            project(brh[b], brl[b], (off, off + P), w)
                pe.wait_ge(S.m_lo, t.up(S.m_lo, 4))
                for _ in range(4):
                    project(uh, ul)

            def ffn():
                for step, third in FFN_STEPS:
                    if step == "up":
                        for _ in range(2 * THIRDS[third]):
                            project(uh, ul)
                    else:
                        pe.wait_ge(S.f_lo, t.up(S.f_lo, THIRDS[third]))
                        for _ in range(DC // 2):
                            project(fh[third % 2], fl[third % 2])

            pe.wait_ge(S.consts_in, 16 * N_LOADS)
            nc.tensor.transpose(X[0][:, 0:N_VEC], vrow[:], ident[0:N_VEC, 0:N_VEC])
            for k in range(3):
                mm = nc.tensor.transpose(X[1][:, k * 2 * FC:(k + 1) * 2 * FC], crow[:, k, :], ident[0:2 * FC, 0:2 * FC])
            mm.then_inc(S.vec_T, 1)
            pe.wait_ge(S.x_in, 16)
            pe.wait_ge(S.vec_ready, t.up(S.vec_ready))
            for c in range(DC):
                if c >= 4:
                    pe.wait_ge(S.x_copied, t.up(S.x_copied))
                for m in range(NT):
                    mm = nc.tensor.transpose(X[c % 4][:, m * P:(m + 1) * P], xtok[:, m, c * P:(c + 1) * P], ident)
                mm.then_inc(S.x_T, 1)
            pe.wait_ge(S.x_copied, t.up(S.x_copied, 4))

            norm()
            for _ in range(4):
                project(uh, ul)
            project(uh, ul, (0,))
            project_tokens()
            project_tokens()
            pe.wait_ge(pair_free[(n.q - 3) % 2], (n.q - 3) // 2 + 1)
            for c in range(MC):
                mm = nc.tensor.matmul(X[c], walpha[:, c * P:(c + 1) * P], gaT[:], start=True, stop=True)
            mm.then_inc(S.alpha_done, 1)
            core()
            core_post()
            for _ in range(6):
                project(uh, ul)
            project(uh, ul)
            project(uh, ul)
            w = project(uh, ul, (0, HD))
            project(uh, ul, (P,), w)
            project_tokens(P)
            pe.wait_ge(S.q_ready, t.up(S.q_ready))
            pe.wait_ge(pair_free[(n.q - 1) % 2], (n.q - 1) // 2 + 1)
            attention(AH, sq, lambda h: sk[HD * (h % 2):HD * (h % 2 + 1), h // 4, :],
                      lambda h, b: sv[:, b, HD * (h // 4):HD * (h // 4 + 1)], lambda m: (max(m - 1, 0), m + 1))
            merge((0, 1, 2))
            norm()
            ffn()
            norm(split=False)

            for l in range(LAYERS):
                norm()
                for _ in range(4):
                    project(uh, ul)
                project_tokens()
                project_tokens()
                core(2 * l)
                core_post()
                for _ in range(4):
                    project(uh, ul)
                    pe.wait_ge(S.r_square, t.up(S.r_square))
                    for i in range(2):
                        mm = nc.tensor.matmul(X[i], blk, tmp[0][:, i, :], start=True, stop=True)
                    mm.then_inc(S.r_summed, 1)
                    pe.wait_ge(S.r_normed, t.up(S.r_normed))
                    for i in range(2):
                        mm = nc.tensor.matmul(X[2 + i], rot, tmp[2][:, i, :], start=True, stop=True)
                    mm.then_inc(S.r_turned, 1)
                for k in range(2):
                    if k == 0:
                        project(uh, ul)
                    else:
                        h, lo = panel()
                        ks = range(DC)
                        for m in range(NT):
                            tok = slice(m * P, (m + 1) * P)
                            products(X[0][:, 4 * m:4 * m + 4], [uh[:, c, tok] for c in ks], [ul[:, c, tok] for c in ks],
                                     [h[:, c, P:P + 4] for c in ks], [lo[:, c, P:P + 4] for c in ks])
                        project(uh, ul, (HD, 0), (h, lo))
                    pe.wait_ge(S.r_normed, t.up(S.r_normed))
                    for i in range(2 - k):
                        mm = nc.tensor.matmul(X[2 + i], rot, tmp[2][:, i, :], start=True, stop=True)
                    mm.then_inc(S.r_turned, 1)
                project_tokens()
                project_tokens()
                pe.wait_ge(S.q_ready, t.up(S.q_ready))
                pe.wait_ge(pair_free[(n.q - 1) % 2], (n.q - 1) // 2 + 1)
                index()
                attention(AH, aq, lambda h: ak[HD * (h % 2):HD * (h % 2 + 1), h // 2, :],
                          lambda h, b: av[:, b, HD * h:HD * (h + 1)], lambda m: (0, m + 1))
                merge((0, 1))
                norm()
                ffn()

            pe.wait_ge(pair_free[(n.q - 1) % 2], (n.q - 1) // 2 + 1)
            for i in range(2 * NT):
                m, half = i // 2, i % 2
                if i >= 4:
                    pe.wait_ge(S.y_out, t.up(S.y_out))
                for c in range(4):
                    mm = nc.tensor.transpose(X[i % 4][:, c * P:(c + 1) * P], xT[:, 4 * half + c, m * P:(m + 1) * P], ident)
                mm.then_inc(S.y_T, 1)

        @block.scalar
        def _(act):
            t = Turns()
            n = Place()
            fn = nc.scalar.activation

            def ahead(upto):
                while n.hi <= min(upto, n_panels - 1):
                    p = n.hi
                    nk, width = panels[p][1:3]
                    act.wait_ge(raw_in[p % 2], 16 * (p // 2 + 1))
                    if p >= 2:
                        act.wait_ge(S.pair_full, pairs_after[p - 2])
                    nc.scalar.copy(wh[p % 2][:, 0:nk * width], raw[p % 2][:, 0:nk * width]).then_inc(S.hi_done, 1)
                    n.hi += 1

            def next_pair(new_panel=True):
                if new_panel:
                    ahead(n.p + 1)
                    n.p += 1
                n.q += 1
                return pair[(n.q - 1) % 2]

            def norm(split=True):
                for c in range(DC):
                    if c >= 4:
                        act.wait_ge(S.n_summed, t.up(S.n_summed))
                    fn(tmp[c // 2 % 2][:, c % 2, :], xT[:, c, :], ACT.Square).then_inc(S.n_square, 1)
                act.wait_ge(S.n_summed, t.up(S.n_summed, 4))
                fn(tmp[2][:, 0, :], X[0], ACT.Sqrt, bias=small[:, 0:1], scale=1.0 / D).then_inc(S.n_root, 1)
                for c in range(DC):
                    act.wait_ge(S.n_normed, t.up(S.n_normed))
                    if split:
                        nc.scalar.copy(uh[:, c, :], tmp[3][:, c % 2, :]).then_inc(S.n_hi, 1)

            def soft(src, dst, b=None):
                if b is None:
                    fn(dst, src, ACT.Abs).then_inc(S.act_chain, 1)
                    act.wait_ge(S.act_chain, t.up(S.act_chain))
                else:
                    fn(dst[:, 0, :], src[:, 0, :], ACT.Abs, bias=b[:, 0:1])
                    fn(dst[:, 1, :], src[:, 1, :], ACT.Abs, bias=b[:, 1:2]).then_inc(S.act_chain, 1)
                    act.wait_ge(S.act_chain, t.up(S.act_chain))
                fn(dst, dst, ACT.Exp, scale=-1.0).then_inc(S.act_chain, 1)
                act.wait_ge(S.act_chain, t.up(S.act_chain))
                return fn(dst, dst, ACT.Ln, bias=1.0)

            def core(scale):
                for m in range(NT):
                    act.wait_ge(S.lg_T, t.up(S.lg_T))
                    fn(lth[:], X[0].rearrange("p (h f) -> p h f", h=H), ACT.Copy, scale=scale).then_inc(S.lt_hi, 1)
                    for h in range(H):
                        act.wait_ge(S.sums_done, t.up(S.sums_done))
                        fn(dec[:, h, :, :].rearrange("p (b l) t -> p b (l t)", b=3), X4[:, 1:4, 0:3 * P],
                                  ACT.Exp).then_inc(S.dec_done, 1)
                    act.wait_ge(S.kd_T, t.up(S.kd_T))
                    nc.scalar.copy(kdt[:], X[0].rearrange("p (h f) -> p h f", h=H)).then_inc(S.kdt_done, 1)

            def core_post(b):
                act.wait_ge(S.out_read, t.up(S.out_read, NT))
                for j in range(2):
                    heads = slice(2 * j, 2 * j + 2)
                    fn(tmp[1][:], gq[:, heads, :], ACT.Square).then_inc(S.g_square, 1)
                    src = next_pair()
                    act.wait_ge(S.pair_full, n.q)
                    fn(tmp[0][:], src, ACT.Silu).then_inc(pair_free[(n.q - 1) % 2], 1)
                    act.wait_ge(S.g_summed, t.up(S.g_summed))
                    fn(tmp[2][:], X4[:, 0:2, :], ACT.Sqrt, bias=small[:, 0:1], scale=1.0 / P).then_inc(S.g_root, 1)
                    act.wait_ge(S.g_prod, t.up(S.g_prod))
                    nc.scalar.copy(brh[b][:, heads, :], tmp[3][:]).then_inc(S.b_hi, 1)

            def attention(heads, blocks, sink, b):
                steps = [(m, h) for m in range(NT) for h in range(heads)]

                def exps(i):
                    m, h = steps[i]
                    kk = (blocks(m)[1] - blocks(m)[0]) * P
                    st = stat[:, 8 * (i % 2):8 * (i % 2) + 8]
                    act.wait_ge(S.negmax, t.up(S.negmax))
                    if sink:
                        fn(st[:, 3:4], sinks[:, h:h + 1], ACT.Exp, bias=st[:, 1:2])
                    fn(prob[i % 2][:, 0:kk], logit[i % 2][:, 0:kk], ACT.Exp, bias=st[:, 1:2],
                              accum_out=st[:, 2:3]).then_inc(S.prob_done, 1)

                exps(0)
                for i, (m, h) in enumerate(steps):
                    if i + 1 < len(steps):
                        exps(i + 1)
                    kk = (blocks(m)[1] - blocks(m)[0]) * P
                    act.wait_ge(S.pt_done, t.up(S.pt_done))
                    nc.scalar.copy(probT[i % 2][:, 0:kk], X[2][:, 0:kk]).then_inc(S.pt_read, 1)
                act.wait_ge(S.pv_read, t.up(S.pv_read, len(steps) // 2))
                src = sq if sink else aq
                for j in range(2):
                    nc.scalar.copy(brh[b][:, 2 * j:2 * j + 2, :], src[:, 2 * j:2 * j + 2, :]).then_inc(S.b_hi, 1)

            def merge(nb):
                for j in range(2):
                    for b in range(nb):
                        if (j, b) != (0, 0):
                            act.wait_ge(pair_free[(n.q - 1) % 2], (n.q - 1) // 2 + 1)
                        for i in range(2):
                            src = next_pair()
                            act.wait_ge(S.pair_full, n.q)
                            fn(tmp[i][:], src, ACT.Sigmoid).then_inc(pair_free[(n.q - 1) % 2], 1)
                        next_pair()
                        next_pair(False)
                for s in range(4):
                    act.wait_ge(S.y_added, t.up(S.y_added))
                    nc.scalar.copy(uh[:, 2 * s:2 * s + 2, :], merged[:, 2 * s:2 * s + 2, :]).then_inc(S.m_hi, 1)
                for _ in range(4):
                    next_pair()

            def ffn(conv):
                for step, third in FFN_STEPS:
                    i0 = sum(THIRDS[:third])
                    if step == "down":
                        for _ in range(DC // 2):
                            next_pair()
                        continue
                    for i in range(i0, i0 + THIRDS[third]):
                        if conv:
                            for part in range(2):
                                src = next_pair()
                                act.wait_ge(S.pair_full, n.q)
                                for c in range(2):
                                    ch = part * FC + 2 * i + c
                                    ins = fn(tmp[part][:, c, :], src[:, c, :], ACT.Copy, scale=fconv[:, 2, ch:ch + 1])
                                ins.then_inc(S.f_tap, 1)
                            act.wait_ge(pair_free[(n.q - 2) % 2], (n.q - 2) // 2 + 1)
                            fn(tmp[0][:], tmp[0][:], ACT.Silu).then_inc(S.f_silu, 1)
                            act.wait_ge(S.f_mult, t.up(S.f_mult))
                        else:
                            src = next_pair()
                            act.wait_ge(S.pair_full, n.q)
                            fn(tmp[0][:], src, ACT.Silu).then_inc(pair_free[(n.q - 1) % 2], 1)
                            next_pair()
                            act.wait_ge(pair_free[(n.q - 1) % 2], (n.q - 1) // 2 + 1)
                        c = 2 * (i - i0)
                        nc.scalar.copy(fh[third % 2][:, c:c + 2, :], tmp[2][:]).then_inc(S.f_hi, 1)

            def evict(dst, tokens=None, **kw):
                src = next_pair()
                act.wait_ge(S.pair_full, n.q)
                if tokens:
                    src = src.rearrange("p b (x c) -> p b x c", x=2)[:, :, :, 0:tokens]
                    dst = dst.rearrange("p (b x) c -> p b x c", b=2)
                fn(dst, src, ACT.Copy, **kw).then_inc(pair_free[(n.q - 1) % 2], 1)

            ahead(1)
            act.wait_ge(S.setup_done, t.up(S.setup_done))
            fn(sinT[:], tmp[3][:, 0, :], ACT.Sin)
            fn(cosT[:], tmp[3][:, 1, :], ACT.Sin)
            fn(small[:, 1:5], small[:, 11:15], ACT.Sigmoid)
            fn(small[:, 5:9], small[:, 15:19], ACT.Sigmoid).then_inc(S.trig_done, 1)
            act.wait_ge(S.x_copied, t.up(S.x_copied, DC))

            norm()
            next_pair()
            next_pair()
            for j in range(2):
                evict(gq[:, 2 * j:2 * j + 2, :], scale=P ** -0.5)
            next_pair()
            for j in range(2):
                evict(gv[:, :, 256 * j:256 * j + 256], 256)
            act.wait_ge(S.alpha_done, t.up(S.alpha_done))
            for j in range(2):
                soft(X4[:, 2 * j:2 * j + 2, :], tmp[2 * j][:], vec[:, V_GLAB + 2 * j:V_GLAB + 2 * j + 2]).then_inc(S.soft_done, 1)
            core(1.0 / GLA_TAU)
            core_post(0)
            for j in range(2):
                for _ in range(3):
                    next_pair()
                act.wait_ge(pair_free[(n.q - 1) % 2], (n.q - 1) // 2 + 1)
                nc.scalar.copy(brh[1][:, 2 * j:2 * j + 2, :], tmp[3][:]).then_inc(S.b_hi, 1)
            for j in range(2):
                evict(sq[:, 2 * j:2 * j + 2, :], scale=HD ** -0.5)
            next_pair()
            next_pair(False)
            evict(sv[:], P)
            attention(AH, lambda m: (max(m - 1, 0), m + 1), True, 2)
            merge(3)
            act.wait_ge(pair_free[(n.q - 1) % 2], (n.q - 1) // 2 + 1)
            norm()
            ffn(True)
            act.wait_ge(pair_free[(n.q - 1) % 2], (n.q - 1) // 2 + 1)
            norm(split=False)

            for l in range(LAYERS):
                if l:
                    act.wait_ge(pair_free[(n.q - 1) % 2], (n.q - 1) // 2 + 1)
                norm()
                for j in range(2):
                    src = next_pair()
                    act.wait_ge(S.pair_full, n.q)
                    ta, tb = tmp[2 * j], tmp[2 * j + 1]
                    if l == 0:
                        ins = soft(src, ta[:])
                        fn(gk[:, 2 * j:2 * j + 2, :], src, ACT.Sigmoid, scale=-1.0)
                        nc.scalar.copy(small[:, 30:31], small[:, 0:1]).then_inc(S.soft_done, 1)
                    else:
                        fn(ta[:], src, ACT.Sigmoid)
                        fn(tb[:], src, ACT.Sigmoid, scale=-1.0).then_inc(S.soft_done, 1)
                        act.wait_ge(S.decay_up, t.up(S.decay_up))
                        fn(lg[:, 2 * j:2 * j + 2, :], ta[:], ACT.Ln).then_inc(S.ln_done, 1)
                for j in range(2):
                    src = next_pair()
                    act.wait_ge(S.pair_full, n.q)
                    fn(gq[:, 2 * j:2 * j + 2, :], src, ACT.Silu).then_inc(pair_free[(n.q - 1) % 2], 1)
                for j in range(2):
                    evict(gv[:, :, 256 * j:256 * j + 256], 256)
                core(1.0)
                core_post(0)
                for j in range(4):
                    src = next_pair()
                    act.wait_ge(S.pair_full, n.q)
                    if j:
                        act.wait_ge(S.rope_done, t.up(S.rope_done))
                    fn(tmp[0][:], src, ACT.Square).then_inc(S.r_square, 1)
                    act.wait_ge(S.r_summed, t.up(S.r_summed))
                    fn(tmp[1][:], X4[:, 0:2, :], ACT.Sqrt, bias=small[:, 0:1], scale=1.0 / HD).then_inc(S.r_root, 1)
                next_pair()
                next_pair()
                act.wait_ge(S.rope_done, t.up(S.rope_done, 3))
                for j in range(2):
                    evict(av[:, :, 256 * j:256 * j + 256], 256)
                for i in range(4 * (NT - 1)):
                    kk = (i // 4 + 2) * P
                    act.wait_ge(S.i_scores, t.up(S.i_scores))
                    if i >= 2:
                        act.wait_ge(S.i_scored, t.up(S.i_scored))
                    fn(tmp[0][:, i % 2, 0:kk], X[i % 2][:, 0:kk], ACT.Relu).then_inc(S.i_relu, 1)
                act.wait_ge(S.i_scored, t.up(S.i_scored, 2))
                attention(AH, lambda m: (0, m + 1), False, 1)
                merge(2)
                act.wait_ge(pair_free[(n.q - 1) % 2], (n.q - 1) // 2 + 1)
                norm()
                ffn(False)

        @block.vector
        def _(dve):
            t = Turns()
            n = Place()
            v = nc.vector

            def next_pair():
                n.q += 1
                return pair[(n.q - 1) % 2]

            def low(dst, src, high, sem=S.dve_chain):
                v.tensor_tensor(dst, src, high.bitcast(F32), ALU.subtract).then_inc(sem, 1)
                dve.wait_ge(sem, t.up(sem))

            def norm(g, split=True):
                dve.wait_ge(S.n_root, t.up(S.n_root))
                v.reciprocal(tmp[2][:, 1, :], tmp[2][:, 0, :]).then_inc(S.dve_chain, 1)
                dve.wait_ge(S.dve_chain, t.up(S.dve_chain))

                def scaled(c):
                    dst = tmp[3][:, c % 2, :] if split else xT[:, c, :]
                    v.scalar_tensor_tensor(dst, xT[:, c, :], vec[:, g + c:g + c + 1], tmp[2][:, 1, :],
                                                  ALU.mult, ALU.mult).then_inc(S.n_normed, 1)
                    dve.wait_ge(S.n_normed, t.up(S.n_normed))

                if not split:
                    for c in range(DC):
                        scaled(c)
                    return
                scaled(0)
                for c in range(DC):
                    if c + 1 < DC:
                        scaled(c + 1)
                    dve.wait_ge(S.n_hi, t.up(S.n_hi))
                    low(ul[:, c, :], tmp[3][:, c % 2, :], uh[:, c, :], S.n_lo)

            def core(scale):
                v.memset(attT[:], 0.0).then_inc(S.dve_chain, 1)
                dve.wait_ge(S.dve_chain, t.up(S.dve_chain))
                decay = small[:, 20:24]
                for m in range(NT):
                    tok = slice(m * P, (m + 1) * P)
                    dve.wait_ge(S.lt_hi, t.up(S.lt_hi))
                    v.scalar_tensor_tensor(ltl[:], X[0].rearrange("p (h f) -> p h f", h=H), scale,
                                                  lth[:].bitcast(F32), ALU.mult, ALU.subtract).then_inc(S.lt_lo, 1)
                    dve.wait_ge(S.lt_lo, t.up(S.lt_lo))
                    dve.wait_ge(S.dec_done, t.up(S.dec_done, H))
                    v.tensor_copy(decay, dec[:, :, LEVELS, P - 1]).then_inc(S.dve_chain, 1)
                    dve.wait_ge(S.dve_chain, t.up(S.dve_chain))
                    v.tensor_tensor(dec[:, :, LEVELS + 1, :], dec[:, :, LEVELS + 1, :], gk[:, :, tok], ALU.mult).then_inc(S.kd_ready, 1)
                    v.tensor_tensor(dec[:, :, LEVELS, :], dec[:, :, LEVELS, :], gq[:, :, tok], ALU.mult)
                    for l in range(LEVELS):
                        w = P >> (l + 1)
                        form = lambda x: x.rearrange("p h (g two w) -> p h g two w", two=2, w=w)
                        e, q, k = form(dec[:, :, l, :]), form(gq[:, :, tok]), form(gk[:, :, tok])
                        for part, x in ((1, q), (0, k)):
                            ins = v.tensor_tensor(e[:, :, :, part, :], e[:, :, :, part, :], x[:, :, :, part, :], ALU.mult)
                        ins.then_inc(S.lev_ready, 1)
                    for l in range(LEVELS + 1):
                        dve.wait_ge(S.att_done, t.up(S.att_done))
                        mask = pairmask[:, l, :].unsqueeze(1).to_broadcast([P, H, P])
                        v.copy_predicated(attT[:], mask, X[1 + l % 3].rearrange("p (h t) -> p h t", h=H)).then_inc(S.pairs_done, 1)
                        dve.wait_ge(S.pairs_done, t.up(S.pairs_done))
                    dve.wait_ge(S.out_done, t.up(S.out_done))
                    v.tensor_copy(gq[:, :, tok], X[0].rearrange("p (h t) -> p h t", h=H)).then_inc(S.out_read, 1)
                    if m < NT - 1:
                        dve.wait_ge(S.kv_done, t.up(S.kv_done))
                        kv = X[1].rearrange("p (h f) -> p h f", h=H)
                        if m == 0:
                            v.tensor_copy(state[:], kv).then_inc(S.state_done, 1)
                            dve.wait_ge(S.state_done, t.up(S.state_done))
                        else:
                            for h in range(H):
                                signal = S.state_done if h == H - 1 else S.dve_chain
                                v.scalar_tensor_tensor(state[:, h, :], state[:, h, :], decay[:, h:h + 1], kv[:, h, :],
                                                              ALU.mult, ALU.add).then_inc(signal, 1)
                                dve.wait_ge(signal, t.up(signal))

            def core_post(g, same, b):
                for j in range(2):
                    next_pair()
                    dve.wait_ge(S.g_root, t.up(S.g_root))
                    v.reciprocal(tmp[2][:], tmp[2][:]).then_inc(S.dve_chain, 1)
                    dve.wait_ge(S.dve_chain, t.up(S.dve_chain))
                    for i in range(2):
                        col = g if same else g + 2 * j + i
                        v.scalar_tensor_tensor(tmp[3][:, i, :], gq[:, 2 * j + i, :], vec[:, col:col + 1],
                                                      tmp[2][:, i, :], ALU.mult, ALU.mult).then_inc(S.dve_chain, 1)
                        dve.wait_ge(S.dve_chain, t.up(S.dve_chain))
                    v.tensor_tensor(tmp[3][:], tmp[3][:], tmp[0][:], ALU.mult).then_inc(S.g_prod, 1)
                    dve.wait_ge(S.g_prod, t.up(S.g_prod))
                    dve.wait_ge(S.b_hi, t.up(S.b_hi))
                    low(brl[b][:, 2 * j:2 * j + 2, :], tmp[3][:], brh[b][:, 2 * j:2 * j + 2, :], S.branch_ready if j else S.dve_chain)

            def attention(heads, blocks, sink, b):
                steps = [(m, h) for m in range(NT) for h in range(heads)]
                dst = sq if sink else aq

                def front(i):
                    m, h = steps[i]
                    kk = (blocks(m)[1] - blocks(m)[0]) * P
                    st = stat[:, 8 * (i % 2):8 * (i % 2) + 8]
                    dve.wait_ge(S.qk_done, t.up(S.qk_done))
                    if sink:
                        v.scalar_tensor_tensor(logit[i % 2][:, 0:kk], dist[:, 2 * P - kk:2 * P], -SLOPES[h],
                                                      X[i % 2][:, 0:kk], ALU.mult, ALU.add).then_inc(S.logit_done, 1)
                        dve.wait_ge(S.logit_done, t.up(S.logit_done))
                        v.tensor_reduce(st[:, 0:1], logit[i % 2][:, 0:kk], AX, ALU.max).then_inc(S.dve_chain, 1)
                        dve.wait_ge(S.dve_chain, t.up(S.dve_chain))
                        v.tensor_scalar(st[:, 1:2], st[:, 0:1], sinks[:, h:h + 1], -1.0, ALU.max, ALU.mult).then_inc(S.negmax, 1)
                    else:
                        mask = causal if m == 0 else bias[:, m, 0:kk]
                        v.tensor_tensor_reduce(out=logit[i % 2][:, 0:kk], in0=X[i % 2][:, 0:kk], in1=mask, scale=1.0,
                                                      scalar=TAKEN, op0=ALU.add, op1=ALU.max, accum_out=st[:, 0:1]).then_inc(S.logit_done, 1)
                        dve.wait_ge(S.logit_done, t.up(S.logit_done))
                        v.tensor_scalar(st[:, 1:2], st[:, 0:1], -1.0, None, ALU.mult).then_inc(S.negmax, 1)

                def back(i):
                    m, h = steps[i]
                    kk = (blocks(m)[1] - blocks(m)[0]) * P
                    st = stat[:, 8 * (i % 2):8 * (i % 2) + 8]
                    dve.wait_ge(S.prob_done, t.up(S.prob_done))
                    if sink:
                        v.tensor_tensor(st[:, 2:3], st[:, 2:3], st[:, 3:4], ALU.add).then_inc(S.dve_chain, 1)
                        dve.wait_ge(S.dve_chain, t.up(S.dve_chain))
                    v.reciprocal(st[:, 4:5], st[:, 2:3]).then_inc(S.dve_chain, 1)
                    dve.wait_ge(S.dve_chain, t.up(S.dve_chain))
                    v.tensor_scalar(prob[i % 2][:, 0:kk], prob[i % 2][:, 0:kk], st[:, 4:5], None, ALU.mult).then_inc(S.scaled, 1)
                    dve.wait_ge(S.scaled, t.up(S.scaled))

                def out(i):
                    m, h = steps[i]
                    dve.wait_ge(S.pv_done, t.up(S.pv_done, 2))
                    v.tensor_copy(dst[:, h // 2, m * P:(m + 1) * P], X[3][:, 0:P]).then_inc(S.pv_read, 1)

                front(0)
                for i in range(len(steps)):
                    if i + 1 < len(steps):
                        front(i + 1)
                    back(i)
                    if i % 2 == 0 and i > 0:
                        out(i - 1)
                out(len(steps) - 1)
                for j in range(2):
                    dve.wait_ge(S.b_hi, t.up(S.b_hi))
                    low(brl[b][:, 2 * j:2 * j + 2, :], dst[:, 2 * j:2 * j + 2, :], brh[b][:, 2 * j:2 * j + 2, :],
                        S.branch_ready if j else S.dve_chain)

            def merge(nb):
                for j in range(2):
                    for b in range(nb):
                        next_pair()
                        next_pair()
                        dve.wait_ge(pair_free[(n.q - 2) % 2], (n.q - 2) // 2 + 1)
                        dve.wait_ge(pair_free[(n.q - 1) % 2], (n.q - 1) // 2 + 1)
                        for s in range(2):
                            src = next_pair()
                            dve.wait_ge(S.pair_full, n.q)
                            acc = merged[:, 4 * j + 2 * s:4 * j + 2 * s + 2, :]
                            if b == 0:
                                v.tensor_tensor(acc, src, tmp[s][:], ALU.mult).then_inc(pair_free[(n.q - 1) % 2], 1)
                                dve.wait_ge(pair_free[(n.q - 1) % 2], (n.q - 1) // 2 + 1)
                            else:
                                v.tensor_tensor(tmp[2][:], src, tmp[s][:], ALU.mult).then_inc(pair_free[(n.q - 1) % 2], 1)
                                dve.wait_ge(pair_free[(n.q - 1) % 2], (n.q - 1) // 2 + 1)
                                signal = S.y_added if b == nb - 1 else S.dve_chain
                                v.tensor_tensor(acc, acc, tmp[2][:], ALU.add).then_inc(signal, 1)
                                dve.wait_ge(signal, t.up(signal))
                for s in range(4):
                    dve.wait_ge(S.m_hi, t.up(S.m_hi))
                    low(ul[:, 2 * s:2 * s + 2, :], merged[:, 2 * s:2 * s + 2, :], uh[:, 2 * s:2 * s + 2, :], S.m_lo)
                residual()

            def residual():
                for s in range(DC // 2):
                    src = next_pair()
                    dve.wait_ge(S.pair_full, n.q)
                    x = xT[:, 2 * s:2 * s + 2, :]
                    v.tensor_tensor(x, x, src, ALU.add).then_inc(pair_free[(n.q - 1) % 2], 1)
                    dve.wait_ge(pair_free[(n.q - 1) % 2], (n.q - 1) // 2 + 1)

            def taps(y, x, w, ch):
                v.scalar_tensor_tensor(y[:, 1:T], x[:, 0:T - 1], w(1, ch), y[:, 1:T], ALU.mult, ALU.add).then_inc(S.dve_chain, 1)
                dve.wait_ge(S.dve_chain, t.up(S.dve_chain))
                return v.scalar_tensor_tensor(y[:, 2:T], x[:, 0:T - 2], w(0, ch), y[:, 2:T], ALU.mult, ALU.add)

            def ffn(conv):
                for step, third in FFN_STEPS:
                    i0 = sum(THIRDS[:third])
                    if step == "down":
                        residual()
                        continue
                    for i in range(i0, i0 + THIRDS[third]):
                        if conv:
                            for part in range(2):
                                src = next_pair()
                                dve.wait_ge(S.pair_full, n.q)
                                dve.wait_ge(S.f_tap, t.up(S.f_tap))
                                w = lambda k, ch: fconv[:, k, ch:ch + 1]
                                for c in range(2):
                                    ins = taps(tmp[part][:, c, :], src[:, c, :], w, part * FC + 2 * i + c)
                                    if c == 0:
                                        ins.then_inc(S.dve_chain, 1)
                                        dve.wait_ge(S.dve_chain, t.up(S.dve_chain))
                                ins.then_inc(pair_free[(n.q - 1) % 2], 1)
                                dve.wait_ge(pair_free[(n.q - 1) % 2], (n.q - 1) // 2 + 1)
                            dve.wait_ge(S.f_silu, t.up(S.f_silu))
                            v.tensor_tensor(tmp[2][:], tmp[0][:], tmp[1][:], ALU.mult).then_inc(S.f_mult, 1)
                            dve.wait_ge(S.f_mult, t.up(S.f_mult))
                        else:
                            next_pair()
                            dve.wait_ge(pair_free[(n.q - 1) % 2], (n.q - 1) // 2 + 1)
                            src = next_pair()
                            dve.wait_ge(S.pair_full, n.q)
                            v.tensor_tensor(tmp[2][:], tmp[0][:], src, ALU.mult).then_inc(pair_free[(n.q - 1) % 2], 1)
                            dve.wait_ge(pair_free[(n.q - 1) % 2], (n.q - 1) // 2 + 1)
                        c = 2 * (i - i0)
                        dve.wait_ge(S.f_hi, t.up(S.f_hi))
                        low(fl[third % 2][:, c:c + 2, :], tmp[2][:], fh[third % 2][:, c:c + 2, :], S.f_lo)

            def rope(dst, g=None, single=False):
                src = next_pair()
                dve.wait_ge(S.pair_full, n.q)
                if g is not None:
                    dve.wait_ge(S.r_root, t.up(S.r_root))
                    v.reciprocal(tmp[1][:], tmp[1][:]).then_inc(S.dve_chain, 1)
                    dve.wait_ge(S.dve_chain, t.up(S.dve_chain))
                    v.scalar_tensor_tensor(tmp[2][:], src, g, tmp[1][:], ALU.mult, ALU.mult).then_inc(S.r_normed, 1)
                    dve.wait_ge(S.r_normed, t.up(S.r_normed))
                elif not single:
                    v.tensor_copy(tmp[2][:], src).then_inc(S.r_normed, 1)
                    dve.wait_ge(S.r_normed, t.up(S.r_normed))
                else:
                    v.tensor_copy(tmp[2][0:HD, 0, :], src[0:HD, 0, :]).then_inc(S.dve_chain, 1)
                    dve.wait_ge(S.dve_chain, t.up(S.dve_chain))
                    v.tensor_copy(tmp[2][HD:P, 0, :], src[HD:P, 1, :]).then_inc(S.r_normed, 1)
                    dve.wait_ge(S.r_normed, t.up(S.r_normed))
                k = 1 if single else 2
                cos = cosT[:].unsqueeze(1).to_broadcast([P, k, T])
                sin = sinT[:].unsqueeze(1).to_broadcast([P, k, T])
                v.tensor_tensor(tmp[1][:, 0:k, :], tmp[2][:, 0:k, :], cos, ALU.mult).then_inc(pair_free[(n.q - 1) % 2], 1)
                dve.wait_ge(pair_free[(n.q - 1) % 2], (n.q - 1) // 2 + 1)
                dve.wait_ge(S.r_turned, t.up(S.r_turned))
                v.tensor_tensor(tmp[3][:, 0:k, :], X4[:, 2:2 + k, :], sin, ALU.mult).then_inc(S.dve_chain, 1)
                dve.wait_ge(S.dve_chain, t.up(S.dve_chain))
                v.tensor_tensor(dst, tmp[1][:, 0:k, :], tmp[3][:, 0:k, :], ALU.add).then_inc(S.rope_done, 1)
                dve.wait_ge(S.rope_done, t.up(S.rope_done))

            def select():
                for m in range(1, NT):
                    kk = (m + 1) * P
                    sc = score[:, 0:kk]
                    for h in range(4):
                        dve.wait_ge(S.i_relu, t.up(S.i_relu))
                        r, wt = tmp[0][:, h % 2, 0:kk], iw[:, m, h:h + 1]
                        if h == 0:
                            v.tensor_scalar(sc, r, wt, None, ALU.mult).then_inc(S.i_scored, 1)
                            dve.wait_ge(S.i_scored, t.up(S.i_scored))
                        else:
                            v.scalar_tensor_tensor(sc, r, wt, sc, ALU.mult, ALU.add).then_inc(S.i_scored, 1)
                            dve.wait_ge(S.i_scored, t.up(S.i_scored))
                    own = score[:, m * P:kk]
                    v.tensor_tensor(own, own, causal, ALU.add).then_inc(S.dve_chain, 1)
                    dve.wait_ge(S.dve_chain, t.up(S.dve_chain))
                    for _ in range(TOPK // 8):
                        v.max(top8[:], sc).then_inc(S.dve_chain, 1)
                        dve.wait_ge(S.dve_chain, t.up(S.dve_chain))
                        v.match_replace(sc, top8[:], sc, TAKEN).then_inc(S.dve_chain, 1)
                        dve.wait_ge(S.dve_chain, t.up(S.dve_chain))
                    v.tensor_scalar(bias[:, m, 0:kk], sc, TAKEN / 3, NEG, ALU.is_gt, ALU.mult).then_inc(S.dve_chain, 1)
                    dve.wait_ge(S.dve_chain, t.up(S.dve_chain))

            v.memset(ones[:], 1.0).then_inc(S.dve_chain, 1)
            dve.wait_ge(S.dve_chain, t.up(S.dve_chain))
            v.memset(small[:, 0:1], EPS).then_inc(S.dve_chain, 1)
            dve.wait_ge(S.dve_chain, t.up(S.dve_chain))
            dve.wait_ge(S.consts_in, 16 * N_LOADS)
            v.tensor_copy(summask[:], mrow[:, 0:N_SUM * P]).then_inc(S.dve_chain, 1)
            dve.wait_ge(S.dve_chain, t.up(S.dve_chain))
            v.tensor_copy(pairmask[:].rearrange("p l t -> p (l t)"), mrow[:, N_SUM * P:]).then_inc(S.dve_chain, 1)
            dve.wait_ge(S.dve_chain, t.up(S.dve_chain))
            dve.wait_ge(S.vec_T, t.up(S.vec_T))
            v.tensor_copy(fconv[:].rearrange("p k c -> p (k c)"), X[1][:, 0:6 * FC]).then_inc(S.dve_chain, 1)
            dve.wait_ge(S.dve_chain, t.up(S.dve_chain))
            v.tensor_copy(vec[:], X[0][:, 0:N_VEC]).then_inc(S.vec_ready, 1)
            dve.wait_ge(S.vec_ready, t.up(S.vec_ready))
            lb0, lb1 = vec[:, V_LB:V_LB + 4], vec[:, V_LB + 4:V_LB + 8]
            v.tensor_tensor(small[:, 11:15], lb1, lb0, ALU.subtract).then_inc(S.dve_chain, 1)
            dve.wait_ge(S.dve_chain, t.up(S.dve_chain))
            v.tensor_tensor(small[:, 15:19], lb0, lb1, ALU.subtract).then_inc(S.dve_chain, 1)
            dve.wait_ge(S.dve_chain, t.up(S.dve_chain))
            for l in range(LAYERS):
                v.tensor_scalar(small[:, 9 + l:10 + l], vec[:, V_QN + l:V_QN + l + 1], HD ** -0.5, None, ALU.mult).then_inc(S.dve_chain, 1)
                dve.wait_ge(S.dve_chain, t.up(S.dve_chain))
            angle, turns = tmp[3][:, 0, :], tmp[3][:, 1, :]
            v.tensor_copy(tmp[2][:, 0, :], posi[:]).then_inc(S.dve_chain, 1)
            dve.wait_ge(S.dve_chain, t.up(S.dve_chain))
            v.tensor_scalar(angle, tmp[2][:, 0, :], const[:, K_INV:K_INV + 1], None, ALU.mult).then_inc(S.dve_chain, 1)
            dve.wait_ge(S.dve_chain, t.up(S.dve_chain))
            v.tensor_scalar(turns, angle, 1.0 / (2 * np.pi), MAGIC, ALU.mult, ALU.add).then_inc(S.dve_chain, 1)
            dve.wait_ge(S.dve_chain, t.up(S.dve_chain))
            v.tensor_scalar(turns, turns, MAGIC, None, ALU.subtract).then_inc(S.dve_chain, 1)
            dve.wait_ge(S.dve_chain, t.up(S.dve_chain))
            for part in TWO_PI:
                v.scalar_tensor_tensor(angle, turns, -part, angle, ALU.mult, ALU.add).then_inc(S.dve_chain, 1)
                dve.wait_ge(S.dve_chain, t.up(S.dve_chain))
            v.tensor_scalar(angle, angle, PI, -PI, ALU.min, ALU.max).then_inc(S.dve_chain, 1)
            dve.wait_ge(S.dve_chain, t.up(S.dve_chain))
            v.tensor_scalar(turns, angle, float(np.pi / 2), -2 * np.pi, ALU.is_gt, ALU.mult).then_inc(S.dve_chain, 1)
            dve.wait_ge(S.dve_chain, t.up(S.dve_chain))
            v.scalar_tensor_tensor(turns, angle, float(np.pi / 2), turns, ALU.add, ALU.add).then_inc(S.dve_chain, 1)
            dve.wait_ge(S.dve_chain, t.up(S.dve_chain))
            v.tensor_scalar(turns, turns, PI, -PI, ALU.min, ALU.max).then_inc(S.setup_done, 1)
            dve.wait_ge(S.setup_done, t.up(S.setup_done))
            for c in range(DC):
                dve.wait_ge(S.x_T, t.up(S.x_T))
                v.tensor_copy(xT[:, c, :], X[c % 4]).then_inc(S.x_copied, 1)
                dve.wait_ge(S.x_copied, t.up(S.x_copied))

            norm(V_GMIX)
            for j in range(2):
                src = next_pair()
                dve.wait_ge(S.pair_full, n.q)
                v.tensor_copy(gk[:, 2 * j:2 * j + 2, :], src).then_inc(pair_free[(n.q - 1) % 2], 1)
                dve.wait_ge(pair_free[(n.q - 1) % 2], (n.q - 1) // 2 + 1)
            next_pair()
            next_pair()
            src = next_pair()
            dve.wait_ge(S.pair_full, n.q)
            v.tensor_copy(gaT[:], src[0:RANK, 0, :]).then_inc(pair_free[(n.q - 1) % 2], 1)
            dve.wait_ge(pair_free[(n.q - 1) % 2], (n.q - 1) // 2 + 1)
            next_pair()
            next_pair()
            for j in range(2):
                dve.wait_ge(S.soft_done, t.up(S.soft_done))
                for i in range(2):
                    c = 2 * j + i
                    v.tensor_scalar(tmp[2 * j + 1][:, i, :], X[c], vec[:, V_GLAB + c:V_GLAB + c + 1], 0.0,
                                           ALU.add, ALU.min).then_inc(S.dve_chain, 1)
                    dve.wait_ge(S.dve_chain, t.up(S.dve_chain))
                signal = S.lg_ready if j else S.dve_chain
                v.tensor_tensor(lg[:, 2 * j:2 * j + 2, :], tmp[2 * j + 1][:], tmp[2 * j][:], ALU.subtract).then_inc(signal, 1)
                dve.wait_ge(signal, t.up(signal))
            core(1.0 / GLA_TAU)
            core_post(V_GLAN, False, 0)
            for j in range(2):
                src = next_pair()
                dve.wait_ge(S.pair_full, n.q)
                v.tensor_copy(tmp[0][:], src).then_inc(pair_free[(n.q - 1) % 2], 1)
                dve.wait_ge(pair_free[(n.q - 1) % 2], (n.q - 1) // 2 + 1)
                src = next_pair()
                dve.wait_ge(S.pair_full, n.q)
                v.tensor_tensor(tmp[1][:], tmp[0][:], src, ALU.mult).then_inc(pair_free[(n.q - 1) % 2], 1)
                dve.wait_ge(pair_free[(n.q - 1) % 2], (n.q - 1) // 2 + 1)
                w = lambda k, ch: vec[:, V_CONV + 4 * k + ch:V_CONV + 4 * k + ch + 1]
                for i in range(2):
                    v.tensor_scalar(tmp[2][:, i, :], tmp[1][:, i, :], w(2, 2 * j + i), None, ALU.mult).then_inc(S.dve_chain, 1)
                    dve.wait_ge(S.dve_chain, t.up(S.dve_chain))
                    taps(tmp[2][:, i, :], tmp[1][:, i, :], w, 2 * j + i).then_inc(S.dve_chain, 1)
                    dve.wait_ge(S.dve_chain, t.up(S.dve_chain))
                src = next_pair()
                dve.wait_ge(S.pair_full, n.q)
                v.tensor_tensor(tmp[3][:], tmp[2][:], src, ALU.mult).then_inc(pair_free[(n.q - 1) % 2], 1)
                dve.wait_ge(pair_free[(n.q - 1) % 2], (n.q - 1) // 2 + 1)
                dve.wait_ge(S.b_hi, t.up(S.b_hi))
                low(brl[1][:, 2 * j:2 * j + 2, :], tmp[3][:], brh[1][:, 2 * j:2 * j + 2, :], S.branch_ready if j else S.dve_chain)
            next_pair()
            next_pair()
            src = next_pair()
            dve.wait_ge(S.pair_full, n.q)
            v.tensor_copy(sk[HD:P, 0, :], src[HD:P, 0, :]).then_inc(S.dve_chain, 1)
            dve.wait_ge(S.dve_chain, t.up(S.dve_chain))
            v.tensor_copy(sk[0:HD, 0, :], src[0:HD, 1, :]).then_inc(S.dve_chain, 1)
            dve.wait_ge(S.dve_chain, t.up(S.dve_chain))
            v.tensor_copy(sk[HD:P, 1, :], src[HD:P, 1, :]).then_inc(pair_free[(n.q - 1) % 2], 1)
            dve.wait_ge(pair_free[(n.q - 1) % 2], (n.q - 1) // 2 + 1)
            src = next_pair()
            dve.wait_ge(S.pair_full, n.q)
            v.tensor_copy(sk[0:HD, 1, :], src[0:HD, 0, :]).then_inc(pair_free[(n.q - 1) % 2], 1)
            dve.wait_ge(pair_free[(n.q - 1) % 2], (n.q - 1) // 2 + 1)
            v.memset(small[:, 31:32], 0.0).then_inc(S.q_ready, 1)
            dve.wait_ge(S.q_ready, t.up(S.q_ready))
            next_pair()
            attention(AH, lambda m: (max(m - 1, 0), m + 1), True, 2)
            merge(3)
            norm(V_GFFN)
            ffn(True)
            norm(V_GFIN, split=False)

            dve.wait_ge(S.trig_done, t.up(S.trig_done))
            v.tensor_scalar(small[:, 1:5], small[:, 1:5], 2.0 ** -60, None, ALU.max).then_inc(S.dve_chain, 1)
            dve.wait_ge(S.dve_chain, t.up(S.dve_chain))
            for l in range(LAYERS):
                norm(V_NMIX + DC * l)
                for j in range(2):
                    src = next_pair()
                    dve.wait_ge(S.pair_full, n.q)
                    ta, tb = tmp[2 * j], tmp[2 * j + 1]
                    if l == 0:
                        dve.wait_ge(S.soft_done, t.up(S.soft_done))
                        v.tensor_scalar(tb[:], src, 0.0, None, ALU.min).then_inc(S.dve_chain, 1)
                        dve.wait_ge(S.dve_chain, t.up(S.dve_chain))
                        v.tensor_tensor(lg[:, 2 * j:2 * j + 2, :], tb[:], ta[:], ALU.subtract).then_inc(pair_free[(n.q - 1) % 2], 1)
                        dve.wait_ge(pair_free[(n.q - 1) % 2], (n.q - 1) // 2 + 1)
                    else:
                        dve.wait_ge(S.soft_done, t.up(S.soft_done))
                        for i in range(2):
                            c = 2 * j + i
                            lo, span = small[:, 1 + c:2 + c], small[:, 5 + c:6 + c]
                            signal = S.decay_up if i else S.dve_chain
                            v.tensor_scalar(ta[:, i, :], ta[:, i, :], span, lo, ALU.mult, ALU.add).then_inc(signal, 1)
                            dve.wait_ge(signal, t.up(signal))
                        for i in range(2):
                            c = 2 * j + i
                            span = small[:, 5 + c:6 + c]
                            ins = v.tensor_scalar(gk[:, c, :], tb[:, i, :], span, None, ALU.mult)
                            if i == 0:
                                ins.then_inc(S.dve_chain, 1)
                                dve.wait_ge(S.dve_chain, t.up(S.dve_chain))
                        ins.then_inc(pair_free[(n.q - 1) % 2], 1)
                        dve.wait_ge(pair_free[(n.q - 1) % 2], (n.q - 1) // 2 + 1)
                v.memset(small[:, 31:32], 0.0).then_inc(S.lg_ready, 1)
                dve.wait_ge(S.lg_ready, t.up(S.lg_ready))
                for _ in range(4):
                    next_pair()
                core(1.0)
                core_post(V_HN + l, True, 0)
                for j in range(2):
                    rope(aq[:, 2 * j:2 * j + 2, :], small[:, 9 + l:10 + l])
                for j in range(2):
                    rope(ak[:, 2 * j:2 * j + 2, :], vec[:, V_KN + l:V_KN + l + 1])
                rope(iq[:])
                rope(ik[:].unsqueeze(1), single=True)
                v.tensor_scalar(iw[:].rearrange("p m h -> p (m h)"), X[0][:, 0:4 * NT], 1.0 / 16, None, ALU.mult).then_inc(S.q_ready, 1)
                dve.wait_ge(S.q_ready, t.up(S.q_ready))
                next_pair()
                next_pair()
                select()
                attention(AH, lambda m: (0, m + 1), False, 1)
                merge(2)
                norm(V_NFFN + DC * l)
                ffn(False)

            for i in range(2 * NT):
                m, half = i // 2, i % 2
                dve.wait_ge(S.y_T, t.up(S.y_T))
                v.tensor_copy(xtok[:, m, MIX * half:MIX * (half + 1)], X[i % 4]).then_inc(S.y_out, 1)
                dve.wait_ge(S.y_out, t.up(S.y_out))


N_LOADS = 20
MAGIC = 1.5 * 2.0 ** 23
TWO_PI = (6.28125, 0.0019350051879882812, 3.0199159819304e-07)
PI = 3.1415925


def shape_constants():
    f = np.float32
    c = np.zeros((P, N_CONST), f)
    i = np.arange(P)
    c[:, K_ID:K_ID + P] = np.eye(P)
    c[:, K_BLK:K_BLK + P] = i[:, None] // HD == i[None, :] // HD
    half = HD // 2
    for o in range(P):
        if o % HD < half:
            c[o + half, K_ROT + o] = -1.0
        else:
            c[o - half, K_ROT + o] = 1.0
    c[:, K_CAUS:K_CAUS + P] = np.where(i[None, :] <= i[:, None], 0.0, NEG)
    d = P + i[:, None] - np.arange(2 * P)[None, :]
    c[:, K_DIST:K_DIST + 2 * P] = np.where((d >= 0) & (d < P), d, FAR)
    c[:, K_INV] = (10000.0 ** (-(2.0 * (i % half)) / HD)).astype(f)
    j, t = i[:, None], i[None, :]
    sums, pairs = [], []
    for l in range(LEVELS):
        w = P >> (l + 1)
        odd = (t // w) % 2 == 1
        start = (t // w) * w
        sums.append(np.where(odd, (j >= start) & (j <= t), (j > t) & (j < start + w)))
        pairs.append(((j // w) % 2 == 0) & (t // w == j // w + 1))
    sums += [j <= t, j > t]
    pairs.append(j == t)
    return c, np.concatenate(sums + pairs, 1).astype(f)


_INS = ['x', 'g_mix', 'w_in', 'gla_w_alpha', 'gla_b_alpha', 'gla_norm_g', 'conv_w', 'swa_sinks', 'w_gla_o',
        'w_conv_o', 'w_swa_o', 'w_o', 'g_ffn', 'w_up', 'ffn_conv_w', 'w_down', 'g_final', 'positions_2', 'w_in_2',
        'w_proj_attn_2', 'w_proj_hgrn_2', 'w_out_2', 'norm_mix_2', 'norm_ffn_2', 'q_norm_2', 'k_norm_2',
        'hgrn_norm_2', 'hgrn_lower_bound_2', 'w_ffn_in_2', 'w_ffn_out_2']


def kernel(**inputs):
    import concourse.bacc as bacc
    from concourse.bass_utils import run_bass_kernel_spmd

    nc = bacc.Bacc("TRN2", target_bir_lowering=False, num_devices=1)
    arrays, aps = {}, {}
    given = {name: np.ascontiguousarray(inputs[name]) for name in _INS}
    given.update(zip(("c_const", "c_masks"), shape_constants()))
    for name, x in given.items():
        arrays[f"in_{name}"] = x
        aps[name] = nc.dram_tensor(f"in_{name}", x.shape, mybir.dt.from_np(x.dtype), kind="ExternalInput").ap()
    out = nc.dram_tensor("out_0", (1, T, D), F32, kind="ExternalOutput").ap()
    build_program(nc, aps, out)
    r = run_bass_kernel_spmd(nc, [arrays], core_ids=[0])
    return r.results[0]["out_0"]
```

```python
from contextlib import ExitStack

import concourse.bass as bass
from concourse import mybir
import numpy as np

F32 = mybir.dt.float32
F32R = mybir.dt.float32r
I32 = mybir.dt.int32
U8 = mybir.dt.uint8
ALU = mybir.AluOpType
ACT = mybir.ActivationFunctionType
AX = mybir.AxisListType.X

P = 128
T = 512
NT = T // P
D = 1024
DC = D // P
EPS = 1e-6
H = 4
MIX = 512
MC = MIX // P
RANK = 16
GLA_TAU = 16.0
D_FF = 2816
FC = D_FF // P
FFN_PAIRS = FC // 2
THIRDS = (4, 4, 3)
AH = 8
HD = 64
LAYERS = 2
TOPK = 128
LEVELS = 7
NEG = -1.0e30
TAKEN = -3.0e38
FAR = 1.0e30

C_GQ, C_GK, C_GV, C_GR, C_GA = 0, 512, 1024, 1536, 2048
C_CX = C_GA + RANK
C_CB, C_CC = C_CX + 512, C_CX + 1024
C_SQ = C_CC + 512
C_SK = C_SQ + 512
C_SV = C_SK + 128
C_GATE = C_SV + 128
C_AQ, C_AK, C_AV, C_IQ, C_IK, C_IW = 0, 512, 1024, 1536, 1792, 1856
C_HQ = C_IW + 4
C_HF, C_HI, C_HG = C_HQ + 512, C_HQ + 1024, C_HQ + 1536
C_G2 = C_HG + 512

V_GMIX, V_GFFN, V_GFIN = 0, 8, 16
V_NMIX, V_NFFN = 24, 40
V_GLAN, V_GLAB = 56, 60
V_CONV = 64
V_HN = 76
V_LB = 78
V_QN, V_KN = 86, 88
N_VEC = 90

K_ID, K_BLK, K_ROT, K_CAUS, K_DIST, K_INV = 0, 128, 256, 384, 512, 768
N_CONST = 769
N_SUM = LEVELS + 2


class Semaphores:
    def __init__(self, sem):
        self.consts_in = sem("consts_in")
        self.x_in = sem("x_in")
        self.raw_in0 = sem("raw_in0")
        self.raw_in1 = sem("raw_in1")
        self.raw_in2 = sem("raw_in2")
        self.setup_done = sem("setup_done")
        self.trig_done = sem("trig_done")
        self.vec_T = sem("vec_T")
        self.vec_ready = sem("vec_ready")
        self.x_T = sem("x_T")
        self.x_copied = sem("x_copied")
        self.hi_done = sem("hi_done")
        self.lo_done = sem("lo_done")
        self.pair_full = sem("pair_full")
        self.pair_free0 = sem("pair_free0")
        self.pair_free1 = sem("pair_free1")
        self.n_square = sem("n_square")
        self.n_summed = sem("n_summed")
        self.n_root = sem("n_root")
        self.n_normed = sem("n_normed")
        self.n_hi = sem("n_hi")
        self.n_lo = sem("n_lo")
        self.alpha_done = sem("alpha_done")
        self.soft_done = sem("soft_done")
        self.decay_up = sem("decay_up")
        self.ln_done = sem("ln_done")
        self.lg_ready = sem("lg_ready")
        self.lg_T = sem("lg_T")
        self.lt_hi = sem("lt_hi")
        self.lt_lo = sem("lt_lo")
        self.sums_done = sem("sums_done")
        self.dec_done = sem("dec_done")
        self.kd_ready = sem("kd_ready")
        self.kd_T = sem("kd_T")
        self.kdt_done = sem("kdt_done")
        self.lev_ready = sem("lev_ready")
        self.att_done = sem("att_done")
        self.pairs_done = sem("pairs_done")
        self.out_done = sem("out_done")
        self.out_read = sem("out_read")
        self.kv_done = sem("kv_done")
        self.state_done = sem("state_done")
        self.g_square = sem("g_square")
        self.g_summed = sem("g_summed")
        self.g_root = sem("g_root")
        self.g_prod = sem("g_prod")
        self.g_split = sem("g_split")
        self.b_hi = sem("b_hi")
        self.branch_ready = sem("branch_ready")
        self.q_ready = sem("q_ready")
        self.qk_done = sem("qk_done")
        self.logit_done = sem("logit_done")
        self.negmax = sem("negmax")
        self.prob_done = sem("prob_done")
        self.scaled = sem("scaled")
        self.pt_done = sem("pt_done")
        self.pt_read = sem("pt_read")
        self.pv_done = sem("pv_done")
        self.pv_read = sem("pv_read")
        self.r_square = sem("r_square")
        self.r_summed = sem("r_summed")
        self.r_root = sem("r_root")
        self.r_normed = sem("r_normed")
        self.r_turned = sem("r_turned")
        self.rope_done = sem("rope_done")
        self.i_scores = sem("i_scores")
        self.i_relu = sem("i_relu")
        self.i_scored = sem("i_scored")
        self.y_added = sem("y_added")
        self.m_hi = sem("m_hi")
        self.m_lo = sem("m_lo")
        self.f_tap = sem("f_tap")
        self.f_silu = sem("f_silu")
        self.f_mult = sem("f_mult")
        self.f_hi = sem("f_hi")
        self.f_lo = sem("f_lo")
        self.y_T = sem("y_T")
        self.y_out = sem("y_out")
        self.out_stored = sem("out_stored")
        self.act_chain = sem("act_chain")
        self.dve_chain = sem("dve_chain")


class Place:
    def __init__(self):
        self.p = self.q = self.hi = self.merged = 0
        self.fresh = self.bare = False


def weight_panels(a):
    out = []

    def cols(w, c0, rows=None):
        r0, nk = rows or (0, w.shape[0] // P)
        v = w[r0 * P:(r0 + nk) * P, :].rearrange("(k p) n -> p k n", p=P)
        width = 256 if nk > 4 or rows else 512
        out.append((v[:, :, c0:c0 + width], nk, width))

    def merge(w, gates, wy, between=None):
        for j in range(2):
            cols(w, gates + 512 * j)
            if j == 0 and between:
                cols(w, between)
            cols(w, gates + 512 * j + 256)
            cols(wy, 512 * j)

    def ffn(w_up, w_down):
        for step, third in FFN_STEPS:
            i0 = sum(THIRDS[:third])
            if step == "up":
                for i in range(i0, i0 + THIRDS[third]):
                    cols(w_up, 256 * i)
                    cols(w_up, D_FF + 256 * i)
            else:
                for m in range(DC // 2):
                    cols(w_down, 256 * m, (2 * i0, 2 * THIRDS[third]))

    w = a["w_in"][0]
    for c in (C_GK, C_GK + 256, C_GQ, C_GQ + 256, C_GA, C_GV, C_GV + 256):
        cols(w, c)
    for j in range(2):
        for c in (C_CX, C_CC, C_CB):
            cols(w, c + 256 * j)
    for c in (C_SQ, C_SQ + 256, C_SK - HD, C_SV, C_GR):
        cols(w, c)
    for b, wy, between in ((1, "w_conv_o", C_GR + 256), (0, "w_gla_o", None), (2, "w_swa_o", None)):
        merge(w, C_GATE + b * D, a[wy][0], between)
    for m in range(4):
        cols(a["w_o"][0], 256 * m)
    ffn(a["w_up"][0], a["w_down"][0])
    for l in range(LAYERS):
        w = a["w_in_2"][l]
        for c in (C_HF, C_HF + 256, C_HQ, C_HQ + 256, C_HI, C_HI + 256,
                  C_AQ, C_AQ + 256, C_AK, C_AK + 256, C_IQ, C_IK - HD, C_AV, C_AV + 256, C_HG):
            cols(w, c)
        merge(w, C_G2 + D, a["w_proj_hgrn_2"][l], C_HG + 256)
        merge(w, C_G2, a["w_proj_attn_2"][l])
        for m in range(4):
            cols(a["w_out_2"][l], 256 * m)
        ffn(a["w_ffn_in_2"][l], a["w_ffn_out_2"][l])
    return out


FFN_STEPS = (("up", 0), ("up", 1), ("down", 0), ("up", 2), ("down", 1), ("down", 2))
CORE_UNITS = NT * H // 2
SIDE_CORE_1 = 2 * 3 * 4 + 2 * 4 + 6 + 4
SIDE_CORE_2 = 4 * 6 + 5 + 6 + 2 * 4
MERGE_STEPS = 2 * (4 + 4 + 4)
SIDE_POST = (4, 4)
SIDE_WINDOW = [(2 * MERGE_STEPS - 8) // NT] * NT
SIDE_SPARSE = [4] * NT
SLOPES = [2.0 ** -(h + 1) for h in range(AH)]


def core_steps(total, unit, slot):
    return (share(total - 5 * CORE_UNITS, CORE_UNITS, unit), 2, 1, 1, 1)[slot]


def share(total, parts, i):
    return total * (i + 1) // parts - total * i // parts


def build_program(nc, a, out):
    panels = weight_panels(a)
    n_panels = len(panels)
    ctx = ExitStack()
    with ctx:
        def sb(name, shape, dt=F32):
            return ctx.enter_context(nc.sbuf_tensor(name, shape, dt))

        xT = sb("xT", [P, DC, T])
        uh = sb("uh", [P, DC, T], F32R)
        ul = sb("ul", [P, DC, T], F32R)
        ring = (nc.sbuf_base + 31) // 32 * 32
        raw = [sb(f"raw{i}", [P, 2048]) for i in range(3)]
        wh = [sb(f"wh{i}", [P, 2048], F32R) for i in range(3)]
        tmp = [sb(f"tmp{i}", [P, 2, T]) for i in range(4)]
        const = sb("const", [P, N_CONST])
        summask = sb("summask", [P, N_SUM * P], F32R)
        pairmask = sb("pairmask", [P, LEVELS + 1, P], U8)
        ones = sb("ones", [P, P])
        vec = sb("vec", [P, N_VEC])
        vech = sb("vech", [P, N_VEC])
        top8 = sb("top8", [P, 8])
        stat = sb("stat", [P, 16])
        fconv = sb("fconv", [P, 3, 2 * FC])
        small = sb("small", [P, 64])
        cosT = sb("cosT", [P, T])
        sinT = sb("sinT", [P, T])
        walpha = sb("walpha", [RANK, MIX])
        sinks = sb("sinks", [P, AH])
        iw = sb("iw", [P, NT, 4])
        ident, blk, rot = const[:, K_ID:K_ID + P], const[:, K_BLK:K_BLK + P], const[:, K_ROT:K_ROT + P]
        causal = const[:, K_CAUS:K_CAUS + P]
        dist = const[:, K_DIST:K_DIST + 2 * P]
        psum = ctx.enter_context(nc.psum_tensor("psum", [P, 8, T], F32))
        pair = [psum[:, 0:2, :], psum[:, 2:4, :]]
        X = [psum[:, 4 + b, :] for b in range(4)]
        X4 = psum[:, 4:8, :]

        arena = (nc.sbuf_base + 31) // 32 * 32

        def at(name, kib, shape, dt=F32):
            return nc.alloc_sbuf_tensor_at(name, shape, dt, offset=arena + int(kib * 1024))

        wl = [nc.alloc_sbuf_tensor_at(f"wl{i}", [P, 2048], F32R, offset=ring + 8192 * i) for i in range(3)]
        brh = [at(f"brh{b}", k, [P, MC, T], F32R) for b, k in enumerate((0, 63, 16))]
        brl = [at(f"brl{b}", k + 8, [P, MC, T], F32R) for b, k in enumerate((0, 63, 16))]
        gk = at("gk", 0, [P, H, T])
        lg = at("lg", 8, [P, H, T])
        gq = at("gq", 16, [P, H, T])
        gv = at("gv", 24, [P, NT, MIX])
        dec = at("dec", 32, [P, 2, N_SUM, P])
        lth = at("lth", 41, [P, 2, 2, P], F32R)
        ltl = at("ltl", 43, [P, 2, 2, P], F32R)
        attT = at("attT", 45, [P, 2, P])
        kdt = at("kdt", 46, [P, 2, P])
        state = at("state", 47, [P, H, P])
        gaT = at("gaT", 63, [RANK, T])
        sq = at("sq", 49, [P, MC, T])
        sk = at("sk", 57, [P, 2, T])
        sv = at("sv", 61, [P, NT, P])
        aq = at("aq", 49, [P, MC, T])
        ak = at("ak", 57, [P, MC, T])
        av = at("av", 65, [P, NT, MIX])
        iq = at("iq", 73, [P, 2, T])
        ik = at("ik", 77, [P, T])
        score = at("score", 16, [P, T])
        bias = at("bias", 18, [P, NT - 1, T])
        logit = [tmp[0][:, i, :] for i in range(2)]
        prob = [tmp[1][:, i, :] for i in range(2)]
        probT = [tmp[2][:, i, :] for i in range(2)]
        merged = at("merged", 32, [P, DC, T])
        early = [at(f"early{i}", 24 + 4 * i, [P, 2, T]) for i in range(2)]
        late = [tmp[0], tmp[1]]
        fh = [at(f"fh{i}", 32 * i, [P, 8, T], F32R) for i in range(2)]
        fl = [at(f"fl{i}", 32 * i + 16, [P, 8, T], F32R) for i in range(2)]
        xtok = at("xtok", 32, [P, NT, D])
        vrow = at("vrow", 48, [N_VEC, P])
        crow = at("crow", 49, [2 * FC, 3, P])
        mrow = at("mrow", 51, [P, (N_SUM + LEVELS + 1) * P])
        posi = at("posi", 60, [P, T], I32)
        assert arena + 79 * 1024 <= nc.sbuf_usable_end, (arena, nc.sbuf_usable_end)

        S = Semaphores(lambda name: ctx.enter_context(nc.semaphore(name)))
        raw_in = [S.raw_in0, S.raw_in1, S.raw_in2]
        pair_free = [S.pair_free0, S.pair_free1]
        panel_end = [0] * n_panels
        block = ctx.enter_context(nc.Block())

        class Turns:
            def __init__(self):
                self.at = {}

            def up(self, sem, by=1):
                self.at[sem.name] = self.at.get(sem.name, 0) + by
                return self.at[sem.name]

        def take_on(side, steps):
            for _ in range(steps):
                next(side)

        def finish(side):
            for _ in side:
                pass

        def wview(t, p):
            nk, width = panels[p][1:3]
            return t[p % 3][:, 0:nk * width].rearrange("p (k n) -> p k n", k=nk)

        @block.tensor
        def _(pe):
            t = Turns()
            n = Place()
            mm = nc.tensor.matmul

            def panel():
                pe.wait_ge(S.lo_done, n.p + 1)
                n.p += 1
                return wview(wh, n.p - 1), wview(wl, n.p - 1)

            def new_pair():
                if n.q >= 2:
                    pe.wait_ge(pair_free[n.q % 2], n.q // 2)
                n.q += 1
                return pair[(n.q - 1) % 2]

            def products(dst, terms, first, last):
                todo = [xy for h, l, r, q in terms for xy in ((h, r), (h, q), (l, r))]
                for i, (x, y) in enumerate(todo):
                    ins = mm(dst, x, y, start=first and i == 0, stop=last and i == len(todo) - 1)
                return ins

            def project(xh, xl, offsets=(0, P), w=None):
                h, l = w or panel()
                dst = new_pair()
                nk = h.shape[1]
                for i, off in enumerate(offsets):
                    for k0 in range(0, nk, 4):
                        ks = range(k0, min(k0 + 4, nk))
                        if n.fresh and i == 0:
                            for k in ks:
                                pe.wait_ge(S.n_lo, t.up(S.n_lo))
                                ins = products(dst[:, i, :], [(h[:, k, off:off + P], l[:, k, off:off + P], xh[:, k, :], xl[:, k, :])],
                                               k == 0, k == nk - 1)
                        else:
                            ins = products(dst[:, i, :], [(h[:, k, off:off + P], l[:, k, off:off + P], xh[:, k, :], xl[:, k, :])
                                                          for k in ks], k0 == 0, k0 + 4 >= nk)
                        if i == len(offsets) - 1 and k0 + 4 >= nk:
                            ins.then_inc(S.pair_full, 1)
                            panel_end[n.p - 1] = n.q
                        yield
                n.fresh = False
                return h, l

            def project_tokens(width=256):
                h, l = panel()
                dst = new_pair()
                for m in range(NT):
                    tok = slice(m * P, (m + 1) * P)
                    ins = products(dst[:, m // 2, 256 * (m % 2):256 * (m % 2) + width],
                                   [(uh[:, k, tok], ul[:, k, tok], h[:, k, 0:width], l[:, k, 0:width]) for k in range(DC)],
                                   True, True)
                    if m == NT - 1:
                        ins.then_inc(S.pair_full, 1)
                        panel_end[n.p - 1] = n.q
                    yield

            def sum_squares(s):
                pe.wait_ge(S.n_square, t.up(S.n_square))
                for i in range(2):
                    ins = mm(X[0], ones[:], tmp[s % 2][:, i, :], start=(s + i == 0), stop=(s + i == DC // 2))
                ins.then_inc(S.n_summed, 1)

            def residual(xh, xl, squares=True):
                for s in range(DC // 2):
                    finish(project(xh, xl))
                    if squares and s > 0:
                        sum_squares(s - 1)
                if squares:
                    sum_squares(DC // 2 - 1)
                    n.fresh = True

            def core(side, total, logs=0):
                def turn_logs(u):
                    m, hp = u // 2, u % 2
                    for i in range(2):
                        ins = nc.tensor.transpose(X[0][:, i * P:(i + 1) * P], lg[:, 2 * hp + i, m * P:(m + 1) * P], ident)
                    ins.then_inc(S.lg_T, 1)

                pe.wait_ge(S.lg_ready, t.up(S.lg_ready))
                pe.wait_ge(pair_free[(n.q - 1) % 2], (n.q - 1) // 2 + 1)
                if logs:
                    pe.wait_ge(S.ln_done, t.up(S.ln_done, logs))
                turn_logs(0)
                for u in range(CORE_UNITS):
                    m, hp = u // 2, u % 2
                    tok = slice(m * P, (m + 1) * P)
                    pe.wait_ge(S.lt_lo, t.up(S.lt_lo))
                    if u > 0:
                        pe.wait_ge(S.state_done, t.up(S.state_done))
                    for i in range(2):
                        if i > 0:
                            take_on(side, core_steps(total, u, 0))
                            pe.wait_ge(S.dec_done, t.up(S.dec_done))
                        for b in range(3):
                            cols = slice(3 * P * b, 3 * P * (b + 1))
                            mm(X[1 + b][:, 0:3 * P], lth[:, u % 2, i, :], summask[:, cols], start=True, stop=False)
                            ins = mm(X[1 + b][:, 0:3 * P], ltl[:, u % 2, i, :], summask[:, cols], start=False, stop=True)
                        ins.then_inc(S.sums_done, 1)
                    if u + 1 < CORE_UNITS:
                        if u > 0:
                            pe.wait_ge(S.out_read, t.up(S.out_read))
                        turn_logs(u + 1)
                    take_on(side, core_steps(total, u, 1))
                    pe.wait_ge(S.dec_done, t.up(S.dec_done))
                    pe.wait_ge(S.kd_ready, t.up(S.kd_ready))
                    if u + 1 == CORE_UNITS:
                        pe.wait_ge(S.out_read, t.up(S.out_read))
                    for i in range(2):
                        ins = nc.tensor.transpose(X[0][:, i * P:(i + 1) * P], dec[:, i, LEVELS + 1, :], ident)
                    ins.then_inc(S.kd_T, 1)
                    for l in range(LEVELS + 1):
                        if l < LEVELS:
                            pe.wait_ge(S.lev_ready, t.up(S.lev_ready))
                        if l == 6:
                            take_on(side, core_steps(total, u, 2))
                            pe.wait_ge(S.pairs_done, t.up(S.pairs_done))
                        for i in range(2):
                            h, c = 2 * hp + i, 2 * P * (l % 2) + i * P
                            lhs, rhs = (dec[:, i, l, :], dec[:, i, l, :]) if l < LEVELS else (gk[:, h, tok], gq[:, h, tok])
                            ins = mm(X[1 + l // 2 % 3][:, c:c + P], lhs, rhs, start=True, stop=True)
                        if l % 2 == 1:
                            ins.then_inc(S.att_done, 1)
                    take_on(side, core_steps(total, u, 3))
                    pe.wait_ge(S.pairs_done, t.up(S.pairs_done, 3))
                    pe.wait_ge(S.kdt_done, t.up(S.kdt_done))
                    for i in range(2):
                        h = 2 * hp + i
                        ins = mm(X[0][:, i * P:(i + 1) * P], gv[:, m, h * P:(h + 1) * P], attT[:, i, :], start=True, stop=(m == 0))
                        if m > 0:
                            ins = mm(X[0][:, i * P:(i + 1) * P], state[:, h, :], dec[:, i, LEVELS, :], start=False, stop=True)
                    ins.then_inc(S.out_done, 1)
                    for i in range(2):
                        h = 2 * hp + i
                        ins = mm(X[1][:, i * P:(i + 1) * P], kdt[:, i, :], gv[:, m, h * P:(h + 1) * P], start=True, stop=True)
                    ins.then_inc(S.kv_done, 1)
                    take_on(side, core_steps(total, u, 4))
                pe.wait_ge(S.out_read, t.up(S.out_read))
                pe.wait_ge(S.state_done, t.up(S.state_done))
                finish(side)

            def core_post(side):
                for j in range(2):
                    finish(project(uh, ul))
                    pe.wait_ge(S.g_square, t.up(S.g_square))
                    for i in range(2):
                        ins = mm(X[i], ones[:], tmp[1][:, i, :], start=True, stop=True)
                    ins.then_inc(S.g_summed, 1)
                    take_on(side, SIDE_POST[j])
                pe.wait_ge(S.g_root, t.up(S.g_root, 2))

            def attention(q, kof, vof, blocks, side, side_steps, indexed=False):
                steps = [(m, h) for m in range(NT) for h in range(AH)]

                def qk(i):
                    m, h = steps[i]
                    half = slice(HD * (h % 2), HD * (h % 2 + 1))
                    if i >= 2:
                        pe.wait_ge(S.logit_done, t.up(S.logit_done))
                    b0, b1 = blocks(m)
                    mm(X[i % 2][:, 0:(b1 - b0) * P], q[half, h // 2, m * P:(m + 1) * P], kof(h)[:, b0 * P:b1 * P],
                       start=True, stop=True).then_inc(S.qk_done, 1)

                def pv(i):
                    m, h = steps[i]
                    b0, b1 = blocks(m)
                    if h % 2 == 0 and i >= 2:
                        pe.wait_ge(S.pv_read, t.up(S.pv_read))
                    for b in range(b0, b1):
                        ins = mm(X[3][HD * (h % 2):HD * (h % 2 + 1), 0:P], vof(h, b), probT[i % 2][:, (b - b0) * P:(b - b0 + 1) * P],
                                 start=(b == b0), stop=(b == b1 - 1))
                    ins.then_inc(S.pv_done, 1)

                qk(0)
                for i, (m, h) in enumerate(steps):
                    if indexed and h == 0 and m + 1 < NT:
                        index(m + 1)
                    if i + 1 < len(steps):
                        qk(i + 1)
                    take_on(side, share(side_steps[m], AH, h))
                    if i > 0:
                        pe.wait_ge(S.pt_read, t.up(S.pt_read))
                    pe.wait_ge(S.scaled, t.up(S.scaled))
                    b0, b1 = blocks(m)
                    for b in range(b1 - b0):
                        ins = nc.tensor.transpose(X[2][:, b * P:(b + 1) * P], prob[i % 2][:, b * P:(b + 1) * P], ident)
                    ins.then_inc(S.pt_done, 1)
                    if i > 0:
                        pv(i - 1)
                pe.wait_ge(S.pt_read, t.up(S.pt_read))
                pv(len(steps) - 1)
                pe.wait_ge(S.pv_read, t.up(S.pv_read))
                pe.wait_ge(S.logit_done, t.up(S.logit_done, 2))
                finish(side)

            def index(m):
                for j in range(2):
                    dst = new_pair()
                    for i in range(2):
                        half = slice(HD * i, HD * (i + 1))
                        ins = mm(dst[:, i, 0:(m + 1) * P], iq[half, j, m * P:(m + 1) * P], ik[half, 0:(m + 1) * P],
                                 start=True, stop=True)
                    ins.then_inc(S.pair_full, 1)

            def merge(b):
                for j in range(2):
                    yield from project(uh, ul)
                    yield from project(uh, ul)
                    w = panel()
                    if j == 0:
                        pe.wait_ge(S.branch_ready, t.up(S.branch_ready))
                    for off in (0, 256):
                        yield from project(brh[b], brl[b], (off, off + P), w)

            def merge_two():
                yield from merge(1)
                yield from merge(0)

            def output():
                pe.wait_ge(S.m_lo, t.up(S.m_lo, 4))
                residual(uh, ul)

            def ffn(squares=True):
                for step, third in FFN_STEPS:
                    if step == "up":
                        for _ in range(2 * THIRDS[third]):
                            finish(project(uh, ul))
                    else:
                        pe.wait_ge(S.f_lo, t.up(S.f_lo, THIRDS[third]))
                        residual(fh[third % 2], fl[third % 2], squares and third == 2)

            def side_core_1():
                for _ in range(8):
                    yield from project(uh, ul)
                w = yield from project(uh, ul, (0, HD))
                yield from project(uh, ul, (P,), w)
                yield from project_tokens(P)

            def turn():
                q = n.q - 1 if n.bare else n.q - 2
                dst = new_pair()
                pe.wait_ge(pair_free[q % 2], q // 2 + 1)
                for i in range(2):
                    ins = mm(dst[:, i, :], rot, tmp[2][:, i, :], start=True, stop=True)
                ins.then_inc(S.pair_full, 1)

            def side_core_2():
                for _ in range(4):
                    yield from project(uh, ul)
                    dst = new_pair()
                    pe.wait_ge(S.r_square, t.up(S.r_square))
                    for i in range(2):
                        ins = mm(dst[:, i, :], blk, tmp[0][:, i, :], start=True, stop=True)
                    ins.then_inc(S.pair_full, 1)
                    yield
                    n.bare = False
                    turn()
                    yield
                yield from project(uh, ul)
                n.bare = True
                turn()
                yield
                h, l = panel()
                dst = new_pair()
                for m in range(NT):
                    tok = slice(m * P, (m + 1) * P)
                    ins = products(dst[:, 0, 4 * m:4 * m + 4],
                                   [(uh[:, c, tok], ul[:, c, tok], h[:, c, P:P + 4], l[:, c, P:P + 4]) for c in range(DC)],
                                   True, True)
                ins.then_inc(S.pair_full, 1)
                yield
                yield from project(uh, ul, (HD, 0), (h, l))
                turn()
                yield
                yield from project_tokens()
                yield from project_tokens()

            pe.wait_ge(S.consts_in, 16 * N_LOADS)
            nc.tensor.transpose(X[0][:, 0:N_VEC], vrow[:], ident[0:N_VEC, 0:N_VEC])
            for k in range(3):
                ins = nc.tensor.transpose(X[1][:, k * 2 * FC:(k + 1) * 2 * FC], crow[:, k, :], ident[0:2 * FC, 0:2 * FC])
            ins.then_inc(S.vec_T, 1)
            pe.wait_ge(S.x_in, 16)
            pe.wait_ge(S.vec_ready, 1)
            for c in range(DC):
                if c >= 4:
                    pe.wait_ge(S.x_copied, t.up(S.x_copied))
                for m in range(NT):
                    ins = nc.tensor.transpose(X[c % 4][:, m * P:(m + 1) * P], xtok[:, m, c * P:(c + 1) * P], ident)
                ins.then_inc(S.x_T, 1)
            pe.wait_ge(S.x_copied, t.up(S.x_copied, 4))
            for s in range(DC // 2):
                sum_squares(s)
            n.fresh = True

            for _ in range(4):
                finish(project(uh, ul))
            finish(project(uh, ul, (0,)))
            finish(project_tokens())
            finish(project_tokens())
            pe.wait_ge(pair_free[(n.q - 3) % 2], (n.q - 3) // 2 + 1)
            for c in range(MC):
                ins = mm(X[c], walpha[:, c * P:(c + 1) * P], gaT[:], start=True, stop=True)
            ins.then_inc(S.alpha_done, 1)
            core(side_core_1(), SIDE_CORE_1)
            side = merge_two()
            core_post(side)
            attention(sq, lambda h: sk[HD * (h % 2):HD * (h % 2 + 1), h // 4, :],
                      lambda h, b: sv[:, b, HD * (h // 4):HD * (h // 4 + 1)], lambda m: (max(m - 1, 0), m + 1),
                      side, SIDE_WINDOW)
            finish(merge(2))
            output()
            ffn()
            n.fresh = False
            for s in range(DC // 2):
                sum_squares(s)
            n.fresh = True

            for l in range(LAYERS):
                for _ in range(4):
                    finish(project(uh, ul))
                finish(project_tokens())
                finish(project_tokens())
                core(side_core_2(), SIDE_CORE_2, 2 * l)
                side = merge(0)
                core_post(side)
                attention(aq, lambda h: ak[HD * (h % 2):HD * (h % 2 + 1), h // 2, :],
                          lambda h, b: av[:, b, HD * h:HD * (h + 1)], lambda m: (0, m + 1),
                          side, SIDE_SPARSE, True)
                finish(merge(2))
                output()
                ffn(l + 1 < LAYERS)

            pe.wait_ge(pair_free[(n.q - 1) % 2], (n.q - 1) // 2 + 1)
            for i in range(2 * NT):
                m, half = i // 2, i % 2
                if i >= 4:
                    pe.wait_ge(S.y_out, t.up(S.y_out))
                for c in range(4):
                    ins = nc.tensor.transpose(X[i % 4][:, c * P:(c + 1) * P], xT[:, 4 * half + c, m * P:(m + 1) * P], ident)
                ins.then_inc(S.y_T, 1)

        @block.sync
        def _(sp):
            sp.dma_start(xtok[:], a["x"][0].rearrange("(n p) d -> p n d", p=P)).then_inc(S.x_in, 16)
            loads = [(const[:], a["c_const"]), (mrow[:], a["c_masks"]),
                     (crow[:], a["ffn_conv_w"][0].rearrange("k (c p) -> c k p", p=P)),
                     (walpha[:], a["gla_w_alpha"][0]),
                     (sinks[:], a["swa_sinks"].partition_broadcast(P)),
                     (posi[:], a["positions_2"].partition_broadcast(P))]

            def rows(r, src):
                src = src.rearrange("a (c p) -> (a c) p", p=P)
                loads.append((vrow[r:r + src.shape[0], :], src))

            rows(V_GMIX, a["g_mix"])
            rows(V_GFFN, a["g_ffn"])
            loads.append((vrow[V_GFIN:V_GFIN + DC, :], a["g_final"].rearrange("(c p) -> c p", p=P)))
            rows(V_NMIX, a["norm_mix_2"])
            rows(V_NFFN, a["norm_ffn_2"])
            rows(V_GLAN, a["gla_norm_g"])
            rows(V_GLAB, a["gla_b_alpha"])
            rows(V_CONV, a["conv_w"][0])
            rows(V_HN, a["hgrn_norm_2"])
            rows(V_LB, a["hgrn_lower_bound_2"])
            for r, src in ((V_QN, a["q_norm_2"]), (V_KN, a["k_norm_2"])):
                for half in range(2):
                    loads.append((vrow[r:r + LAYERS, HD * half:HD * (half + 1)], src))
            assert len(loads) == N_LOADS
            for dst, src in loads:
                sp.dma_start(dst, src).then_inc(S.consts_in, 16)
            for p, (src, nk, width) in enumerate(panels):
                if p >= 3:
                    sp.wait_ge(S.pair_full, panel_end[p - 3])
                sp.dma_start(wview(raw, p), src).then_inc(raw_in[p % 3], 16)
            for n in range(NT):
                sp.wait_ge(S.y_out, 2 * n + 2)
                sp.dma_start(out[0, n * P:(n + 1) * P, :], xtok[:, n, :]).then_inc(S.out_stored, 16)
            sp.wait_ge(S.out_stored, 16 * NT)

        @block.gpsimd
        def _(pool):
            for p in range(n_panels):
                nk, width = panels[p][1:3]
                w = slice(0, nk * width)
                pool.wait_ge(S.hi_done, p + 1)
                nc.gpsimd.tensor_tensor(wl[p % 3][:, w], raw[p % 3][:, w], wh[p % 3][:, w].bitcast(F32),
                                        ALU.subtract).then_inc(S.lo_done, 1)

        @block.scalar
        def _(act):
            t = Turns()
            n = Place()
            fn = nc.scalar.activation

            def ahead():
                while n.hi < n_panels and (n.hi < 3 or panel_end[n.hi - 3] < n.q):
                    p = n.hi
                    nk, width = panels[p][1:3]
                    act.wait_ge(raw_in[p % 3], 16 * (p // 3 + 1))
                    nc.scalar.copy(wh[p % 3][:, 0:nk * width], raw[p % 3][:, 0:nk * width]).then_inc(S.hi_done, 1)
                    n.hi += 1

            def next_pair(new_panel=True):
                if new_panel:
                    n.p += 1
                n.q += 1
                return pair[(n.q - 1) % 2]

            def evict(dst, tokens=None, **kw):
                yield from wait_steps(3)
                src = next_pair()
                if tokens:
                    src = src.rearrange("p b (x c) -> p b x c", x=2)[:, :, :, 0:tokens]
                    dst = dst.rearrange("p (b x) c -> p b x c", b=2)
                act.wait_ge(S.pair_full, n.q)
                fn(dst, src, ACT.Copy, **kw).then_inc(pair_free[(n.q - 1) % 2], 1)
                ahead()
                yield

            def wait_steps(k):
                for _ in range(k):
                    yield

            def passed(steps, new_panel=True):
                yield from wait_steps(steps - 1)
                next_pair(new_panel)
                ahead()
                yield

            def squares(of):
                for s in range(DC // 2):
                    if of == "residual":
                        next_pair()
                        ahead()
                        act.wait_ge(pair_free[(n.q - 1) % 2], (n.q - 1) // 2 + 1)
                    elif of == "input":
                        act.wait_ge(S.x_copied, t.up(S.x_copied, 2))
                    else:
                        act.wait_ge(S.n_normed, t.up(S.n_normed, 2))
                    if s >= 2:
                        act.wait_ge(S.n_summed, t.up(S.n_summed))
                    fn(tmp[s % 2][:], xT[:, 2 * s:2 * s + 2, :], ACT.Square).then_inc(S.n_square, 1)

            def norm(split=True):
                act.wait_ge(S.n_summed, t.up(S.n_summed, 2))
                fn(tmp[2][:, 0, :], X[0], ACT.Sqrt, bias=small[:, 0:1], scale=1.0 / D).then_inc(S.n_root, 1)
                if split:
                    for c in range(DC):
                        act.wait_ge(S.n_normed, t.up(S.n_normed))
                        nc.scalar.copy(uh[:, c, :], tmp[3][:, c % 2, :]).then_inc(S.n_hi, 1)

            def soft(src, dst, b=None):
                if b is None:
                    fn(dst, src, ACT.Abs).then_inc(S.act_chain, 1)
                else:
                    fn(dst[:, 0, :], src[:, 0, :], ACT.Abs, bias=b[:, 0:1])
                    fn(dst[:, 1, :], src[:, 1, :], ACT.Abs, bias=b[:, 1:2]).then_inc(S.act_chain, 1)
                act.wait_ge(S.act_chain, t.up(S.act_chain))
                fn(dst, dst, ACT.Exp, scale=-1.0).then_inc(S.act_chain, 1)
                act.wait_ge(S.act_chain, t.up(S.act_chain))
                return fn(dst, dst, ACT.Ln, bias=1.0)

            def core(scale, side, total):
                def copy_logs(u):
                    act.wait_ge(S.lg_T, t.up(S.lg_T))
                    fn(lth[:, u % 2, :, :], X[0][:, 0:2 * P].rearrange("p (h f) -> p h f", h=2), ACT.Copy,
                       scale=scale).then_inc(S.lt_hi, 1)

                copy_logs(0)
                for u in range(CORE_UNITS):
                    for i in range(2):
                        if i > 0:
                            take_on(side, core_steps(total, u, 0))
                        act.wait_ge(S.sums_done, t.up(S.sums_done))
                        fn(dec[:, i, :, :].rearrange("p (b l) t -> p b (l t)", b=3), X4[:, 1:4, 0:3 * P],
                           ACT.Exp).then_inc(S.dec_done, 1)
                    if u + 1 < CORE_UNITS:
                        copy_logs(u + 1)
                    take_on(side, core_steps(total, u, 1))
                    act.wait_ge(S.kd_T, t.up(S.kd_T))
                    nc.scalar.copy(kdt[:], X[0][:, 0:2 * P].rearrange("p (h f) -> p h f", h=2)).then_inc(S.kdt_done, 1)
                    for slot in (2, 3, 4):
                        take_on(side, core_steps(total, u, slot))
                finish(side)

            def inverse_root(src, scale, x, y, free):
                fn(x, src, ACT.Identity, bias=small[:, 0:1], scale=scale).then_inc(free, 1)
                act.wait_ge(free, t.up(free) if free is S.act_chain else (n.q - 1) // 2 + 1)
                fn(y, x, ACT.Ln).then_inc(S.act_chain, 1)
                act.wait_ge(S.act_chain, t.up(S.act_chain))
                fn(y, y, ACT.Exp, scale=-0.5).then_inc(S.act_chain, 1)
                act.wait_ge(S.act_chain, t.up(S.act_chain))
                return fn(tmp[3][:], y, ACT.Square)

            def core_post(side):
                act.wait_ge(S.out_read, t.up(S.out_read, CORE_UNITS))
                for j in range(2):
                    heads = slice(2 * j, 2 * j + 2)
                    fn(tmp[1][:], gq[:, heads, :], ACT.Square).then_inc(S.g_square, 1)
                    src = next_pair()
                    act.wait_ge(S.pair_full, n.q)
                    fn(tmp[0][:], src, ACT.Silu).then_inc(pair_free[(n.q - 1) % 2], 1)
                    ahead()
                    act.wait_ge(S.g_summed, t.up(S.g_summed))
                    if j:
                        act.wait_ge(S.g_split, t.up(S.g_split))
                    inverse_root(X4[:, 0:2, :], 1.0 / P, tmp[1][:], tmp[2][:], S.act_chain).then_inc(S.g_root, 1)
                    act.wait_ge(S.g_prod, t.up(S.g_prod))
                    nc.scalar.copy(brh[0][:, heads, :], tmp[3][:]).then_inc(S.b_hi, 1)
                    take_on(side, SIDE_POST[j])

            def attention(blocks, sink, side, side_steps):
                steps = [(m, h) for m in range(NT) for h in range(AH)]

                def exps(i):
                    m, h = steps[i]
                    kk = (blocks(m)[1] - blocks(m)[0]) * P
                    st = stat[:, 8 * (i % 2):8 * (i % 2) + 8]
                    act.wait_ge(S.negmax, t.up(S.negmax))
                    if sink:
                        fn(st[:, 3:4], sinks[:, h:h + 1], ACT.Exp, bias=st[:, 1:2])
                    fn(prob[i % 2][:, 0:kk], logit[i % 2][:, 0:kk], ACT.Exp, bias=st[:, 1:2],
                       accum_out=st[:, 2:3]).then_inc(S.prob_done, 1)

                exps(0)
                for i, (m, h) in enumerate(steps):
                    if not sink and h == 0 and m + 1 < NT:
                        for j in range(2):
                            kk = (m + 2) * P
                            src = next_pair(False)
                            act.wait_ge(S.pair_full, n.q)
                            if j > 0:
                                act.wait_ge(S.i_scored, t.up(S.i_scored))
                            fn(tmp[3][:, :, 0:kk], src[:, :, 0:kk], ACT.Relu).then_inc(pair_free[(n.q - 1) % 2], 1)
                        act.wait_ge(S.i_scored, t.up(S.i_scored))
                    if i + 1 < len(steps):
                        exps(i + 1)
                    take_on(side, share(side_steps[m], AH, h))
                    kk = (blocks(m)[1] - blocks(m)[0]) * P
                    act.wait_ge(S.pt_done, t.up(S.pt_done))
                    nc.scalar.copy(probT[i % 2][:, 0:kk], X[2][:, 0:kk]).then_inc(S.pt_read, 1)
                act.wait_ge(S.pv_read, t.up(S.pv_read, len(steps) // 2))
                src = sq if sink else aq
                finish(side)
                for j in range(2):
                    nc.scalar.copy(brh[2][:, 2 * j:2 * j + 2, :], src[:, 2 * j:2 * j + 2, :]).then_inc(S.b_hi, 1)

            def merge(gates):
                for j in range(2):
                    for i in range(2):
                        yield from wait_steps(3)
                        src = next_pair()
                        act.wait_ge(S.pair_full, n.q)
                        if i == 0 and n.merged:
                            act.wait_ge(pair_free[(n.merged - 1) % 2], (n.merged - 1) // 2 + 1)
                        fn(gates[i][:], src, ACT.Tanh, scale=0.5).then_inc(pair_free[(n.q - 1) % 2], 1)
                        ahead()
                        yield
                    yield from passed(2)
                    yield from passed(2, False)
                    n.merged = n.q

            def merge_two():
                yield from merge(early)
                yield from merge(early)

            def output():
                for s in range(4):
                    act.wait_ge(S.y_added, t.up(S.y_added))
                    fn(uh[:, 2 * s:2 * s + 2, :], merged[:, 2 * s:2 * s + 2, :], ACT.Copy, scale=0.5).then_inc(S.m_hi, 1)
                squares("residual")

            def ffn(conv, last=False):
                for step, third in FFN_STEPS:
                    i0 = sum(THIRDS[:third])
                    if step == "down":
                        if third == 2 and not last:
                            squares("residual")
                        else:
                            for _ in range(DC // 2):
                                finish(passed(1))
                        continue
                    for i in range(i0, i0 + THIRDS[third]):
                        if conv:
                            for part in range(2):
                                src = next_pair()
                                act.wait_ge(S.pair_full, n.q)
                                for c in range(2):
                                    ch = part * FC + 2 * i + c
                                    ins = fn(tmp[part][:, c, :], src[:, c, :], ACT.Copy, scale=fconv[:, 2, ch:ch + 1])
                                ins.then_inc(S.f_tap, 1)
                                ahead()
                            act.wait_ge(pair_free[(n.q - 2) % 2], (n.q - 2) // 2 + 1)
                            fn(tmp[0][:], tmp[0][:], ACT.Silu).then_inc(S.f_silu, 1)
                            act.wait_ge(S.f_mult, t.up(S.f_mult))
                        else:
                            src = next_pair()
                            act.wait_ge(S.pair_full, n.q)
                            fn(tmp[0][:], src, ACT.Silu).then_inc(pair_free[(n.q - 1) % 2], 1)
                            ahead()
                            next_pair()
                            ahead()
                            act.wait_ge(pair_free[(n.q - 1) % 2], (n.q - 1) // 2 + 1)
                        c = 2 * (i - i0)
                        nc.scalar.copy(fh[third % 2][:, c:c + 2, :], tmp[2][:]).then_inc(S.f_hi, 1)

            def side_core_1():
                for j in range(2):
                    yield from passed(4)
                    yield from passed(4)
                    yield from passed(4)
                    act.wait_ge(pair_free[(n.q - 1) % 2], (n.q - 1) // 2 + 1)
                    nc.scalar.copy(brh[1][:, 2 * j:2 * j + 2, :], tmp[3][:]).then_inc(S.b_hi, 1)
                for j in range(2):
                    yield from evict(sq[:, 2 * j:2 * j + 2, :], scale=HD ** -0.5)
                yield from passed(4)
                yield from passed(2, False)
                yield from evict(sv[:], P)

            def side_core_2():
                for j in range(4):
                    yield from wait_steps(3)
                    src = next_pair()
                    act.wait_ge(S.pair_full, n.q)
                    fn(tmp[0][:], src, ACT.Square).then_inc(S.r_square, 1)
                    ahead()
                    yield
                    src = next_pair(False)
                    if j:
                        act.wait_ge(S.rope_done, t.up(S.rope_done))
                    act.wait_ge(S.pair_full, n.q)
                    inverse_root(src, 1.0 / HD, tmp[1][:], tmp[0][:], pair_free[(n.q - 1) % 2]).then_inc(S.r_root, 1)
                    yield
                    next_pair(False)
                    yield
                yield from passed(4)
                yield from passed(1, False)
                yield from passed(1)
                yield from passed(4, False)
                yield from passed(1, False)
                for j in range(2):
                    yield from evict(av[:, :, 256 * j:256 * j + 256], 256)
                act.wait_ge(S.rope_done, t.up(S.rope_done, 3))

            ahead()
            act.wait_ge(S.setup_done, 1)
            fn(sinT[:], tmp[3][:, 0, :], ACT.Sin)
            fn(cosT[:], tmp[3][:, 1, :], ACT.Sin)
            fn(small[:, 1:5], small[:, 11:15], ACT.Sigmoid)
            fn(small[:, 5:9], small[:, 15:19], ACT.Sigmoid).then_inc(S.trig_done, 1)

            squares("input")
            norm()
            finish(passed(1))
            finish(passed(1))
            for j in range(2):
                finish(evict(gq[:, 2 * j:2 * j + 2, :], scale=P ** -0.5))
            finish(passed(1))
            for j in range(2):
                finish(evict(gv[:, :, 256 * j:256 * j + 256], 256))
            act.wait_ge(S.alpha_done, 1)
            for j in range(2):
                soft(X4[:, 2 * j:2 * j + 2, :], tmp[2 * j][:],
                     vec[:, V_GLAB + 2 * j:V_GLAB + 2 * j + 2]).then_inc(S.soft_done, 1)
            core(1.0 / GLA_TAU, side_core_1(), SIDE_CORE_1)
            n.merged = 0
            side = merge_two()
            core_post(side)
            attention(lambda m: (max(m - 1, 0), m + 1), True, side, SIDE_WINDOW)
            n.merged = 0
            finish(merge(late))
            output()
            norm()
            ffn(True)
            norm(split=False)
            squares("normed")

            for l in range(LAYERS):
                norm()
                for j in range(2):
                    src = next_pair()
                    act.wait_ge(S.pair_full, n.q)
                    ta, tb = tmp[2 * j], tmp[2 * j + 1]
                    if l == 0:
                        soft(src, ta[:])
                        fn(gk[:, 2 * j:2 * j + 2, :], src, ACT.Sigmoid, scale=-1.0).then_inc(S.soft_done, 1)
                    else:
                        fn(ta[:], src, ACT.Sigmoid)
                        fn(tb[:], src, ACT.Sigmoid, scale=-1.0).then_inc(S.soft_done, 1)
                        act.wait_ge(S.decay_up, t.up(S.decay_up))
                        fn(lg[:, 2 * j:2 * j + 2, :], ta[:], ACT.Ln).then_inc(S.ln_done, 1)
                    ahead()
                for j in range(2):
                    src = next_pair()
                    act.wait_ge(S.pair_full, n.q)
                    fn(gq[:, 2 * j:2 * j + 2, :], src, ACT.Silu).then_inc(pair_free[(n.q - 1) % 2], 1)
                    ahead()
                for j in range(2):
                    finish(evict(gv[:, :, 256 * j:256 * j + 256], 256))
                core(1.0, side_core_2(), SIDE_CORE_2)
                n.merged = 0
                side = merge(early)
                core_post(side)
                attention(lambda m: (0, m + 1), False, side, SIDE_SPARSE)
                n.merged = 0
                finish(merge(late))
                output()
                norm()
                ffn(False, l + 1 == LAYERS)

        @block.vector
        def _(dve):
            t = Turns()
            n = Place()
            v = nc.vector

            def next_pair():
                n.q += 1
                return pair[(n.q - 1) % 2]

            def wait_steps(k):
                for _ in range(k):
                    yield

            def passed(steps):
                yield from wait_steps(steps - 1)
                next_pair()
                yield

            def low(dst, src, high, sem=S.dve_chain):
                v.tensor_tensor(dst, src, high.bitcast(F32), ALU.subtract).then_inc(sem, 1)
                dve.wait_ge(sem, t.up(sem))

            def norm(g, split=True):
                dve.wait_ge(S.n_root, t.up(S.n_root))
                v.reciprocal(tmp[2][:, 1, :], tmp[2][:, 0, :]).then_inc(S.dve_chain, 1)
                dve.wait_ge(S.dve_chain, t.up(S.dve_chain))

                def scaled(c):
                    dst = tmp[3][:, c % 2, :] if split else xT[:, c, :]
                    v.scalar_tensor_tensor(dst, xT[:, c, :], vec[:, g + c:g + c + 1], tmp[2][:, 1, :],
                                                  ALU.mult, ALU.mult).then_inc(S.n_normed, 1)
                    dve.wait_ge(S.n_normed, t.up(S.n_normed))

                if not split:
                    for c in range(DC):
                        scaled(c)
                    return
                scaled(0)
                for c in range(DC):
                    if c + 1 < DC:
                        scaled(c + 1)
                    dve.wait_ge(S.n_hi, t.up(S.n_hi))
                    low(ul[:, c, :], tmp[3][:, c % 2, :], uh[:, c, :], S.n_lo)

            def core(scale, side, total):
                v.memset(attT[:], 0.0).then_inc(S.dve_chain, 1)
                dve.wait_ge(S.dve_chain, t.up(S.dve_chain))
                decay = small[:, 20:22]

                def low_logs(u):
                    dve.wait_ge(S.lt_hi, t.up(S.lt_hi))
                    v.scalar_tensor_tensor(ltl[:, u % 2, :, :], X[0][:, 0:2 * P].rearrange("p (h f) -> p h f", h=2), scale,
                                           lth[:, u % 2, :, :].bitcast(F32), ALU.mult, ALU.subtract).then_inc(S.lt_lo, 1)

                low_logs(0)
                for u in range(CORE_UNITS):
                    m, hp = u // 2, u % 2
                    tok, heads = slice(m * P, (m + 1) * P), slice(2 * hp, 2 * hp + 2)
                    take_on(side, core_steps(total, u, 0))
                    dve.wait_ge(S.dec_done, t.up(S.dec_done, 2))
                    v.tensor_copy(decay, dec[:, :, LEVELS, P - 1]).then_inc(S.dve_chain, 1)
                    dve.wait_ge(S.dve_chain, t.up(S.dve_chain))
                    if u + 1 < CORE_UNITS:
                        low_logs(u + 1)
                    v.tensor_tensor(dec[:, :, LEVELS + 1, :], dec[:, :, LEVELS + 1, :], gk[:, heads, tok],
                                    ALU.mult).then_inc(S.kd_ready, 1)
                    v.tensor_tensor(dec[:, :, LEVELS, :], dec[:, :, LEVELS, :], gq[:, heads, tok], ALU.mult)
                    for l in range(LEVELS):
                        w = P >> (l + 1)
                        form = lambda x: x.rearrange("p h (g two w) -> p h g two w", two=2, w=w)
                        e, q, k = form(dec[:, :, l, :]), form(gq[:, heads, tok]), form(gk[:, heads, tok])
                        for part, x in ((1, q), (0, k)):
                            ins = v.tensor_tensor(e[:, :, :, part, :], e[:, :, :, part, :], x[:, :, :, part, :], ALU.mult)
                        ins.then_inc(S.lev_ready, 1)
                    take_on(side, core_steps(total, u, 1))
                    for l in range(LEVELS + 1):
                        if l == 6:
                            take_on(side, core_steps(total, u, 2))
                        if l % 2 == 0:
                            dve.wait_ge(S.att_done, t.up(S.att_done))
                        mask = pairmask[:, l, :].unsqueeze(1).to_broadcast([P, 2, P])
                        src = X[1 + l // 2 % 3][:, 2 * P * (l % 2):2 * P * (l % 2 + 1)].rearrange("p (h t) -> p h t", h=2)
                        signal = S.pairs_done if l % 2 else S.dve_chain
                        v.copy_predicated(attT[:], mask, src).then_inc(signal, 1)
                        dve.wait_ge(signal, t.up(signal))
                    take_on(side, core_steps(total, u, 3))
                    dve.wait_ge(S.out_done, t.up(S.out_done))
                    v.tensor_copy(gq[:, heads, tok], X[0][:, 0:2 * P].rearrange("p (h t) -> p h t", h=2)).then_inc(S.out_read, 1)
                    dve.wait_ge(S.kv_done, t.up(S.kv_done))
                    kv = X[1][:, 0:2 * P].rearrange("p (h f) -> p h f", h=2)
                    if m == 0:
                        v.tensor_copy(state[:, heads, :], kv).then_inc(S.state_done, 1)
                    else:
                        for i in range(2):
                            h = 2 * hp + i
                            ins = v.scalar_tensor_tensor(state[:, h, :], state[:, h, :], decay[:, i:i + 1], kv[:, i, :],
                                                         ALU.mult, ALU.add)
                        ins.then_inc(S.state_done, 1)
                    dve.wait_ge(S.state_done, t.up(S.state_done))
                    take_on(side, core_steps(total, u, 4))
                finish(side)

            def newton(x, y):
                v.tensor_tensor(tmp[3][:], tmp[3][:], x, ALU.mult).then_inc(S.dve_chain, 1)
                dve.wait_ge(S.dve_chain, t.up(S.dve_chain))
                v.scalar_tensor_tensor(tmp[3][:], tmp[3][:], 3.0, y, ALU.subtract, ALU.mult).then_inc(S.dve_chain, 1)
                dve.wait_ge(S.dve_chain, t.up(S.dve_chain))

            def core_post(g, same, side):
                for j in range(2):
                    next_pair()
                    dve.wait_ge(S.g_root, t.up(S.g_root))
                    newton(tmp[1][:], tmp[2][:])
                    for i in range(2):
                        col = g if same else g + 2 * j + i
                        ins = v.scalar_tensor_tensor(tmp[3][:, i, :], gq[:, 2 * j + i, :], vech[:, col:col + 1],
                                                     tmp[3][:, i, :], ALU.mult, ALU.mult)
                    ins.then_inc(S.dve_chain, 1)
                    dve.wait_ge(S.dve_chain, t.up(S.dve_chain))
                    v.tensor_tensor(tmp[3][:], tmp[3][:], tmp[0][:], ALU.mult).then_inc(S.g_prod, 1)
                    dve.wait_ge(S.g_prod, t.up(S.g_prod))
                    dve.wait_ge(S.b_hi, t.up(S.b_hi))
                    low(brl[0][:, 2 * j:2 * j + 2, :], tmp[3][:], brh[0][:, 2 * j:2 * j + 2, :],
                        S.branch_ready if j else S.g_split)
                    take_on(side, SIDE_POST[j])

            def attention(blocks, sink, side, side_steps):
                steps = [(m, h) for m in range(NT) for h in range(AH)]
                dst = sq if sink else aq

                def front(i):
                    m, h = steps[i]
                    kk = (blocks(m)[1] - blocks(m)[0]) * P
                    st = stat[:, 8 * (i % 2):8 * (i % 2) + 8]
                    dve.wait_ge(S.qk_done, t.up(S.qk_done))
                    if sink:
                        v.scalar_tensor_tensor(logit[i % 2][:, 0:kk], dist[:, 2 * P - kk:2 * P], -SLOPES[h],
                                                      X[i % 2][:, 0:kk], ALU.mult, ALU.add).then_inc(S.logit_done, 1)
                        dve.wait_ge(S.logit_done, t.up(S.logit_done))
                        v.tensor_reduce(st[:, 0:1], logit[i % 2][:, 0:kk], AX, ALU.max).then_inc(S.dve_chain, 1)
                        dve.wait_ge(S.dve_chain, t.up(S.dve_chain))
                        v.tensor_scalar(st[:, 1:2], st[:, 0:1], sinks[:, h:h + 1], -1.0, ALU.max, ALU.mult).then_inc(S.negmax, 1)
                    else:
                        mask = causal if m == 0 else bias[:, m - 1, 0:kk]
                        v.tensor_tensor_reduce(out=logit[i % 2][:, 0:kk], in0=X[i % 2][:, 0:kk], in1=mask, scale=1.0,
                                                      scalar=TAKEN, op0=ALU.add, op1=ALU.max, accum_out=st[:, 0:1]).then_inc(S.logit_done, 1)
                        dve.wait_ge(S.logit_done, t.up(S.logit_done))
                        v.tensor_scalar(st[:, 1:2], st[:, 0:1], -1.0, None, ALU.mult).then_inc(S.negmax, 1)

                def back(i):
                    m, h = steps[i]
                    kk = (blocks(m)[1] - blocks(m)[0]) * P
                    st = stat[:, 8 * (i % 2):8 * (i % 2) + 8]
                    dve.wait_ge(S.prob_done, t.up(S.prob_done))
                    if sink:
                        v.tensor_tensor(st[:, 2:3], st[:, 2:3], st[:, 3:4], ALU.add).then_inc(S.dve_chain, 1)
                        dve.wait_ge(S.dve_chain, t.up(S.dve_chain))
                    v.reciprocal(st[:, 4:5], st[:, 2:3]).then_inc(S.dve_chain, 1)
                    dve.wait_ge(S.dve_chain, t.up(S.dve_chain))
                    v.tensor_scalar(prob[i % 2][:, 0:kk], prob[i % 2][:, 0:kk], st[:, 4:5], None, ALU.mult).then_inc(S.scaled, 1)
                    dve.wait_ge(S.scaled, t.up(S.scaled))

                def out(i):
                    m, h = steps[i]
                    dve.wait_ge(S.pv_done, t.up(S.pv_done, 2))
                    v.tensor_copy(dst[:, h // 2, m * P:(m + 1) * P], X[3][:, 0:P]).then_inc(S.pv_read, 1)

                front(0)
                for i, (m, h) in enumerate(steps):
                    select_more = not sink and m + 1 < NT
                    if select_more and h == AH - 1:
                        take_on(selection, 2)
                    if i + 1 < len(steps):
                        front(i + 1)
                    if i % 2 == 1 and i > 1:
                        out(i - 2)
                    back(i)
                    if select_more and h == 0:
                        selection = select(m + 1)
                        next(selection)
                    if select_more and h < AH - 1:
                        take_on(selection, 2)
                    take_on(side, share(side_steps[m], AH, h))
                out(len(steps) - 1)
                finish(side)
                for j in range(2):
                    dve.wait_ge(S.b_hi, t.up(S.b_hi))
                    low(brl[2][:, 2 * j:2 * j + 2, :], dst[:, 2 * j:2 * j + 2, :], brh[2][:, 2 * j:2 * j + 2, :],
                        S.branch_ready if j else S.dve_chain)

            def merge(b, gates, first=False, last=False):
                for j in range(2):
                    yield from passed(4)
                    yield from passed(4)
                    dve.wait_ge(pair_free[(n.q - 2) % 2], (n.q - 2) // 2 + 1)
                    dve.wait_ge(pair_free[(n.q - 1) % 2], (n.q - 1) // 2 + 1)
                    for s in range(2):
                        yield
                        src = next_pair()
                        dve.wait_ge(S.pair_full, n.q)
                        acc = merged[:, 4 * j + 2 * s:4 * j + 2 * s + 2, :]
                        dst = acc if first else tmp[3][:]
                        v.scalar_tensor_tensor(dst, gates[s][:], 1.0, src, ALU.add, ALU.mult).then_inc(pair_free[(n.q - 1) % 2], 1)
                        dve.wait_ge(pair_free[(n.q - 1) % 2], (n.q - 1) // 2 + 1)
                        if not first:
                            signal = S.y_added if last else S.dve_chain
                            v.tensor_tensor(acc, acc, tmp[3][:], ALU.add).then_inc(signal, 1)
                            dve.wait_ge(signal, t.up(signal))
                        yield

            def merge_two():
                yield from merge(1, early, first=True)
                yield from merge(0, early)

            def output():
                for s in range(4):
                    dve.wait_ge(S.m_hi, t.up(S.m_hi))
                    v.scalar_tensor_tensor(ul[:, 2 * s:2 * s + 2, :], merged[:, 2 * s:2 * s + 2, :], 0.5,
                                           uh[:, 2 * s:2 * s + 2, :].bitcast(F32), ALU.mult, ALU.subtract).then_inc(S.m_lo, 1)
                residual()

            def residual():
                for s in range(DC // 2):
                    src = next_pair()
                    dve.wait_ge(S.pair_full, n.q)
                    x = xT[:, 2 * s:2 * s + 2, :]
                    v.tensor_tensor(x, x, src, ALU.add).then_inc(pair_free[(n.q - 1) % 2], 1)
                    dve.wait_ge(pair_free[(n.q - 1) % 2], (n.q - 1) // 2 + 1)

            def taps(y, x, w, ch):
                v.scalar_tensor_tensor(y[:, 1:T], x[:, 0:T - 1], w(1, ch), y[:, 1:T], ALU.mult, ALU.add).then_inc(S.dve_chain, 1)
                dve.wait_ge(S.dve_chain, t.up(S.dve_chain))
                return v.scalar_tensor_tensor(y[:, 2:T], x[:, 0:T - 2], w(0, ch), y[:, 2:T], ALU.mult, ALU.add)

            def ffn(conv):
                for step, third in FFN_STEPS:
                    i0 = sum(THIRDS[:third])
                    if step == "down":
                        residual()
                        continue
                    for i in range(i0, i0 + THIRDS[third]):
                        if conv:
                            for part in range(2):
                                src = next_pair()
                                dve.wait_ge(S.pair_full, n.q)
                                dve.wait_ge(S.f_tap, t.up(S.f_tap))
                                w = lambda k, ch: fconv[:, k, ch:ch + 1]
                                for c in range(2):
                                    ins = taps(tmp[part][:, c, :], src[:, c, :], w, part * FC + 2 * i + c)
                                    if c == 0:
                                        ins.then_inc(S.dve_chain, 1)
                                        dve.wait_ge(S.dve_chain, t.up(S.dve_chain))
                                ins.then_inc(pair_free[(n.q - 1) % 2], 1)
                                dve.wait_ge(pair_free[(n.q - 1) % 2], (n.q - 1) // 2 + 1)
                            dve.wait_ge(S.f_silu, t.up(S.f_silu))
                            v.tensor_tensor(tmp[2][:], tmp[0][:], tmp[1][:], ALU.mult).then_inc(S.f_mult, 1)
                            dve.wait_ge(S.f_mult, t.up(S.f_mult))
                        else:
                            next_pair()
                            dve.wait_ge(pair_free[(n.q - 1) % 2], (n.q - 1) // 2 + 1)
                            src = next_pair()
                            dve.wait_ge(S.pair_full, n.q)
                            v.tensor_tensor(tmp[2][:], tmp[0][:], src, ALU.mult).then_inc(pair_free[(n.q - 1) % 2], 1)
                            dve.wait_ge(pair_free[(n.q - 1) % 2], (n.q - 1) // 2 + 1)
                        c = 2 * (i - i0)
                        dve.wait_ge(S.f_hi, t.up(S.f_hi))
                        low(fl[third % 2][:, c:c + 2, :], tmp[2][:], fh[third % 2][:, c:c + 2, :], S.f_lo)

            def rope(dst, g=None, single=False):
                yield from wait_steps(3)
                src = next_pair()
                mine = n.q - 1
                dve.wait_ge(S.pair_full, n.q)
                if g is not None:
                    yield
                    next_pair()
                    dve.wait_ge(S.r_root, t.up(S.r_root))
                    newton(tmp[1][:], tmp[0][:])
                    v.scalar_tensor_tensor(tmp[2][:], src, g, tmp[3][:], ALU.mult, ALU.mult).then_inc(pair_free[mine % 2], 1)
                elif not single:
                    v.tensor_copy(tmp[2][:], src).then_inc(pair_free[mine % 2], 1)
                else:
                    v.tensor_copy(tmp[2][0:HD, 0, :], src[0:HD, 0, :])
                    v.tensor_copy(tmp[2][HD:P, 0, :], src[HD:P, 1, :]).then_inc(pair_free[mine % 2], 1)
                dve.wait_ge(pair_free[mine % 2], mine // 2 + 1)
                k = 1 if single else 2
                cos = cosT[:].unsqueeze(1).to_broadcast([P, k, T])
                sin = sinT[:].unsqueeze(1).to_broadcast([P, k, T])
                v.tensor_tensor(tmp[1][:, 0:k, :], tmp[2][:, 0:k, :], cos, ALU.mult)
                yield
                src = next_pair()
                dve.wait_ge(S.pair_full, n.q)
                v.tensor_tensor(tmp[3][:, 0:k, :], src[:, 0:k, :], sin, ALU.mult).then_inc(pair_free[(n.q - 1) % 2], 1)
                dve.wait_ge(pair_free[(n.q - 1) % 2], (n.q - 1) // 2 + 1)
                v.tensor_tensor(dst, tmp[1][:, 0:k, :], tmp[3][:, 0:k, :], ALU.add).then_inc(S.rope_done, 1)
                dve.wait_ge(S.rope_done, t.up(S.rope_done))
                yield

            def select(m):
                kk = (m + 1) * P
                sc = score[:, 0:kk]
                for j in range(2):
                    next_pair()
                    dve.wait_ge(pair_free[(n.q - 1) % 2], (n.q - 1) // 2 + 1)
                    for i in range(2):
                        r, wt = tmp[3][:, i, 0:kk], iw[:, m, 2 * j + i:2 * j + i + 1]
                        signal = S.i_scored if i else S.dve_chain
                        if i + j == 0:
                            v.tensor_scalar(sc, r, wt, None, ALU.mult).then_inc(signal, 1)
                        else:
                            v.scalar_tensor_tensor(sc, r, wt, sc, ALU.mult, ALU.add).then_inc(signal, 1)
                        dve.wait_ge(signal, t.up(signal))
                own = score[:, m * P:kk]
                v.tensor_tensor(own, own, causal, ALU.add).then_inc(S.dve_chain, 1)
                dve.wait_ge(S.dve_chain, t.up(S.dve_chain))
                yield
                for r in range(TOPK // 8):
                    v.max(top8[:], sc).then_inc(S.dve_chain, 1)
                    dve.wait_ge(S.dve_chain, t.up(S.dve_chain))
                    v.match_replace(sc, top8[:], sc, TAKEN).then_inc(S.dve_chain, 1)
                    dve.wait_ge(S.dve_chain, t.up(S.dve_chain))
                    if r == TOPK // 8 - 1:
                        v.tensor_scalar(bias[:, m - 1, 0:kk], sc, TAKEN / 3, NEG, ALU.is_gt, ALU.mult).then_inc(S.dve_chain, 1)
                        dve.wait_ge(S.dve_chain, t.up(S.dve_chain))
                    yield

            def side_core_1():
                w = lambda k, ch: vec[:, V_CONV + 4 * k + ch:V_CONV + 4 * k + ch + 1]
                for j in range(2):
                    yield from wait_steps(3)
                    src = next_pair()
                    dve.wait_ge(S.pair_full, n.q)
                    v.tensor_copy(tmp[0][:], src).then_inc(pair_free[(n.q - 1) % 2], 1)
                    dve.wait_ge(pair_free[(n.q - 1) % 2], (n.q - 1) // 2 + 1)
                    yield
                    yield from wait_steps(3)
                    src = next_pair()
                    dve.wait_ge(S.pair_full, n.q)
                    v.tensor_tensor(tmp[1][:], tmp[0][:], src, ALU.mult).then_inc(pair_free[(n.q - 1) % 2], 1)
                    dve.wait_ge(pair_free[(n.q - 1) % 2], (n.q - 1) // 2 + 1)
                    yield
                    for i in range(2):
                        v.tensor_scalar(tmp[2][:, i, :], tmp[1][:, i, :], w(2, 2 * j + i), None, ALU.mult).then_inc(S.dve_chain, 1)
                        dve.wait_ge(S.dve_chain, t.up(S.dve_chain))
                        taps(tmp[2][:, i, :], tmp[1][:, i, :], w, 2 * j + i).then_inc(S.dve_chain, 1)
                        dve.wait_ge(S.dve_chain, t.up(S.dve_chain))
                    yield from wait_steps(3)
                    src = next_pair()
                    dve.wait_ge(S.pair_full, n.q)
                    v.tensor_tensor(tmp[3][:], tmp[2][:], src, ALU.mult).then_inc(pair_free[(n.q - 1) % 2], 1)
                    dve.wait_ge(pair_free[(n.q - 1) % 2], (n.q - 1) // 2 + 1)
                    yield
                    dve.wait_ge(S.b_hi, t.up(S.b_hi))
                    low(brl[1][:, 2 * j:2 * j + 2, :], tmp[3][:], brh[1][:, 2 * j:2 * j + 2, :],
                        S.branch_ready if j else S.dve_chain)
                yield from passed(4)
                yield from passed(4)
                yield from wait_steps(3)
                src = next_pair()
                dve.wait_ge(S.pair_full, n.q)
                v.tensor_copy(sk[HD:P, 0, :], src[HD:P, 0, :])
                v.tensor_copy(sk[0:HD, 0, :], src[0:HD, 1, :])
                v.tensor_copy(sk[HD:P, 1, :], src[HD:P, 1, :]).then_inc(pair_free[(n.q - 1) % 2], 1)
                yield
                yield
                src = next_pair()
                dve.wait_ge(S.pair_full, n.q)
                v.tensor_copy(sk[0:HD, 1, :], src[0:HD, 0, :]).then_inc(pair_free[(n.q - 1) % 2], 1)
                yield
                yield from passed(4)

            def side_core_2(l):
                for j in range(2):
                    yield from rope(aq[:, 2 * j:2 * j + 2, :], small[:, 9 + l:10 + l])
                for j in range(2):
                    yield from rope(ak[:, 2 * j:2 * j + 2, :], vech[:, V_KN + l:V_KN + l + 1])
                yield from rope(iq[:])
                src = next_pair()
                dve.wait_ge(S.pair_full, n.q)
                v.tensor_scalar(iw[:].rearrange("p m h -> p (m h)"), src[:, 0, 0:4 * NT], 1.0 / 16, None,
                                ALU.mult).then_inc(pair_free[(n.q - 1) % 2], 1)
                yield
                yield from rope(ik[:].unsqueeze(1), single=True)
                yield from passed(4)
                yield from passed(4)

            v.memset(ones[:], 1.0).then_inc(S.dve_chain, 1)
            dve.wait_ge(S.dve_chain, t.up(S.dve_chain))
            v.memset(small[:, 0:1], EPS).then_inc(S.dve_chain, 1)
            dve.wait_ge(S.dve_chain, t.up(S.dve_chain))
            dve.wait_ge(S.consts_in, 16 * N_LOADS)
            v.tensor_copy(summask[:], mrow[:, 0:N_SUM * P]).then_inc(S.dve_chain, 1)
            dve.wait_ge(S.dve_chain, t.up(S.dve_chain))
            v.tensor_copy(pairmask[:].rearrange("p l t -> p (l t)"), mrow[:, N_SUM * P:]).then_inc(S.dve_chain, 1)
            dve.wait_ge(S.dve_chain, t.up(S.dve_chain))
            dve.wait_ge(S.vec_T, t.up(S.vec_T))
            v.tensor_copy(fconv[:].rearrange("p k c -> p (k c)"), X[1][:, 0:6 * FC]).then_inc(S.dve_chain, 1)
            dve.wait_ge(S.dve_chain, t.up(S.dve_chain))
            v.tensor_copy(vec[:], X[0][:, 0:N_VEC]).then_inc(S.vec_ready, 1)
            dve.wait_ge(S.vec_ready, t.up(S.vec_ready))
            v.tensor_scalar(vech[:], vec[:], -0.5, None, ALU.mult).then_inc(S.dve_chain, 1)
            dve.wait_ge(S.dve_chain, t.up(S.dve_chain))
            lb0, lb1 = vec[:, V_LB:V_LB + 4], vec[:, V_LB + 4:V_LB + 8]
            v.tensor_tensor(small[:, 11:15], lb1, lb0, ALU.subtract).then_inc(S.dve_chain, 1)
            dve.wait_ge(S.dve_chain, t.up(S.dve_chain))
            v.tensor_tensor(small[:, 15:19], lb0, lb1, ALU.subtract).then_inc(S.dve_chain, 1)
            dve.wait_ge(S.dve_chain, t.up(S.dve_chain))
            for l in range(LAYERS):
                v.tensor_scalar(small[:, 9 + l:10 + l], vech[:, V_QN + l:V_QN + l + 1], HD ** -0.5, None, ALU.mult).then_inc(S.dve_chain, 1)
                dve.wait_ge(S.dve_chain, t.up(S.dve_chain))
            angle, turns = tmp[3][:, 0, :], tmp[3][:, 1, :]
            v.tensor_copy(tmp[2][:, 0, :], posi[:]).then_inc(S.dve_chain, 1)
            dve.wait_ge(S.dve_chain, t.up(S.dve_chain))
            v.tensor_scalar(angle, tmp[2][:, 0, :], const[:, K_INV:K_INV + 1], None, ALU.mult).then_inc(S.dve_chain, 1)
            dve.wait_ge(S.dve_chain, t.up(S.dve_chain))
            v.tensor_scalar(turns, angle, 1.0 / (2 * np.pi), MAGIC, ALU.mult, ALU.add).then_inc(S.dve_chain, 1)
            dve.wait_ge(S.dve_chain, t.up(S.dve_chain))
            v.tensor_scalar(turns, turns, MAGIC, None, ALU.subtract).then_inc(S.dve_chain, 1)
            dve.wait_ge(S.dve_chain, t.up(S.dve_chain))
            for part in TWO_PI:
                v.scalar_tensor_tensor(angle, turns, -part, angle, ALU.mult, ALU.add).then_inc(S.dve_chain, 1)
                dve.wait_ge(S.dve_chain, t.up(S.dve_chain))
            v.tensor_scalar(angle, angle, PI, -PI, ALU.min, ALU.max).then_inc(S.dve_chain, 1)
            dve.wait_ge(S.dve_chain, t.up(S.dve_chain))
            v.tensor_scalar(turns, angle, float(np.pi / 2), -2 * np.pi, ALU.is_gt, ALU.mult).then_inc(S.dve_chain, 1)
            dve.wait_ge(S.dve_chain, t.up(S.dve_chain))
            v.scalar_tensor_tensor(turns, angle, float(np.pi / 2), turns, ALU.add, ALU.add).then_inc(S.dve_chain, 1)
            dve.wait_ge(S.dve_chain, t.up(S.dve_chain))
            v.tensor_scalar(turns, turns, PI, -PI, ALU.min, ALU.max).then_inc(S.setup_done, 1)
            dve.wait_ge(S.setup_done, t.up(S.setup_done))
            for c in range(DC):
                dve.wait_ge(S.x_T, t.up(S.x_T))
                v.tensor_copy(xT[:, c, :], X[c % 4]).then_inc(S.x_copied, 1)
                dve.wait_ge(S.x_copied, t.up(S.x_copied))

            norm(V_GMIX)
            for j in range(2):
                src = next_pair()
                dve.wait_ge(S.pair_full, n.q)
                v.tensor_copy(gk[:, 2 * j:2 * j + 2, :], src).then_inc(pair_free[(n.q - 1) % 2], 1)
                dve.wait_ge(pair_free[(n.q - 1) % 2], (n.q - 1) // 2 + 1)
            next_pair()
            next_pair()
            src = next_pair()
            dve.wait_ge(S.pair_full, n.q)
            v.tensor_copy(gaT[:], src[0:RANK, 0, :]).then_inc(pair_free[(n.q - 1) % 2], 1)
            dve.wait_ge(pair_free[(n.q - 1) % 2], (n.q - 1) // 2 + 1)
            next_pair()
            next_pair()
            for j in range(2):
                dve.wait_ge(S.soft_done, t.up(S.soft_done))
                for i in range(2):
                    c = 2 * j + i
                    v.tensor_scalar(tmp[2 * j + 1][:, i, :], X[c], vec[:, V_GLAB + c:V_GLAB + c + 1], 0.0,
                                           ALU.add, ALU.min).then_inc(S.dve_chain, 1)
                    dve.wait_ge(S.dve_chain, t.up(S.dve_chain))
                signal = S.lg_ready if j else S.dve_chain
                v.tensor_tensor(lg[:, 2 * j:2 * j + 2, :], tmp[2 * j + 1][:], tmp[2 * j][:], ALU.subtract).then_inc(signal, 1)
                dve.wait_ge(signal, t.up(signal))
            core(1.0 / GLA_TAU, side_core_1(), SIDE_CORE_1)
            side = merge_two()
            core_post(V_GLAN, False, side)
            attention(lambda m: (max(m - 1, 0), m + 1), True, side, SIDE_WINDOW)
            finish(merge(2, late, last=True))
            output()
            norm(V_GFFN)
            ffn(True)
            norm(V_GFIN, split=False)

            dve.wait_ge(S.trig_done, t.up(S.trig_done))
            v.tensor_scalar(small[:, 1:5], small[:, 1:5], 2.0 ** -60, None, ALU.max).then_inc(S.dve_chain, 1)
            dve.wait_ge(S.dve_chain, t.up(S.dve_chain))
            for l in range(LAYERS):
                norm(V_NMIX + DC * l)
                for j in range(2):
                    src = next_pair()
                    dve.wait_ge(S.pair_full, n.q)
                    ta, tb = tmp[2 * j], tmp[2 * j + 1]
                    if l == 0:
                        dve.wait_ge(S.soft_done, t.up(S.soft_done))
                        v.tensor_scalar(tb[:], src, 0.0, None, ALU.min).then_inc(S.dve_chain, 1)
                        dve.wait_ge(S.dve_chain, t.up(S.dve_chain))
                        v.tensor_tensor(lg[:, 2 * j:2 * j + 2, :], tb[:], ta[:], ALU.subtract).then_inc(pair_free[(n.q - 1) % 2], 1)
                        dve.wait_ge(pair_free[(n.q - 1) % 2], (n.q - 1) // 2 + 1)
                    else:
                        dve.wait_ge(S.soft_done, t.up(S.soft_done))
                        for i in range(2):
                            c = 2 * j + i
                            lo, span = small[:, 1 + c:2 + c], small[:, 5 + c:6 + c]
                            signal = S.decay_up if i else S.dve_chain
                            v.tensor_scalar(ta[:, i, :], ta[:, i, :], span, lo, ALU.mult, ALU.add).then_inc(signal, 1)
                            dve.wait_ge(signal, t.up(signal))
                        for i in range(2):
                            c = 2 * j + i
                            span = small[:, 5 + c:6 + c]
                            ins = v.tensor_scalar(gk[:, c, :], tb[:, i, :], span, None, ALU.mult)
                            if i == 0:
                                ins.then_inc(S.dve_chain, 1)
                                dve.wait_ge(S.dve_chain, t.up(S.dve_chain))
                        ins.then_inc(pair_free[(n.q - 1) % 2], 1)
                        dve.wait_ge(pair_free[(n.q - 1) % 2], (n.q - 1) // 2 + 1)
                v.memset(small[:, 31:32], 0.0).then_inc(S.lg_ready, 1)
                dve.wait_ge(S.lg_ready, t.up(S.lg_ready))
                for _ in range(4):
                    next_pair()
                core(1.0, side_core_2(l), SIDE_CORE_2)
                side = merge(0, early, first=True)
                core_post(V_HN + l, True, side)
                attention(lambda m: (0, m + 1), False, side, SIDE_SPARSE)
                finish(merge(2, late, last=True))
                output()
                norm(V_NFFN + DC * l)
                ffn(False)

            for i in range(2 * NT):
                m, half = i // 2, i % 2
                dve.wait_ge(S.y_T, t.up(S.y_T))
                v.tensor_copy(xtok[:, m, MIX * half:MIX * (half + 1)], X[i % 4]).then_inc(S.y_out, 1)
                dve.wait_ge(S.y_out, t.up(S.y_out))


N_LOADS = 20
MAGIC = 1.5 * 2.0 ** 23
TWO_PI = (6.28125, 0.0019350051879882812, 3.0199159819304e-07)
PI = 3.1415925


def shape_constants():
    f = np.float32
    c = np.zeros((P, N_CONST), f)
    i = np.arange(P)
    c[:, K_ID:K_ID + P] = np.eye(P)
    c[:, K_BLK:K_BLK + P] = i[:, None] // HD == i[None, :] // HD
    half = HD // 2
    for o in range(P):
        if o % HD < half:
            c[o + half, K_ROT + o] = -1.0
        else:
            c[o - half, K_ROT + o] = 1.0
    c[:, K_CAUS:K_CAUS + P] = np.where(i[None, :] <= i[:, None], 0.0, NEG)
    d = P + i[:, None] - np.arange(2 * P)[None, :]
    c[:, K_DIST:K_DIST + 2 * P] = np.where((d >= 0) & (d < P), d, FAR)
    c[:, K_INV] = (10000.0 ** (-(2.0 * (i % half)) / HD)).astype(f)
    j, t = i[:, None], i[None, :]
    sums, pairs = [], []
    for l in range(LEVELS):
        w = P >> (l + 1)
        odd = (t // w) % 2 == 1
        start = (t // w) * w
        sums.append(np.where(odd, (j >= start) & (j <= t), (j > t) & (j < start + w)))
        pairs.append(((j // w) % 2 == 0) & (t // w == j // w + 1))
    sums += [j <= t, j > t]
    pairs.append(j == t)
    return c, np.concatenate(sums + pairs, 1).astype(f)


_INS = ['x', 'g_mix', 'w_in', 'gla_w_alpha', 'gla_b_alpha', 'gla_norm_g', 'conv_w', 'swa_sinks', 'w_gla_o',
        'w_conv_o', 'w_swa_o', 'w_o', 'g_ffn', 'w_up', 'ffn_conv_w', 'w_down', 'g_final', 'positions_2', 'w_in_2',
        'w_proj_attn_2', 'w_proj_hgrn_2', 'w_out_2', 'norm_mix_2', 'norm_ffn_2', 'q_norm_2', 'k_norm_2',
        'hgrn_norm_2', 'hgrn_lower_bound_2', 'w_ffn_in_2', 'w_ffn_out_2']


def kernel(**inputs):
    import concourse.bacc as bacc
    from concourse.bass_utils import run_bass_kernel_spmd

    nc = bacc.Bacc("TRN2", target_bir_lowering=False, num_devices=1)
    arrays, aps = {}, {}
    given = {name: np.ascontiguousarray(inputs[name]) for name in _INS}
    given.update(zip(("c_const", "c_masks"), shape_constants()))
    for name, x in given.items():
        arrays[f"in_{name}"] = x
        aps[name] = nc.dram_tensor(f"in_{name}", x.shape, mybir.dt.from_np(x.dtype), kind="ExternalInput").ap()
    out = nc.dram_tensor("out_0", (1, T, D), F32, kind="ExternalOutput").ap()
    build_program(nc, aps, out)
    r = run_bass_kernel_spmd(nc, [arrays], core_ids=[0])
    return r.results[0]["out_0"]
```

```python
from contextlib import ExitStack

import concourse.bass as bass
from concourse import mybir
import numpy as np

F32 = mybir.dt.float32
F32R = mybir.dt.float32r
I32 = mybir.dt.int32
U8 = mybir.dt.uint8
ALU = mybir.AluOpType
ACT = mybir.ActivationFunctionType
AX = mybir.AxisListType.X

P = 128
T = 512
NT = T // P
D = 1024
DC = D // P
EPS = 1e-6
H = 4
MIX = 512
MC = MIX // P
RANK = 16
GLA_TAU = 16.0
D_FF = 2816
FC = D_FF // P
FFN_PAIRS = FC // 2
THIRDS = (4, 4, 3)
AH = 8
HD = 64
LAYERS = 2
TOPK = 128
LEVELS = 7
NEG = -1.0e30
TAKEN = -3.0e38
FAR = 1.0e30

C_GQ, C_GK, C_GV, C_GR, C_GA = 0, 512, 1024, 1536, 2048
C_CX = C_GA + RANK
C_CB, C_CC = C_CX + 512, C_CX + 1024
C_SQ = C_CC + 512
C_SK = C_SQ + 512
C_SV = C_SK + 128
C_GATE = C_SV + 128
C_AQ, C_AK, C_AV, C_IQ, C_IK, C_IW = 0, 512, 1024, 1536, 1792, 1856
C_HQ = C_IW + 4
C_HF, C_HI, C_HG = C_HQ + 512, C_HQ + 1024, C_HQ + 1536
C_G2 = C_HG + 512

V_GMIX, V_GFFN, V_GFIN = 0, 8, 16
V_NMIX, V_NFFN = 24, 40
V_GLAN, V_GLAB = 56, 60
V_CONV = 64
V_HN = 76
V_LB = 78
V_QN, V_KN = 86, 88
N_VEC = 90

K_ID, K_BLK, K_ROT, K_CAUS, K_DIST, K_INV = 0, 128, 256, 384, 512, 768
N_CONST = 769
N_SUM = LEVELS + 2


class Semaphores:
    def __init__(self, sem):
        self.ident_in = sem("ident_in")
        self.consts_in = sem("consts_in")
        self.masks_in = sem("masks_in")
        self.x_in = sem("x_in")
        self.raw_in0 = sem("raw_in0")
        self.raw_in1 = sem("raw_in1")
        self.raw_in2 = sem("raw_in2")
        self.setup_done = sem("setup_done")
        self.trig_done = sem("trig_done")
        self.vec_T = sem("vec_T")
        self.vec_ready = sem("vec_ready")
        self.x_T = sem("x_T")
        self.x_copied = sem("x_copied")
        self.hi_done = sem("hi_done")
        self.lo_done = sem("lo_done")
        self.pair_full = sem("pair_full")
        self.pair_free0 = sem("pair_free0")
        self.pair_free1 = sem("pair_free1")
        self.half_added = sem("half_added")
        self.n_square = sem("n_square")
        self.n_summed = sem("n_summed")
        self.n_root = sem("n_root")
        self.n_normed = sem("n_normed")
        self.n_hi = sem("n_hi")
        self.n_lo = sem("n_lo")
        self.alpha_done = sem("alpha_done")
        self.soft_done = sem("soft_done")
        self.decay_up = sem("decay_up")
        self.ln_done = sem("ln_done")
        self.lg_ready = sem("lg_ready")
        self.lg_T = sem("lg_T")
        self.lt_hi = sem("lt_hi")
        self.lt_lo = sem("lt_lo")
        self.sums_done = sem("sums_done")
        self.dec_done = sem("dec_done")
        self.kd_ready = sem("kd_ready")
        self.kd_T = sem("kd_T")
        self.kdt_done = sem("kdt_done")
        self.lev_ready = sem("lev_ready")
        self.att_done = sem("att_done")
        self.pairs_done = sem("pairs_done")
        self.out_done = sem("out_done")
        self.out_read = sem("out_read")
        self.kv_done = sem("kv_done")
        self.state_done = sem("state_done")
        self.g_square = sem("g_square")
        self.g_summed = sem("g_summed")
        self.g_root = sem("g_root")
        self.g_prod = sem("g_prod")
        self.g_split = sem("g_split")
        self.b_hi = sem("b_hi")
        self.branch_ready = sem("branch_ready")
        self.qk_done = sem("qk_done")
        self.logit_done = sem("logit_done")
        self.negmax = sem("negmax")
        self.prob_done = sem("prob_done")
        self.scaled = sem("scaled")
        self.pt_done = sem("pt_done")
        self.pt_read = sem("pt_read")
        self.pv_done = sem("pv_done")
        self.pv_read = sem("pv_read")
        self.r_root = sem("r_root")
        self.r_normed = sem("r_normed")
        self.rope_done = sem("rope_done")
        self.i_scored = sem("i_scored")
        self.y_added = sem("y_added")
        self.m_hi = sem("m_hi")
        self.m_lo = sem("m_lo")
        self.f_tap = sem("f_tap")
        self.f_silu = sem("f_silu")
        self.f_mult = sem("f_mult")
        self.f_hi = sem("f_hi")
        self.f_lo = sem("f_lo")
        self.y_T = sem("y_T")
        self.y_out = sem("y_out")
        self.out_stored = sem("out_stored")
        self.act_chain = sem("act_chain")
        self.dve_chain = sem("dve_chain")


class Place:
    def __init__(self):
        self.p = self.q = self.hi = self.merged = 0
        self.fresh = 0


def weight_panels(a):
    out = []

    def cols(w, c0, rows=None):
        r0, nk = rows or (0, w.shape[0] // P)
        v = w[r0 * P:(r0 + nk) * P, :].rearrange("(k p) n -> p k n", p=P)
        width = 256 if nk > 4 or rows else 512
        out.append((v[:, :, c0:c0 + width], nk, width))

    def merge(w, gates, wy, between=None):
        for j in range(2):
            cols(w, gates + 512 * j)
            if j == 0 and between:
                cols(w, between)
            cols(w, gates + 512 * j + 256)
            cols(wy, 512 * j)

    def ffn(w_up, w_down):
        for step, third in FFN_STEPS:
            i0 = sum(THIRDS[:third])
            if step == "up":
                for i in range(i0, i0 + THIRDS[third]):
                    cols(w_up, 256 * i)
                    cols(w_up, D_FF + 256 * i)
            else:
                for m in range(DC // 2):
                    cols(w_down, 256 * m, (2 * i0, 2 * THIRDS[third]))

    w = a["w_in"][0]
    for c in (C_GK, C_GK + 256, C_GA, C_GQ, C_GQ + 256, C_GV, C_GV + 256):
        cols(w, c)
    for j in range(2):
        for c in (C_CX, C_CC, C_CB):
            cols(w, c + 256 * j)
    for c in (C_SQ, C_SQ + 256, C_SK - HD, C_SV, C_GR):
        cols(w, c)
    for b, wy, between in ((1, "w_conv_o", C_GR + 256), (0, "w_gla_o", None), (2, "w_swa_o", None)):
        merge(w, C_GATE + b * D, a[wy][0], between)
    for m in range(4):
        cols(a["w_o"][0], 256 * m)
    ffn(a["w_up"][0], a["w_down"][0])
    for l in range(LAYERS):
        w = a["w_in_2"][l]
        for c in (C_HF, C_HQ, C_HF + 256, C_HQ + 256, C_HI, C_HI + 256,
                  C_AQ, C_AQ + 256, C_AK, C_AK + 256, C_IQ, C_IK - HD, C_AV, C_AV + 256, C_HG):
            cols(w, c)
        merge(w, C_G2 + D, a["w_proj_hgrn_2"][l], C_HG + 256)
        merge(w, C_G2, a["w_proj_attn_2"][l])
        for m in range(4):
            cols(a["w_out_2"][l], 256 * m)
        ffn(a["w_ffn_in_2"][l], a["w_ffn_out_2"][l])
    return out


FFN_STEPS = (("up", 0), ("up", 1), ("down", 0), ("up", 2), ("down", 1), ("down", 2))
CORE_UNITS = NT * H // 2
SIDE_CORE_1 = 2 * 3 * 4 + 2 * 4 + 6 + 4
SIDE_CORE_2 = 4 * 6 + 5 + 6 + 2 * 4
MERGE_STEPS = 2 * (4 + 4 + 4)
SIDE_POST_1 = (4, 8)
SIDE_POST_2 = (4, 4)
SIDE_WINDOW = [8, 9, 9, 10]
SIDE_SPARSE = [4] * NT
SELECT_EARLY = 14
SELECT_LATE = ((NT - 1) * TOPK // 8 - 2 * SELECT_EARLY, (NT - 1) * AH)
assert sum(SIDE_POST_1) + sum(SIDE_WINDOW) == 2 * MERGE_STEPS and sum(SIDE_POST_2) + sum(SIDE_SPARSE) == MERGE_STEPS
SLOPES = [2.0 ** -(h + 1) for h in range(AH)]


def core_steps(total, unit, slot):
    return (1, 2, share(total - 5 * CORE_UNITS, CORE_UNITS, unit), 1, 1)[slot]


def share(total, parts, i):
    return total * (i + 1) // parts - total * i // parts


def build_program(nc, a, out):
    panels = weight_panels(a)
    n_panels = len(panels)
    ctx = ExitStack()
    with ctx:
        def sb(name, shape, dt=F32):
            return ctx.enter_context(nc.sbuf_tensor(name, shape, dt))

        xT = sb("xT", [P, DC, T])
        uh = sb("uh", [P, DC, T], F32R)
        ul = sb("ul", [P, DC, T], F32R)
        ring = (nc.sbuf_base + 31) // 32 * 32
        raw = [sb(f"raw{i}", [P, 2048]) for i in range(3)]
        wh = [sb(f"wh{i}", [P, 2048], F32R) for i in range(3)]
        tmp = [sb(f"tmp{i}", [P, 2, T]) for i in range(4)]
        const = sb("const", [P, N_CONST])
        summask = sb("summask", [P, N_SUM * P], F32R)
        pairmask = sb("pairmask", [P, LEVELS + 1, P], U8)
        ones = sb("ones", [P, P])
        vec = sb("vec", [P, N_VEC])
        vech = sb("vech", [P, N_VEC])
        top8 = sb("top8", [P, 8])
        stat = sb("stat", [P, 16])
        fconv = sb("fconv", [P, 3, 2 * FC])
        small = sb("small", [P, 64])
        cosT = sb("cosT", [P, T])
        sinT = sb("sinT", [P, T])
        walpha = sb("walpha", [RANK, MIX])
        sinks = sb("sinks", [P, AH])
        iw = sb("iw", [P, NT, 4])
        ident, blk, rot = const[:, K_ID:K_ID + P], const[:, K_BLK:K_BLK + P], const[:, K_ROT:K_ROT + P]
        causal = const[:, K_CAUS:K_CAUS + P]
        dist = const[:, K_DIST:K_DIST + 2 * P]
        psum = ctx.enter_context(nc.psum_tensor("psum", [P, 8, T], F32))
        pair = [psum[:, 0:2, :], psum[:, 2:4, :]]
        X = [psum[:, 4 + b, :] for b in range(4)]
        X4 = psum[:, 4:8, :]

        arena = (nc.sbuf_base + 31) // 32 * 32

        def at(name, kib, shape, dt=F32):
            return nc.alloc_sbuf_tensor_at(name, shape, dt, offset=arena + int(kib * 1024))

        wl = [nc.alloc_sbuf_tensor_at(f"wl{i}", [P, 2048], F32R, offset=ring + 8192 * i) for i in range(3)]
        brh = [at(f"brh{b}", k, [P, MC, T], F32R) for b, k in enumerate((0, 63, 16))]
        brl = [at(f"brl{b}", k + 8, [P, MC, T], F32R) for b, k in enumerate((0, 63, 16))]
        gk = at("gk", 0, [P, H, T])
        lg = at("lg", 8, [P, H, T])
        gq = at("gq", 16, [P, H, T])
        gv = at("gv", 24, [P, NT, MIX])
        dec = at("dec", 32, [P, 2, N_SUM, P])
        lth = at("lth", 41, [P, 2, 2, P], F32R)
        ltl = at("ltl", 43, [P, 2, 2, P], F32R)
        attT = at("attT", 45, [P, 2, P])
        kdt = at("kdt", 46, [P, 2, P])
        state = at("state", 47, [P, H, P])
        gaT = at("gaT", 63, [RANK, T])
        sq = at("sq", 49, [P, MC, T])
        sk = at("sk", 57, [P, 2, T])
        sv = at("sv", 61, [P, NT, P])
        aq = at("aq", 49, [P, MC, T])
        ak = at("ak", 57, [P, MC, T])
        av = at("av", 65, [P, NT, MIX])
        iq = at("iq", 73, [P, 2, T])
        ik = at("ik", 77, [P, T])
        qk_pair = [aq[:, 0:2, :], aq[:, 2:4, :], ak[:, 0:2, :], ak[:, 2:4, :]]
        score1 = at("score1", 46, [P, 2 * P])
        score2 = at("score2", 40, [P, 3 * P])
        score3 = at("score3", 16, [P, 4 * P])
        scores = [score1[:], score2[:], score3[:]]
        hidden = at("hidden", 48, [P, P])
        bias1 = at("bias1", 44, [P, 2 * P])
        bias2 = at("bias2", 42, [P, 3 * P])
        bias3 = at("bias3", 20, [P, 4 * P])
        logit = [tmp[0][:, i, :] for i in range(2)]
        prob = [tmp[1][:, i, :] for i in range(2)]
        probT = [tmp[2][:, i, :] for i in range(2)]
        merged = at("merged", 32, [P, DC, T])
        early = [at(f"early{i}", 24 + 4 * i, [P, 2, T]) for i in range(2)]
        late = [tmp[0], tmp[1]]
        fh = [at(f"fh{i}", 32 * i, [P, 8, T], F32R) for i in range(2)]
        fl = [at(f"fl{i}", 32 * i + 16, [P, 8, T], F32R) for i in range(2)]
        xtok = at("xtok", 32, [P, NT, D])
        vrow = at("vrow", 48, [N_VEC, P])
        crow = at("crow", 49, [2 * FC, 3, P])
        mrow = at("mrow", 51, [P, (N_SUM + LEVELS + 1) * P])
        posi = at("posi", 60, [P, T], I32)
        assert arena + 79 * 1024 <= nc.sbuf_usable_end, (arena, nc.sbuf_usable_end)

        S = Semaphores(lambda name: ctx.enter_context(nc.semaphore(name)))
        raw_in = [S.raw_in0, S.raw_in1, S.raw_in2]
        pair_free = [S.pair_free0, S.pair_free1]
        panel_end = [0] * n_panels
        block = ctx.enter_context(nc.Block())

        class Turns:
            def __init__(self):
                self.at = {}

            def up(self, sem, by=1):
                self.at[sem.name] = self.at.get(sem.name, 0) + by
                return self.at[sem.name]

        def take_on(side, steps):
            for _ in range(steps):
                next(side)

        def finish(side):
            for _ in side:
                pass

        def wview(t, p):
            nk, width = panels[p][1:3]
            return t[p % 3][:, 0:nk * width].rearrange("p (k n) -> p k n", k=nk)

        @block.tensor
        def _(pe):
            t = Turns()
            n = Place()
            mm = nc.tensor.matmul

            def panel():
                pe.wait_ge(S.lo_done, n.p + 1)
                n.p += 1
                return wview(wh, n.p - 1), wview(wl, n.p - 1)

            def new_pair():
                if n.q >= 2:
                    pe.wait_ge(pair_free[n.q % 2], n.q // 2)
                n.q += 1
                return pair[(n.q - 1) % 2]

            def products(dst, terms, first, last):
                todo = [xy for h, l, r, q in terms for xy in ((h, r), (h, q), (l, r))]
                for i, (x, y) in enumerate(todo):
                    ins = mm(dst, x, y, start=first and i == 0, stop=last and i == len(todo) - 1)
                return ins

            def project(xh, xl, offsets=(0, P), w=None):
                h, l = w or panel()
                dst = new_pair()
                nk = h.shape[1]
                if n.fresh:
                    for k in range(nk):
                        if n.fresh == 1 or k % 2 == 0:
                            sem = S.n_lo if n.fresh == 1 else S.m_lo
                            pe.wait_ge(sem, t.up(sem))
                        for i, off in enumerate(offsets):
                            ins = products(dst[:, i, :], [(h[:, k, off:off + P], l[:, k, off:off + P], xh[:, k, :], xl[:, k, :])],
                                           k == 0, k == nk - 1)
                    ins.then_inc(S.pair_full, 1)
                    panel_end[n.p - 1] = n.q
                    n.fresh = 0
                    yield
                    return h, l
                for i, off in enumerate(offsets):
                    for k0 in range(0, nk, 4):
                        ks = range(k0, min(k0 + 4, nk))
                        ins = products(dst[:, i, :], [(h[:, k, off:off + P], l[:, k, off:off + P], xh[:, k, :], xl[:, k, :])
                                                      for k in ks], k0 == 0, k0 + 4 >= nk)
                        if i == len(offsets) - 1 and k0 + 4 >= nk:
                            ins.then_inc(S.pair_full, 1)
                            panel_end[n.p - 1] = n.q
                        yield
                return h, l

            def project_tokens(width=256):
                h, l = panel()
                dst = new_pair()
                for m in range(NT):
                    tok = slice(m * P, (m + 1) * P)
                    ins = products(dst[:, m // 2, 256 * (m % 2):256 * (m % 2) + width],
                                   [(uh[:, k, tok], ul[:, k, tok], h[:, k, 0:width], l[:, k, 0:width]) for k in range(DC)],
                                   True, True)
                    if m == NT - 1:
                        ins.then_inc(S.pair_full, 1)
                        panel_end[n.p - 1] = n.q
                    yield

            def sum_squares(s):
                for i in range(2):
                    if i == 0 or s == DC // 2 - 1:
                        pe.wait_ge(S.n_square, t.up(S.n_square))
                    ins = mm(X[0], ones[:], tmp[s % 2][:, i, :], start=(s + i == 0), stop=(s + i == DC // 2))
                ins.then_inc(S.n_summed, 1)

            def residual(xh, xl, squares=True):
                for s in range(DC // 2):
                    finish(project(xh, xl))
                    if squares and s > 0:
                        sum_squares(s - 1)
                if squares:
                    sum_squares(DC // 2 - 1)
                    n.fresh = 1

            def core(side, total, logs=0):
                def turn_logs(u):
                    m, hp = u // 2, u % 2
                    for i in range(2):
                        ins = nc.tensor.transpose(X[0][:, i * P:(i + 1) * P], lg[:, 2 * hp + i, m * P:(m + 1) * P], ident)
                    ins.then_inc(S.lg_T, 1)

                pe.wait_ge(S.lg_ready, t.up(S.lg_ready))
                pe.wait_ge(pair_free[(n.q - 1) % 2], (n.q - 1) // 2 + 1)
                if logs:
                    pe.wait_ge(S.ln_done, t.up(S.ln_done, logs))
                turn_logs(0)
                for u in range(CORE_UNITS):
                    m, hp = u // 2, u % 2
                    tok = slice(m * P, (m + 1) * P)
                    pe.wait_ge(S.lt_lo, t.up(S.lt_lo))
                    if u > 0:
                        pe.wait_ge(S.state_done, t.up(S.state_done))
                    for i in range(2):
                        if i > 0:
                            take_on(side, core_steps(total, u, 0))
                            pe.wait_ge(S.dec_done, t.up(S.dec_done))
                        for b in range(3):
                            cols = slice(3 * P * b, 3 * P * (b + 1))
                            mm(X[1 + b][:, 0:3 * P], lth[:, u % 2, i, :], summask[:, cols], start=True, stop=False)
                            ins = mm(X[1 + b][:, 0:3 * P], ltl[:, u % 2, i, :], summask[:, cols], start=False, stop=True)
                        ins.then_inc(S.sums_done, 1)
                    if u + 1 < CORE_UNITS:
                        if u > 0:
                            pe.wait_ge(S.out_read, t.up(S.out_read))
                        turn_logs(u + 1)
                    take_on(side, core_steps(total, u, 1))
                    pe.wait_ge(S.dec_done, t.up(S.dec_done))
                    pe.wait_ge(S.kd_ready, t.up(S.kd_ready))
                    if u + 1 == CORE_UNITS:
                        pe.wait_ge(S.out_read, t.up(S.out_read))
                    for i in range(2):
                        ins = nc.tensor.transpose(X[0][:, i * P:(i + 1) * P], dec[:, i, LEVELS + 1, :], ident)
                    ins.then_inc(S.kd_T, 1)
                    for l in range(LEVELS + 1):
                        if l < LEVELS:
                            pe.wait_ge(S.lev_ready, t.up(S.lev_ready))
                        if l == 6:
                            take_on(side, core_steps(total, u, 2))
                            pe.wait_ge(S.pairs_done, t.up(S.pairs_done))
                        for i in range(2):
                            h, c = 2 * hp + i, 2 * P * (l % 2) + i * P
                            lhs, rhs = (dec[:, i, l, :], dec[:, i, l, :]) if l < LEVELS else (gk[:, h, tok], gq[:, h, tok])
                            ins = mm(X[1 + l // 2 % 3][:, c:c + P], lhs, rhs, start=True, stop=True)
                        if l % 2 == 1:
                            ins.then_inc(S.att_done, 1)
                    take_on(side, core_steps(total, u, 3))
                    pe.wait_ge(S.pairs_done, t.up(S.pairs_done, 3))
                    pe.wait_ge(S.kdt_done, t.up(S.kdt_done))
                    for i in range(2):
                        h = 2 * hp + i
                        ins = mm(X[0][:, i * P:(i + 1) * P], gv[:, m, h * P:(h + 1) * P], attT[:, i, :], start=True, stop=(m == 0))
                        if m > 0:
                            ins = mm(X[0][:, i * P:(i + 1) * P], state[:, h, :], dec[:, i, LEVELS, :], start=False, stop=True)
                    ins.then_inc(S.out_done, 1)
                    for i in range(2):
                        h = 2 * hp + i
                        ins = mm(X[1][:, i * P:(i + 1) * P], kdt[:, i, :], gv[:, m, h * P:(h + 1) * P], start=True, stop=True)
                    ins.then_inc(S.kv_done, 1)
                    take_on(side, core_steps(total, u, 4))
                pe.wait_ge(S.out_read, t.up(S.out_read))
                pe.wait_ge(S.state_done, t.up(S.state_done))
                finish(side)

            def core_post(side, side_steps):
                for j in range(2):
                    finish(project(uh, ul))
                    pe.wait_ge(S.g_square, t.up(S.g_square))
                    for i in range(2):
                        ins = mm(X[i], ones[:], tmp[1][:, i, :], start=True, stop=True)
                    ins.then_inc(S.g_summed, 1)
                    take_on(side, side_steps[j])
                pe.wait_ge(S.g_root, t.up(S.g_root, 2))

            def attention(q, kof, vof, blocks, side, side_steps, indexed=False):
                steps = [(m, h) for m in range(NT) for h in range(AH)]

                def qk(i):
                    m, h = steps[i]
                    half = slice(HD * (h % 2), HD * (h % 2 + 1))
                    if i >= 2:
                        pe.wait_ge(S.logit_done, t.up(S.logit_done))
                    b0, b1 = blocks(m)
                    mm(X[i % 2][:, 0:(b1 - b0) * P], q[half, h // 2, m * P:(m + 1) * P], kof(h)[:, b0 * P:b1 * P],
                       start=True, stop=True).then_inc(S.qk_done, 1)

                def pv(i):
                    m, h = steps[i]
                    b0, b1 = blocks(m)
                    if h % 2 == 0 and i >= 2:
                        pe.wait_ge(S.pv_read, t.up(S.pv_read))
                    for b in range(b0, b1):
                        ins = mm(X[3][HD * (h % 2):HD * (h % 2 + 1), 0:P], vof(h, b), probT[i % 2][:, (b - b0) * P:(b - b0 + 1) * P],
                                 start=(b == b0), stop=(b == b1 - 1))
                    ins.then_inc(S.pv_done, 1)

                qk(0)
                for i, (m, h) in enumerate(steps):
                    if indexed and i == 0:
                        index(NT - 1)
                    if i + 1 < len(steps):
                        qk(i + 1)
                    take_on(side, share(side_steps[m], AH, h))
                    if i > 0:
                        pe.wait_ge(S.pt_read, t.up(S.pt_read))
                    pe.wait_ge(S.scaled, t.up(S.scaled))
                    b0, b1 = blocks(m)
                    for b in range(b1 - b0):
                        ins = nc.tensor.transpose(X[2][:, b * P:(b + 1) * P], prob[i % 2][:, b * P:(b + 1) * P], ident)
                    ins.then_inc(S.pt_done, 1)
                    if i > 0:
                        pv(i - 1)
                pe.wait_ge(S.pt_read, t.up(S.pt_read))
                pv(len(steps) - 1)
                pe.wait_ge(S.pv_read, t.up(S.pv_read))
                pe.wait_ge(S.logit_done, t.up(S.logit_done, 2))
                finish(side)

            def index(m):
                for j in range(2):
                    dst = new_pair()
                    for i in range(2):
                        half = slice(HD * i, HD * (i + 1))
                        ins = mm(dst[:, i, 0:(m + 1) * P], iq[half, j, m * P:(m + 1) * P], ik[half, 0:(m + 1) * P],
                                 start=True, stop=True)
                    ins.then_inc(S.pair_full, 1)

            def merge(b):
                for j in range(2):
                    yield from project(uh, ul)
                    yield from project(uh, ul)
                    w = panel()
                    if j == 0:
                        pe.wait_ge(S.branch_ready, t.up(S.branch_ready))
                    for off in (0, 256):
                        yield from project(brh[b], brl[b], (off, off + P), w)

            def merge_two():
                yield from merge(1)
                yield from merge(0)

            def output():
                n.fresh = 2
                residual(uh, ul)

            def ffn(squares=True):
                for step, third in FFN_STEPS:
                    if step == "up":
                        for _ in range(2 * THIRDS[third]):
                            finish(project(uh, ul))
                    else:
                        pe.wait_ge(S.f_lo, t.up(S.f_lo, THIRDS[third]))
                        residual(fh[third % 2], fl[third % 2], squares and third == 2)

            def side_core_1():
                for _ in range(8):
                    yield from project(uh, ul)
                w = yield from project(uh, ul, (0, HD))
                yield from project(uh, ul, (P,), w)
                yield from project_tokens(P)

            def turn(src, ready=None):
                dst = new_pair()
                if ready is None:
                    pe.wait_ge(S.r_normed, t.up(S.r_normed))
                else:
                    pe.wait_ge(pair_free[ready % 2], ready // 2 + 1)
                for i in range(src.shape[1]):
                    ins = mm(dst[:, i, :], rot, src[:, i, :], start=True, stop=True)
                ins.then_inc(S.pair_full, 1)

            def side_core_2():
                for j in range(4):
                    yield from project(uh, ul)
                    mine = n.q - 1
                    if j > 0:
                        turn(qk_pair[j - 1])
                        yield
                    dst = new_pair()
                    pe.wait_ge(pair_free[mine % 2], mine // 2 + 1)
                    for i in range(2):
                        ins = mm(dst[:, i, :], blk, tmp[0][:, i, :], start=True, stop=True)
                    ins.then_inc(S.pair_full, 1)
                    yield
                yield from project(uh, ul)
                mine = n.q - 1
                turn(qk_pair[3])
                yield
                h, l = panel()
                dst = new_pair()
                for m in range(NT):
                    tok = slice(m * P, (m + 1) * P)
                    ins = products(dst[:, 0, 4 * m:4 * m + 4],
                                   [(uh[:, c, tok], ul[:, c, tok], h[:, c, P:P + 4], l[:, c, P:P + 4]) for c in range(DC)],
                                   True, True)
                ins.then_inc(S.pair_full, 1)
                yield
                turn(iq, mine)
                yield
                yield from project(uh, ul, (HD, 0), (h, l))
                mine = n.q - 1
                yield from project_tokens()
                turn(ik[:].unsqueeze(1), mine)
                yield
                yield from project_tokens()

            pe.wait_ge(S.ident_in, 16)
            pe.wait_ge(S.x_in, 16)
            for c in range(DC):
                if c >= 4:
                    pe.wait_ge(S.x_copied, t.up(S.x_copied))
                for m in range(NT):
                    ins = nc.tensor.transpose(X[c % 4][:, m * P:(m + 1) * P], xtok[:, m, c * P:(c + 1) * P], ident)
                ins.then_inc(S.x_T, 1)
            pe.wait_ge(S.x_copied, t.up(S.x_copied, 4))
            for s in range(DC // 2):
                sum_squares(s)
            pe.wait_ge(S.consts_in, 16 * N_LOADS)
            nc.tensor.transpose(pair[0][:, 0, 0:N_VEC], vrow[:], ident[0:N_VEC, 0:N_VEC])
            for k in range(3):
                ins = nc.tensor.transpose(pair[0][:, 1, k * 2 * FC:(k + 1) * 2 * FC], crow[:, k, :], ident[0:2 * FC, 0:2 * FC])
            ins.then_inc(S.vec_T, 1)
            pe.wait_ge(S.vec_ready, 1)
            n.fresh = 1

            finish(project(uh, ul))
            finish(project(uh, ul))
            finish(project(uh, ul, (0,)))
            finish(project(uh, ul))
            pe.wait_ge(pair_free[(n.q - 2) % 2], (n.q - 2) // 2 + 1)
            for c in range(MC):
                ins = mm(X[c], walpha[:, c * P:(c + 1) * P], gaT[:], start=True, stop=True)
            ins.then_inc(S.alpha_done, 1)
            finish(project(uh, ul))
            finish(project_tokens())
            finish(project_tokens())
            core(side_core_1(), SIDE_CORE_1)
            side = merge_two()
            core_post(side, SIDE_POST_1)
            attention(sq, lambda h: sk[HD * (h % 2):HD * (h % 2 + 1), h // 4, :],
                      lambda h, b: sv[:, b, HD * (h // 4):HD * (h // 4 + 1)], lambda m: (max(m - 1, 0), m + 1),
                      side, SIDE_WINDOW)
            finish(merge(2))
            output()
            ffn()
            n.fresh = 0
            for s in range(DC // 2):
                sum_squares(s)
            n.fresh = 1

            for l in range(LAYERS):
                for _ in range(4):
                    finish(project(uh, ul))
                finish(project_tokens())
                finish(project_tokens())
                core(side_core_2(), SIDE_CORE_2, 2 * l)
                side = merge(0)
                index(1)
                index(2)
                core_post(side, SIDE_POST_2)
                attention(aq, lambda h: ak[HD * (h % 2):HD * (h % 2 + 1), h // 2, :],
                          lambda h, b: av[:, b, HD * h:HD * (h + 1)], lambda m: (0, m + 1),
                          side, SIDE_SPARSE, True)
                finish(merge(2))
                output()
                ffn(l + 1 < LAYERS)

            pe.wait_ge(pair_free[(n.q - 1) % 2], (n.q - 1) // 2 + 1)
            for i in range(2 * NT):
                m, half = i // 2, i % 2
                if i >= 4:
                    pe.wait_ge(S.y_out, t.up(S.y_out))
                for c in range(4):
                    ins = nc.tensor.transpose(X[i % 4][:, c * P:(c + 1) * P], xT[:, 4 * half + c, m * P:(m + 1) * P], ident)
                ins.then_inc(S.y_T, 1)

        @block.sync
        def _(sp):
            sp.dma_start(const[:], a["c_const"]).then_inc(S.ident_in, 16)
            sp.dma_start(xtok[:], a["x"][0].rearrange("(n p) d -> p n d", p=P)).then_inc(S.x_in, 16)
            loads = [(crow[:], a["ffn_conv_w"][0].rearrange("k (c p) -> c k p", p=P)),
                     (walpha[:], a["gla_w_alpha"][0]),
                     (sinks[:], a["swa_sinks"].partition_broadcast(P))]

            def rows(r, src):
                src = src.rearrange("a (c p) -> (a c) p", p=P)
                loads.append((vrow[r:r + src.shape[0], :], src))

            rows(V_GMIX, a["g_mix"])
            rows(V_GFFN, a["g_ffn"])
            loads.append((vrow[V_GFIN:V_GFIN + DC, :], a["g_final"].rearrange("(c p) -> c p", p=P)))
            rows(V_NMIX, a["norm_mix_2"])
            rows(V_NFFN, a["norm_ffn_2"])
            rows(V_GLAN, a["gla_norm_g"])
            rows(V_GLAB, a["gla_b_alpha"])
            rows(V_CONV, a["conv_w"][0])
            rows(V_HN, a["hgrn_norm_2"])
            rows(V_LB, a["hgrn_lower_bound_2"])
            for r, src in ((V_QN, a["q_norm_2"]), (V_KN, a["k_norm_2"])):
                for half in range(2):
                    loads.append((vrow[r:r + LAYERS, HD * half:HD * (half + 1)], src))
            assert len(loads) == N_LOADS
            for dst, src in loads:
                sp.dma_start(dst, src).then_inc(S.consts_in, 16)
            for p, (src, nk, width) in enumerate(panels):
                if p >= 3:
                    sp.wait_ge(S.pair_full, panel_end[p - 3])
                sp.dma_start(wview(raw, p), src).then_inc(raw_in[p % 3], 16)
                if p == 2:
                    sp.dma_start(mrow[:], a["c_masks"]).then_inc(S.masks_in, 16)
                    sp.dma_start(posi[:], a["positions_2"].partition_broadcast(P)).then_inc(S.masks_in, 16)
            for n in range(NT):
                sp.wait_ge(S.y_out, 2 * n + 2)
                sp.dma_start(out[0, n * P:(n + 1) * P, :], xtok[:, n, :]).then_inc(S.out_stored, 16)
            sp.wait_ge(S.out_stored, 16 * NT)

        @block.gpsimd
        def _(pool):
            for p in range(n_panels):
                nk, width = panels[p][1:3]
                w = slice(0, nk * width)
                pool.wait_ge(S.hi_done, p + 1)
                nc.gpsimd.tensor_tensor(wl[p % 3][:, w], raw[p % 3][:, w], wh[p % 3][:, w].bitcast(F32),
                                        ALU.subtract).then_inc(S.lo_done, 1)

        @block.scalar
        def _(act):
            t = Turns()
            n = Place()
            fn = nc.scalar.activation

            def ahead(end=n_panels):
                while n.hi < end and (n.hi < 3 or panel_end[n.hi - 3] < n.q):
                    p = n.hi
                    nk, width = panels[p][1:3]
                    act.wait_ge(raw_in[p % 3], 16 * (p // 3 + 1))
                    nc.scalar.copy(wh[p % 3][:, 0:nk * width], raw[p % 3][:, 0:nk * width]).then_inc(S.hi_done, 1)
                    n.hi += 1

            def next_pair():
                n.q += 1
                return pair[(n.q - 1) % 2]

            def evict(dst, tokens=None, **kw):
                yield from wait_steps(3)
                src = next_pair()
                if tokens:
                    src = src.rearrange("p b (x c) -> p b x c", x=2)[:, :, :, 0:tokens]
                    dst = dst.rearrange("p (b x) c -> p b x c", b=2)
                act.wait_ge(S.pair_full, n.q)
                fn(dst, src, ACT.Copy, **kw).then_inc(pair_free[(n.q - 1) % 2], 1)
                ahead()
                yield

            def wait_steps(k):
                for _ in range(k):
                    yield

            def passed(steps):
                yield from wait_steps(steps - 1)
                next_pair()
                ahead()
                yield

            def squares(of):
                for s in range(DC // 2):
                    last = s == DC // 2 - 1
                    if of == "residual":
                        next_pair()
                        ahead()
                        if last:
                            act.wait_ge(S.half_added, t.up(S.half_added))
                        else:
                            act.wait_ge(pair_free[(n.q - 1) % 2], (n.q - 1) // 2 + 1)
                    elif of == "input":
                        if s == 2:
                            ahead(1)
                        act.wait_ge(S.x_copied, t.up(S.x_copied, 2))
                    else:
                        act.wait_ge(S.n_normed, t.up(S.n_normed, 2))
                    if s >= 2:
                        act.wait_ge(S.n_summed, t.up(S.n_summed))
                    if last:
                        fn(tmp[s % 2][:, 0, :], xT[:, 2 * s, :], ACT.Square).then_inc(S.n_square, 1)
                        if of == "residual":
                            act.wait_ge(pair_free[(n.q - 1) % 2], (n.q - 1) // 2 + 1)
                        fn(tmp[s % 2][:, 1, :], xT[:, 2 * s + 1, :], ACT.Square).then_inc(S.n_square, 1)
                    else:
                        fn(tmp[s % 2][:], xT[:, 2 * s:2 * s + 2, :], ACT.Square).then_inc(S.n_square, 1)

            def norm(split=True):
                act.wait_ge(S.n_summed, t.up(S.n_summed, 2))
                fn(tmp[2][:, 0, :], X[0], ACT.Sqrt, bias=small[:, 0:1], scale=1.0 / D).then_inc(S.n_root, 1)
                if split:
                    for c in range(DC):
                        act.wait_ge(S.n_normed, t.up(S.n_normed))
                        nc.scalar.copy(uh[:, c, :], tmp[3][:, c % 2, :]).then_inc(S.n_hi, 1)

            def soft(src, dst, b=None):
                if b is None:
                    fn(dst, src, ACT.Abs).then_inc(S.act_chain, 1)
                else:
                    fn(dst[:, 0, :], src[:, 0, :], ACT.Abs, bias=b[:, 0:1])
                    fn(dst[:, 1, :], src[:, 1, :], ACT.Abs, bias=b[:, 1:2]).then_inc(S.act_chain, 1)
                act.wait_ge(S.act_chain, t.up(S.act_chain))
                fn(dst, dst, ACT.Exp, scale=-1.0).then_inc(S.act_chain, 1)
                act.wait_ge(S.act_chain, t.up(S.act_chain))
                return fn(dst, dst, ACT.Ln, bias=1.0)

            def core(scale, side, total):
                def copy_logs(u):
                    act.wait_ge(S.lg_T, t.up(S.lg_T))
                    fn(lth[:, u % 2, :, :], X[0][:, 0:2 * P].rearrange("p (h f) -> p h f", h=2), ACT.Copy,
                       scale=scale).then_inc(S.lt_hi, 1)

                copy_logs(0)
                for u in range(CORE_UNITS):
                    for i in range(2):
                        if i > 0:
                            take_on(side, core_steps(total, u, 0))
                        act.wait_ge(S.sums_done, t.up(S.sums_done))
                        fn(dec[:, i, :, :].rearrange("p (b l) t -> p b (l t)", b=3), X4[:, 1:4, 0:3 * P],
                           ACT.Exp).then_inc(S.dec_done, 1)
                    if u + 1 < CORE_UNITS:
                        copy_logs(u + 1)
                    take_on(side, core_steps(total, u, 1))
                    act.wait_ge(S.kd_T, t.up(S.kd_T))
                    nc.scalar.copy(kdt[:], X[0][:, 0:2 * P].rearrange("p (h f) -> p h f", h=2)).then_inc(S.kdt_done, 1)
                    for slot in (2, 3, 4):
                        take_on(side, core_steps(total, u, slot))
                finish(side)

            def mean_square(x, src, scale, signal):
                fn(x, src, ACT.Identity, bias=small[:, 0:1], scale=scale).then_inc(signal, 1)

            def logarithm(y, x):
                fn(y, x, ACT.Ln).then_inc(S.act_chain, 1)
                act.wait_ge(S.act_chain, t.up(S.act_chain))

            def inverse_root(y):
                fn(y, y, ACT.Exp, scale=-0.5).then_inc(S.act_chain, 1)
                act.wait_ge(S.act_chain, t.up(S.act_chain))
                return fn(tmp[3][:], y, ACT.Square)

            def core_post(side, side_steps):
                act.wait_ge(S.out_read, t.up(S.out_read, CORE_UNITS))
                for j in range(2):
                    heads = slice(2 * j, 2 * j + 2)
                    fn(tmp[1][:], gq[:, heads, :], ACT.Square).then_inc(S.g_square, 1)
                    src = next_pair()
                    act.wait_ge(S.pair_full, n.q)
                    fn(tmp[0][:], src, ACT.Silu).then_inc(pair_free[(n.q - 1) % 2], 1)
                    ahead()
                    act.wait_ge(S.g_summed, t.up(S.g_summed))
                    if j:
                        act.wait_ge(S.g_split, t.up(S.g_split))
                    mean_square(tmp[1][:], X4[:, 0:2, :], 1.0 / P, S.act_chain)
                    act.wait_ge(S.act_chain, t.up(S.act_chain))
                    logarithm(tmp[2][:], tmp[1][:])
                    inverse_root(tmp[2][:]).then_inc(S.g_root, 1)
                    act.wait_ge(S.g_prod, t.up(S.g_prod))
                    nc.scalar.copy(brh[0][:, heads, :], tmp[3][:]).then_inc(S.b_hi, 1)
                    take_on(side, side_steps[j])

            def indexed(m):
                for j in range(2):
                    kk = (m + 1) * P
                    src = next_pair()
                    act.wait_ge(S.pair_full, n.q)
                    if j > 0:
                        act.wait_ge(S.i_scored, t.up(S.i_scored))
                    fn(tmp[3][:, :, 0:kk], src[:, :, 0:kk], ACT.Relu).then_inc(pair_free[(n.q - 1) % 2], 1)
                act.wait_ge(S.i_scored, t.up(S.i_scored))

            def attention(blocks, sink, side, side_steps):
                steps = [(m, h) for m in range(NT) for h in range(AH)]

                def exps(i):
                    m, h = steps[i]
                    kk = (blocks(m)[1] - blocks(m)[0]) * P
                    st = stat[:, 8 * (i % 2):8 * (i % 2) + 8]
                    act.wait_ge(S.logit_done, t.up(S.logit_done))
                    if sink:
                        act.wait_ge(S.negmax, t.up(S.negmax))
                    if sink:
                        fn(st[:, 3:4], sinks[:, h:h + 1], ACT.Exp, bias=st[:, 1:2])
                    fn(prob[i % 2][:, 0:kk], logit[i % 2][:, 0:kk], ACT.Exp, bias=st[:, 1:2], scale=1.0 if sink else -1.0,
                       accum_out=st[:, 2:3]).then_inc(S.prob_done, 1)

                exps(0)
                for i, (m, h) in enumerate(steps):
                    if not sink and i == 0:
                        indexed(NT - 1)
                    if i + 1 < len(steps):
                        exps(i + 1)
                    take_on(side, share(side_steps[m], AH, h))
                    kk = (blocks(m)[1] - blocks(m)[0]) * P
                    act.wait_ge(S.pt_done, t.up(S.pt_done))
                    nc.scalar.copy(probT[i % 2][:, 0:kk], X[2][:, 0:kk]).then_inc(S.pt_read, 1)
                act.wait_ge(S.pv_read, t.up(S.pv_read, len(steps) // 2))
                src = sq if sink else aq
                finish(side)
                for j in range(2):
                    nc.scalar.copy(brh[2][:, 2 * j:2 * j + 2, :], src[:, 2 * j:2 * j + 2, :]).then_inc(S.b_hi, 1)

            def halve(s):
                act.wait_ge(S.y_added, t.up(S.y_added))
                fn(uh[:, 2 * s:2 * s + 2, :], merged[:, 2 * s:2 * s + 2, :], ACT.Copy, scale=0.5).then_inc(S.m_hi, 1)

            def merge(gates, last=False):
                for j in range(2):
                    for i in range(2):
                        yield from wait_steps(3)
                        src = next_pair()
                        act.wait_ge(S.pair_full, n.q)
                        if i == 0 and n.merged:
                            act.wait_ge(pair_free[(n.merged - 1) % 2], (n.merged - 1) // 2 + 1)
                        fn(gates[i][:], src, ACT.Tanh, scale=0.5).then_inc(pair_free[(n.q - 1) % 2], 1)
                        ahead()
                        yield
                    if last and j == 1:
                        halve(0)
                        halve(1)
                    for s in range(2):
                        yield from passed(2)
                        if last and j == 1:
                            halve(2 + s)
                    n.merged = n.q

            def merge_two():
                yield from merge(early)
                yield from merge(early)

            def ffn(conv, last=False):
                for step, third in FFN_STEPS:
                    i0 = sum(THIRDS[:third])
                    if step == "down":
                        if third == 2 and not last:
                            squares("residual")
                        else:
                            for _ in range(DC // 2):
                                finish(passed(1))
                        continue
                    for i in range(i0, i0 + THIRDS[third]):
                        if conv:
                            for part in range(2):
                                src = next_pair()
                                act.wait_ge(S.pair_full, n.q)
                                for c in range(2):
                                    ch = part * FC + 2 * i + c
                                    ins = fn(tmp[part][:, c, :], src[:, c, :], ACT.Copy, scale=fconv[:, 2, ch:ch + 1])
                                ins.then_inc(S.f_tap, 1)
                                ahead()
                            act.wait_ge(pair_free[(n.q - 2) % 2], (n.q - 2) // 2 + 1)
                            fn(tmp[0][:], tmp[0][:], ACT.Silu).then_inc(S.f_silu, 1)
                            act.wait_ge(S.f_mult, t.up(S.f_mult))
                        else:
                            src = next_pair()
                            act.wait_ge(S.pair_full, n.q)
                            fn(tmp[0][:], src, ACT.Silu).then_inc(pair_free[(n.q - 1) % 2], 1)
                            ahead()
                            next_pair()
                            ahead()
                            act.wait_ge(pair_free[(n.q - 1) % 2], (n.q - 1) // 2 + 1)
                        c = 2 * (i - i0)
                        nc.scalar.copy(fh[third % 2][:, c:c + 2, :], tmp[2][:]).then_inc(S.f_hi, 1)

            def side_core_1():
                for j in range(2):
                    yield from passed(4)
                    yield from passed(4)
                    yield from passed(4)
                    act.wait_ge(pair_free[(n.q - 1) % 2], (n.q - 1) // 2 + 1)
                    nc.scalar.copy(brh[1][:, 2 * j:2 * j + 2, :], tmp[3][:]).then_inc(S.b_hi, 1)
                for j in range(2):
                    yield from evict(sq[:, 2 * j:2 * j + 2, :], scale=HD ** -0.5)
                yield from passed(4)
                yield from passed(2)
                yield from evict(sv[:], P)

            def side_core_2():
                for j in range(5):
                    if j > 0:
                        act.wait_ge(pair_free[(n.q - 1) % 2], (n.q - 1) // 2 + 1)
                        logarithm(tmp[0][:], tmp[1][:])
                    yield
                    if j > 0:
                        inverse_root(tmp[0][:]).then_inc(S.r_root, 1)
                    yield
                    yield
                    src = next_pair()
                    if j == 4:
                        act.wait_ge(S.r_normed, t.up(S.r_normed))
                        ahead()
                        yield
                        break
                    act.wait_ge(S.pair_full, n.q)
                    fn(qk_pair[j], src, ACT.Copy)
                    if j > 0:
                        act.wait_ge(S.r_normed, t.up(S.r_normed))
                    fn(tmp[0][:], src, ACT.Square).then_inc(pair_free[(n.q - 1) % 2], 1)
                    if j == 0:
                        ahead()
                    yield
                    if j > 0:
                        next_pair()
                        yield
                    src = next_pair()
                    if j > 0:
                        act.wait_ge(S.rope_done, t.up(S.rope_done))
                    act.wait_ge(S.pair_full, n.q)
                    mean_square(tmp[1][:], src, 1.0 / HD, pair_free[(n.q - 1) % 2])
                    ahead()
                    yield
                yield from passed(1)
                yield from passed(1)
                yield from passed(1)
                yield from passed(4)
                yield from evict(av[:, :, 0:256], 256)
                yield from passed(1)
                yield from evict(av[:, :, 256:512], 256)
                act.wait_ge(S.rope_done, t.up(S.rope_done, 3))

            squares("input")
            norm()
            finish(passed(1))
            finish(passed(1))
            act.wait_ge(S.setup_done, 1)
            fn(sinT[:], tmp[3][:, 0, :], ACT.Sin)
            fn(cosT[:], tmp[3][:, 1, :], ACT.Sin)
            fn(small[:, 1:5], small[:, 11:15], ACT.Sigmoid)
            fn(small[:, 5:9], small[:, 15:19], ACT.Sigmoid).then_inc(S.trig_done, 1)
            finish(passed(1))
            finish(evict(gq[:, 0:2, :], scale=P ** -0.5))
            act.wait_ge(S.alpha_done, 1)
            for j in range(2):
                soft(X4[:, 2 * j:2 * j + 2, :], tmp[2 * j][:],
                     vec[:, V_GLAB + 2 * j:V_GLAB + 2 * j + 2]).then_inc(S.soft_done, 1)
                if j == 0:
                    finish(evict(gq[:, 2:4, :], scale=P ** -0.5))
            for j in range(2):
                finish(evict(gv[:, :, 256 * j:256 * j + 256], 256))
            core(1.0 / GLA_TAU, side_core_1(), SIDE_CORE_1)
            n.merged = 0
            side = merge_two()
            core_post(side, SIDE_POST_1)
            attention(lambda m: (max(m - 1, 0), m + 1), True, side, SIDE_WINDOW)
            n.merged = 0
            finish(merge(late, last=True))
            squares("residual")
            norm()
            ffn(True)
            norm(split=False)
            squares("normed")

            for l in range(LAYERS):
                norm()
                for j in range(2):
                    src = next_pair()
                    act.wait_ge(S.pair_full, n.q)
                    ahead()
                    ta, tb = tmp[2 * j], tmp[2 * j + 1]
                    if l == 0:
                        soft(src, ta[:])
                        fn(gk[:, 2 * j:2 * j + 2, :], src, ACT.Sigmoid, scale=-1.0).then_inc(S.soft_done, 1)
                    else:
                        fn(ta[:], src, ACT.Sigmoid)
                        fn(tb[:], src, ACT.Sigmoid, scale=-1.0).then_inc(S.soft_done, 1)
                        act.wait_ge(S.decay_up, t.up(S.decay_up))
                        fn(lg[:, 2 * j:2 * j + 2, :], ta[:], ACT.Ln).then_inc(S.ln_done, 1)
                    ahead()
                    src = next_pair()
                    act.wait_ge(S.pair_full, n.q)
                    fn(gq[:, 2 * j:2 * j + 2, :], src, ACT.Silu).then_inc(pair_free[(n.q - 1) % 2], 1)
                    ahead()
                for j in range(2):
                    finish(evict(gv[:, :, 256 * j:256 * j + 256], 256))
                core(1.0, side_core_2(), SIDE_CORE_2)
                n.merged = 0
                side = merge(early)
                indexed(1)
                indexed(2)
                core_post(side, SIDE_POST_2)
                attention(lambda m: (0, m + 1), False, side, SIDE_SPARSE)
                n.merged = 0
                finish(merge(late, last=True))
                squares("residual")
                norm()
                ffn(False, l + 1 == LAYERS)

        @block.vector
        def _(dve):
            t = Turns()
            n = Place()
            v = nc.vector

            def next_pair():
                n.q += 1
                return pair[(n.q - 1) % 2]

            def wait_steps(k):
                for _ in range(k):
                    yield

            def passed(steps):
                yield from wait_steps(steps - 1)
                next_pair()
                yield

            def low(dst, src, high, sem=S.dve_chain):
                v.tensor_tensor(dst, src, high.bitcast(F32), ALU.subtract).then_inc(sem, 1)
                dve.wait_ge(sem, t.up(sem))

            def norm(g, split=True):
                dve.wait_ge(S.n_root, t.up(S.n_root))
                v.reciprocal(tmp[2][:, 1, :], tmp[2][:, 0, :]).then_inc(S.dve_chain, 1)
                dve.wait_ge(S.dve_chain, t.up(S.dve_chain))

                def scaled(c):
                    dst = tmp[3][:, c % 2, :] if split else xT[:, c, :]
                    v.scalar_tensor_tensor(dst, xT[:, c, :], vec[:, g + c:g + c + 1], tmp[2][:, 1, :],
                                                  ALU.mult, ALU.mult).then_inc(S.n_normed, 1)
                    dve.wait_ge(S.n_normed, t.up(S.n_normed))

                if not split:
                    for c in range(DC):
                        scaled(c)
                    return
                scaled(0)
                for c in range(DC):
                    if c + 1 < DC:
                        scaled(c + 1)
                    dve.wait_ge(S.n_hi, t.up(S.n_hi))
                    low(ul[:, c, :], tmp[3][:, c % 2, :], uh[:, c, :], S.n_lo)

            def core(scale, side, total):
                v.memset(attT[:], 0.0).then_inc(S.dve_chain, 1)
                dve.wait_ge(S.dve_chain, t.up(S.dve_chain))
                decay = small[:, 20:22]

                def low_logs(u):
                    dve.wait_ge(S.lt_hi, t.up(S.lt_hi))
                    v.scalar_tensor_tensor(ltl[:, u % 2, :, :], X[0][:, 0:2 * P].rearrange("p (h f) -> p h f", h=2), scale,
                                           lth[:, u % 2, :, :].bitcast(F32), ALU.mult, ALU.subtract).then_inc(S.lt_lo, 1)

                low_logs(0)
                for u in range(CORE_UNITS):
                    m, hp = u // 2, u % 2
                    tok, heads = slice(m * P, (m + 1) * P), slice(2 * hp, 2 * hp + 2)
                    take_on(side, core_steps(total, u, 0))
                    dve.wait_ge(S.dec_done, t.up(S.dec_done, 2))
                    v.tensor_copy(decay, dec[:, :, LEVELS, P - 1]).then_inc(S.dve_chain, 1)
                    dve.wait_ge(S.dve_chain, t.up(S.dve_chain))
                    if u + 1 < CORE_UNITS:
                        low_logs(u + 1)
                    v.tensor_tensor(dec[:, :, LEVELS + 1, :], dec[:, :, LEVELS + 1, :], gk[:, heads, tok],
                                    ALU.mult).then_inc(S.kd_ready, 1)
                    v.tensor_tensor(dec[:, :, LEVELS, :], dec[:, :, LEVELS, :], gq[:, heads, tok], ALU.mult)
                    for l in range(LEVELS):
                        w = P >> (l + 1)
                        form = lambda x: x.rearrange("p h (g two w) -> p h g two w", two=2, w=w)
                        e, q, k = form(dec[:, :, l, :]), form(gq[:, heads, tok]), form(gk[:, heads, tok])
                        for part, x in ((1, q), (0, k)):
                            ins = v.tensor_tensor(e[:, :, :, part, :], e[:, :, :, part, :], x[:, :, :, part, :], ALU.mult)
                        ins.then_inc(S.lev_ready, 1)
                    take_on(side, core_steps(total, u, 1))
                    for l in range(LEVELS + 1):
                        if l == 6:
                            take_on(side, core_steps(total, u, 2))
                        if l % 2 == 0:
                            dve.wait_ge(S.att_done, t.up(S.att_done))
                        mask = pairmask[:, l, :].unsqueeze(1).to_broadcast([P, 2, P])
                        src = X[1 + l // 2 % 3][:, 2 * P * (l % 2):2 * P * (l % 2 + 1)].rearrange("p (h t) -> p h t", h=2)
                        signal = S.pairs_done if l % 2 else S.dve_chain
                        v.copy_predicated(attT[:], mask, src).then_inc(signal, 1)
                        dve.wait_ge(signal, t.up(signal))
                    take_on(side, core_steps(total, u, 3))
                    dve.wait_ge(S.out_done, t.up(S.out_done))
                    v.tensor_copy(gq[:, heads, tok], X[0][:, 0:2 * P].rearrange("p (h t) -> p h t", h=2)).then_inc(S.out_read, 1)
                    dve.wait_ge(S.kv_done, t.up(S.kv_done))
                    kv = X[1][:, 0:2 * P].rearrange("p (h f) -> p h f", h=2)
                    if m == 0:
                        v.tensor_copy(state[:, heads, :], kv).then_inc(S.state_done, 1)
                    else:
                        for i in range(2):
                            h = 2 * hp + i
                            ins = v.scalar_tensor_tensor(state[:, h, :], state[:, h, :], decay[:, i:i + 1], kv[:, i, :],
                                                         ALU.mult, ALU.add)
                        ins.then_inc(S.state_done, 1)
                    dve.wait_ge(S.state_done, t.up(S.state_done))
                    take_on(side, core_steps(total, u, 4))
                finish(side)

            def newton(x, y):
                v.tensor_tensor(tmp[3][:], tmp[3][:], x, ALU.mult).then_inc(S.dve_chain, 1)
                dve.wait_ge(S.dve_chain, t.up(S.dve_chain))
                v.scalar_tensor_tensor(tmp[3][:], tmp[3][:], 3.0, y, ALU.subtract, ALU.mult).then_inc(S.dve_chain, 1)
                dve.wait_ge(S.dve_chain, t.up(S.dve_chain))

            def core_post(g, same, side, side_steps, selection=None):
                for j in range(2):
                    if selection:
                        take_on(selection, SELECT_EARLY)
                    next_pair()
                    dve.wait_ge(S.g_root, t.up(S.g_root))
                    newton(tmp[1][:], tmp[2][:])
                    for i in range(2):
                        col = g if same else g + 2 * j + i
                        ins = v.scalar_tensor_tensor(tmp[3][:, i, :], gq[:, 2 * j + i, :], vech[:, col:col + 1],
                                                     tmp[3][:, i, :], ALU.mult, ALU.mult)
                    ins.then_inc(S.dve_chain, 1)
                    dve.wait_ge(S.dve_chain, t.up(S.dve_chain))
                    v.tensor_tensor(tmp[3][:], tmp[3][:], tmp[0][:], ALU.mult).then_inc(S.g_prod, 1)
                    dve.wait_ge(S.g_prod, t.up(S.g_prod))
                    dve.wait_ge(S.b_hi, t.up(S.b_hi))
                    low(brl[0][:, 2 * j:2 * j + 2, :], tmp[3][:], brh[0][:, 2 * j:2 * j + 2, :],
                        S.branch_ready if j else S.g_split)
                    take_on(side, side_steps[j])

            def attention(blocks, sink, side, side_steps, selection=None):
                steps = [(m, h) for m in range(NT) for h in range(AH)]
                dst = sq if sink else aq

                def front(i):
                    m, h = steps[i]
                    kk = (blocks(m)[1] - blocks(m)[0]) * P
                    st = stat[:, 8 * (i % 2):8 * (i % 2) + 8]
                    dve.wait_ge(S.qk_done, t.up(S.qk_done))
                    if sink:
                        v.scalar_tensor_tensor(logit[i % 2][:, 0:kk], dist[:, 2 * P - kk:2 * P], -SLOPES[h],
                                                      X[i % 2][:, 0:kk], ALU.mult, ALU.add).then_inc(S.logit_done, 1)
                        dve.wait_ge(S.logit_done, t.up(S.logit_done))
                        v.tensor_reduce(st[:, 0:1], logit[i % 2][:, 0:kk], AX, ALU.max).then_inc(S.dve_chain, 1)
                        dve.wait_ge(S.dve_chain, t.up(S.dve_chain))
                        v.tensor_scalar(st[:, 1:2], st[:, 0:1], sinks[:, h:h + 1], -1.0, ALU.max, ALU.mult).then_inc(S.negmax, 1)
                    else:
                        mask = hidden[:] if m == 0 else selected(m)
                        v.tensor_tensor_reduce(out=logit[i % 2][:, 0:kk], in0=X[i % 2][:, 0:kk], in1=mask, scale=1.0,
                                                      scalar=-TAKEN, op0=ALU.add, op1=ALU.min, accum_out=st[:, 1:2]).then_inc(S.logit_done, 1)
                        t.up(S.logit_done)

                def back(i):
                    m, h = steps[i]
                    kk = (blocks(m)[1] - blocks(m)[0]) * P
                    st = stat[:, 8 * (i % 2):8 * (i % 2) + 8]
                    dve.wait_ge(S.prob_done, t.up(S.prob_done))
                    if sink:
                        v.tensor_tensor(st[:, 2:3], st[:, 2:3], st[:, 3:4], ALU.add).then_inc(S.dve_chain, 1)
                        dve.wait_ge(S.dve_chain, t.up(S.dve_chain))
                    v.reciprocal(st[:, 4:5], st[:, 2:3]).then_inc(S.dve_chain, 1)
                    dve.wait_ge(S.dve_chain, t.up(S.dve_chain))
                    v.tensor_scalar(prob[i % 2][:, 0:kk], prob[i % 2][:, 0:kk], st[:, 4:5], None, ALU.mult).then_inc(S.scaled, 1)
                    dve.wait_ge(S.scaled, t.up(S.scaled))

                def out(i):
                    m, h = steps[i]
                    dve.wait_ge(S.pv_done, t.up(S.pv_done, 2))
                    v.tensor_copy(dst[:, h // 2, m * P:(m + 1) * P], X[3][:, 0:P]).then_inc(S.pv_read, 1)

                front(0)
                for i, (m, h) in enumerate(steps):
                    back(i)
                    rounds = share(*SELECT_LATE, i) if selection and m + 1 < NT else 0
                    if h == AH - 1:
                        take_on(selection, rounds)
                    if i + 1 < len(steps):
                        front(i + 1)
                    if i % 2 == 1 and i > 1:
                        out(i - 2)
                    if selection and i == 0:
                        score_keys(NT - 1)
                    if h < AH - 1:
                        take_on(selection, rounds)
                    take_on(side, share(side_steps[m], AH, h))
                out(len(steps) - 1)
                finish(side)
                for j in range(2):
                    dve.wait_ge(S.b_hi, t.up(S.b_hi))
                    low(brl[2][:, 2 * j:2 * j + 2, :], dst[:, 2 * j:2 * j + 2, :], brh[2][:, 2 * j:2 * j + 2, :],
                        S.branch_ready if j else S.dve_chain)

            def halve(s):
                dve.wait_ge(S.m_hi, t.up(S.m_hi))
                v.scalar_tensor_tensor(ul[:, 2 * s:2 * s + 2, :], merged[:, 2 * s:2 * s + 2, :], 0.5,
                                       uh[:, 2 * s:2 * s + 2, :].bitcast(F32), ALU.mult, ALU.subtract).then_inc(S.m_lo, 1)

            def merge(gates, first=False, last=False):
                for j in range(2):
                    yield from passed(4)
                    yield from passed(4)
                    dve.wait_ge(pair_free[(n.q - 2) % 2], (n.q - 2) // 2 + 1)
                    dve.wait_ge(pair_free[(n.q - 1) % 2], (n.q - 1) // 2 + 1)
                    if last and j == 1:
                        halve(0)
                        halve(1)
                    for s in range(2):
                        yield
                        src = next_pair()
                        dve.wait_ge(S.pair_full, n.q)
                        acc = merged[:, 4 * j + 2 * s:4 * j + 2 * s + 2, :]
                        dst = acc if first else tmp[3][:]
                        v.scalar_tensor_tensor(dst, gates[s][:], 1.0, src, ALU.add, ALU.mult).then_inc(pair_free[(n.q - 1) % 2], 1)
                        dve.wait_ge(pair_free[(n.q - 1) % 2], (n.q - 1) // 2 + 1)
                        if not first:
                            signal = S.y_added if last else S.dve_chain
                            v.tensor_tensor(acc, acc, tmp[3][:], ALU.add).then_inc(signal, 1)
                            dve.wait_ge(signal, t.up(signal))
                        if last and j == 1:
                            halve(2 + s)
                        yield

            def merge_two():
                yield from merge(early, first=True)
                yield from merge(early)

            def residual(squared=True):
                for s in range(DC // 2):
                    src = next_pair()
                    dve.wait_ge(S.pair_full, n.q)
                    x = xT[:, 2 * s:2 * s + 2, :]
                    if squared and s == DC // 2 - 1:
                        v.tensor_tensor(x[:, 0, :], x[:, 0, :], src[:, 0, :], ALU.add).then_inc(S.half_added, 1)
                        dve.wait_ge(S.half_added, t.up(S.half_added))
                        x, src = x[:, 1, :], src[:, 1, :]
                    v.tensor_tensor(x, x, src, ALU.add).then_inc(pair_free[(n.q - 1) % 2], 1)
                    dve.wait_ge(pair_free[(n.q - 1) % 2], (n.q - 1) // 2 + 1)

            def taps(y, x, w, ch):
                v.scalar_tensor_tensor(y[:, 1:T], x[:, 0:T - 1], w(1, ch), y[:, 1:T], ALU.mult, ALU.add).then_inc(S.dve_chain, 1)
                dve.wait_ge(S.dve_chain, t.up(S.dve_chain))
                return v.scalar_tensor_tensor(y[:, 2:T], x[:, 0:T - 2], w(0, ch), y[:, 2:T], ALU.mult, ALU.add)

            def ffn(conv, last=False):
                for step, third in FFN_STEPS:
                    i0 = sum(THIRDS[:third])
                    if step == "down":
                        residual(third == 2 and not last)
                        continue
                    for i in range(i0, i0 + THIRDS[third]):
                        if conv:
                            for part in range(2):
                                src = next_pair()
                                dve.wait_ge(S.pair_full, n.q)
                                dve.wait_ge(S.f_tap, t.up(S.f_tap))
                                w = lambda k, ch: fconv[:, k, ch:ch + 1]
                                for c in range(2):
                                    ins = taps(tmp[part][:, c, :], src[:, c, :], w, part * FC + 2 * i + c)
                                    if c == 0:
                                        ins.then_inc(S.dve_chain, 1)
                                        dve.wait_ge(S.dve_chain, t.up(S.dve_chain))
                                ins.then_inc(pair_free[(n.q - 1) % 2], 1)
                                dve.wait_ge(pair_free[(n.q - 1) % 2], (n.q - 1) // 2 + 1)
                            dve.wait_ge(S.f_silu, t.up(S.f_silu))
                            v.tensor_tensor(tmp[2][:], tmp[0][:], tmp[1][:], ALU.mult).then_inc(S.f_mult, 1)
                            dve.wait_ge(S.f_mult, t.up(S.f_mult))
                        else:
                            next_pair()
                            dve.wait_ge(pair_free[(n.q - 1) % 2], (n.q - 1) // 2 + 1)
                            src = next_pair()
                            dve.wait_ge(S.pair_full, n.q)
                            v.tensor_tensor(tmp[2][:], tmp[0][:], src, ALU.mult).then_inc(pair_free[(n.q - 1) % 2], 1)
                            dve.wait_ge(pair_free[(n.q - 1) % 2], (n.q - 1) // 2 + 1)
                        c = 2 * (i - i0)
                        dve.wait_ge(S.f_hi, t.up(S.f_hi))
                        low(fl[third % 2][:, c:c + 2, :], tmp[2][:], fh[third % 2][:, c:c + 2, :], S.f_lo)

            def cosine(x):
                k = x.shape[1]
                v.tensor_tensor(tmp[2][:, 0:k, :], x, cosT[:].unsqueeze(1).to_broadcast([P, k, T]), ALU.mult).then_inc(S.dve_chain, 1)
                dve.wait_ge(S.dve_chain, t.up(S.dve_chain))

            def turned(dst):
                k = dst.shape[1]
                src = next_pair()
                dve.wait_ge(S.pair_full, n.q)
                v.tensor_tensor(tmp[3][:, 0:k, :], src[:, 0:k, :], sinT[:].unsqueeze(1).to_broadcast([P, k, T]),
                                ALU.mult).then_inc(pair_free[(n.q - 1) % 2], 1)
                dve.wait_ge(pair_free[(n.q - 1) % 2], (n.q - 1) // 2 + 1)
                v.tensor_tensor(dst, tmp[2][:, 0:k, :], tmp[3][:, 0:k, :], ALU.add).then_inc(S.rope_done, 1)
                dve.wait_ge(S.rope_done, t.up(S.rope_done))

            def selected(m):
                return (bias1[:], bias2[:], bias3[:])[m - 1]

            def score_keys(m):
                sc = scores[m - 1]
                for j in range(2):
                    next_pair()
                    dve.wait_ge(pair_free[(n.q - 1) % 2], (n.q - 1) // 2 + 1)
                    for i in range(2):
                        r, wt = tmp[3][:, i, 0:(m + 1) * P], iw[:, m, 2 * j + i:2 * j + i + 1]
                        signal = S.i_scored if i else S.dve_chain
                        if i + j == 0:
                            v.tensor_scalar(sc, r, wt, None, ALU.mult).then_inc(signal, 1)
                        else:
                            v.scalar_tensor_tensor(sc, r, wt, sc, ALU.mult, ALU.add).then_inc(signal, 1)
                        dve.wait_ge(signal, t.up(signal))
                own = sc[:, m * P:]
                v.tensor_tensor(own, own, causal, ALU.add).then_inc(S.dve_chain, 1)
                dve.wait_ge(S.dve_chain, t.up(S.dve_chain))

            def select(m):
                sc = scores[m - 1]
                for r in range(TOPK // 8):
                    v.max(top8[:], sc).then_inc(S.dve_chain, 1)
                    dve.wait_ge(S.dve_chain, t.up(S.dve_chain))
                    v.match_replace(sc, top8[:], sc, TAKEN).then_inc(S.dve_chain, 1)
                    dve.wait_ge(S.dve_chain, t.up(S.dve_chain))
                    if r == TOPK // 8 - 1:
                        v.tensor_scalar(selected(m), sc, TAKEN / 3, -NEG, ALU.is_gt, ALU.mult).then_inc(S.dve_chain, 1)
                        dve.wait_ge(S.dve_chain, t.up(S.dve_chain))
                    yield

            def select_all():
                for m in range(1, NT):
                    yield from select(m)

            def side_core_1():
                w = lambda k, ch: vec[:, V_CONV + 4 * k + ch:V_CONV + 4 * k + ch + 1]
                for j in range(2):
                    yield from wait_steps(3)
                    src = next_pair()
                    dve.wait_ge(S.pair_full, n.q)
                    v.tensor_copy(tmp[0][:], src).then_inc(pair_free[(n.q - 1) % 2], 1)
                    dve.wait_ge(pair_free[(n.q - 1) % 2], (n.q - 1) // 2 + 1)
                    yield
                    yield from wait_steps(3)
                    src = next_pair()
                    dve.wait_ge(S.pair_full, n.q)
                    v.tensor_tensor(tmp[1][:], tmp[0][:], src, ALU.mult).then_inc(pair_free[(n.q - 1) % 2], 1)
                    dve.wait_ge(pair_free[(n.q - 1) % 2], (n.q - 1) // 2 + 1)
                    yield
                    for i in range(2):
                        v.tensor_scalar(tmp[2][:, i, :], tmp[1][:, i, :], w(2, 2 * j + i), None, ALU.mult).then_inc(S.dve_chain, 1)
                        dve.wait_ge(S.dve_chain, t.up(S.dve_chain))
                        taps(tmp[2][:, i, :], tmp[1][:, i, :], w, 2 * j + i).then_inc(S.dve_chain, 1)
                        dve.wait_ge(S.dve_chain, t.up(S.dve_chain))
                    yield from wait_steps(3)
                    src = next_pair()
                    dve.wait_ge(S.pair_full, n.q)
                    v.tensor_tensor(tmp[3][:], tmp[2][:], src, ALU.mult).then_inc(pair_free[(n.q - 1) % 2], 1)
                    dve.wait_ge(pair_free[(n.q - 1) % 2], (n.q - 1) // 2 + 1)
                    yield
                    dve.wait_ge(S.b_hi, t.up(S.b_hi))
                    low(brl[1][:, 2 * j:2 * j + 2, :], tmp[3][:], brh[1][:, 2 * j:2 * j + 2, :],
                        S.branch_ready if j else S.dve_chain)
                yield from passed(4)
                yield from passed(4)
                yield from wait_steps(3)
                src = next_pair()
                dve.wait_ge(S.pair_full, n.q)
                v.tensor_copy(sk[HD:P, 0, :], src[HD:P, 0, :])
                v.tensor_copy(sk[0:HD, 0, :], src[0:HD, 1, :])
                v.tensor_copy(sk[HD:P, 1, :], src[HD:P, 1, :]).then_inc(pair_free[(n.q - 1) % 2], 1)
                yield
                yield
                src = next_pair()
                dve.wait_ge(S.pair_full, n.q)
                v.tensor_copy(sk[0:HD, 1, :], src[0:HD, 0, :]).then_inc(pair_free[(n.q - 1) % 2], 1)
                yield
                yield from passed(4)

            def side_core_2(l):
                def normed(j):
                    g = small[:, 9 + l:10 + l] if j < 2 else vech[:, V_KN + l:V_KN + l + 1]
                    yield
                    yield
                    dve.wait_ge(S.r_root, t.up(S.r_root))
                    newton(tmp[1][:], tmp[0][:])
                    yield
                    v.scalar_tensor_tensor(qk_pair[j], qk_pair[j], g, tmp[3][:], ALU.mult, ALU.mult).then_inc(S.r_normed, 1)
                    dve.wait_ge(S.r_normed, t.up(S.r_normed))
                    cosine(qk_pair[j])

                for j in range(4):
                    yield from (normed(j - 1) if j > 0 else wait_steps(3))
                    next_pair()
                    yield
                    if j > 0:
                        turned(qk_pair[j - 1])
                        yield
                    next_pair()
                    yield
                yield from normed(3)
                src = next_pair()
                dve.wait_ge(S.pair_full, n.q)
                v.tensor_copy(iq[:], src).then_inc(pair_free[(n.q - 1) % 2], 1)
                dve.wait_ge(pair_free[(n.q - 1) % 2], (n.q - 1) // 2 + 1)
                yield
                turned(qk_pair[3])
                cosine(iq[:])
                yield
                src = next_pair()
                dve.wait_ge(S.pair_full, n.q)
                v.tensor_scalar(iw[:].rearrange("p m h -> p (m h)"), src[:, 0, 0:4 * NT], 1.0 / 16, None,
                                ALU.mult).then_inc(pair_free[(n.q - 1) % 2], 1)
                yield
                turned(iq[:])
                yield
                yield from wait_steps(3)
                src = next_pair()
                dve.wait_ge(S.pair_full, n.q)
                v.tensor_copy(ik[0:HD, :], src[0:HD, 0, :])
                v.tensor_copy(ik[HD:P, :], src[HD:P, 1, :]).then_inc(pair_free[(n.q - 1) % 2], 1)
                dve.wait_ge(pair_free[(n.q - 1) % 2], (n.q - 1) // 2 + 1)
                cosine(ik[:].unsqueeze(1))
                yield
                yield from passed(4)
                turned(ik[:].unsqueeze(1))
                yield
                yield from passed(4)

            v.memset(ones[:], 1.0).then_inc(S.dve_chain, 1)
            dve.wait_ge(S.dve_chain, t.up(S.dve_chain))
            v.memset(small[:, 0:1], EPS).then_inc(S.dve_chain, 1)
            dve.wait_ge(S.dve_chain, t.up(S.dve_chain))
            for c in range(DC):
                dve.wait_ge(S.x_T, t.up(S.x_T))
                v.tensor_copy(xT[:, c, :], X[c % 4]).then_inc(S.x_copied, 1)
                dve.wait_ge(S.x_copied, t.up(S.x_copied))
            dve.wait_ge(S.vec_T, t.up(S.vec_T))
            v.tensor_copy(fconv[:].rearrange("p k c -> p (k c)"), pair[0][:, 1, 0:6 * FC]).then_inc(S.dve_chain, 1)
            dve.wait_ge(S.dve_chain, t.up(S.dve_chain))
            v.tensor_copy(vec[:], pair[0][:, 0, 0:N_VEC]).then_inc(S.vec_ready, 1)
            dve.wait_ge(S.vec_ready, t.up(S.vec_ready))
            v.tensor_scalar(vech[:], vec[:], -0.5, None, ALU.mult).then_inc(S.dve_chain, 1)
            dve.wait_ge(S.dve_chain, t.up(S.dve_chain))

            norm(V_GMIX)
            for j in range(2):
                src = next_pair()
                dve.wait_ge(S.pair_full, n.q)
                v.tensor_copy(gk[:, 2 * j:2 * j + 2, :], src).then_inc(pair_free[(n.q - 1) % 2], 1)
                dve.wait_ge(pair_free[(n.q - 1) % 2], (n.q - 1) // 2 + 1)

            dve.wait_ge(S.masks_in, 32)
            v.tensor_copy(summask[:], mrow[:, 0:N_SUM * P]).then_inc(S.dve_chain, 1)
            dve.wait_ge(S.dve_chain, t.up(S.dve_chain))
            v.tensor_copy(pairmask[:].rearrange("p l t -> p (l t)"), mrow[:, N_SUM * P:]).then_inc(S.dve_chain, 1)
            dve.wait_ge(S.dve_chain, t.up(S.dve_chain))
            lb0, lb1 = vec[:, V_LB:V_LB + 4], vec[:, V_LB + 4:V_LB + 8]
            v.tensor_tensor(small[:, 11:15], lb1, lb0, ALU.subtract).then_inc(S.dve_chain, 1)
            dve.wait_ge(S.dve_chain, t.up(S.dve_chain))
            v.tensor_tensor(small[:, 15:19], lb0, lb1, ALU.subtract).then_inc(S.dve_chain, 1)
            dve.wait_ge(S.dve_chain, t.up(S.dve_chain))
            for l in range(LAYERS):
                v.tensor_scalar(small[:, 9 + l:10 + l], vech[:, V_QN + l:V_QN + l + 1], -HD ** -0.5, None, ALU.mult).then_inc(S.dve_chain, 1)
                dve.wait_ge(S.dve_chain, t.up(S.dve_chain))
            angle, turns = tmp[3][:, 0, :], tmp[3][:, 1, :]
            v.tensor_copy(tmp[2][:, 0, :], posi[:]).then_inc(S.dve_chain, 1)
            dve.wait_ge(S.dve_chain, t.up(S.dve_chain))
            v.tensor_scalar(angle, tmp[2][:, 0, :], const[:, K_INV:K_INV + 1], None, ALU.mult).then_inc(S.dve_chain, 1)
            dve.wait_ge(S.dve_chain, t.up(S.dve_chain))
            v.tensor_scalar(turns, angle, 1.0 / (2 * np.pi), MAGIC, ALU.mult, ALU.add).then_inc(S.dve_chain, 1)
            dve.wait_ge(S.dve_chain, t.up(S.dve_chain))
            v.tensor_scalar(turns, turns, MAGIC, None, ALU.subtract).then_inc(S.dve_chain, 1)
            dve.wait_ge(S.dve_chain, t.up(S.dve_chain))
            for part in TWO_PI:
                v.scalar_tensor_tensor(angle, turns, -part, angle, ALU.mult, ALU.add).then_inc(S.dve_chain, 1)
                dve.wait_ge(S.dve_chain, t.up(S.dve_chain))
            v.tensor_scalar(angle, angle, PI, -PI, ALU.min, ALU.max).then_inc(S.dve_chain, 1)
            dve.wait_ge(S.dve_chain, t.up(S.dve_chain))
            v.tensor_scalar(turns, angle, float(np.pi / 2), -2 * np.pi, ALU.is_gt, ALU.mult).then_inc(S.dve_chain, 1)
            dve.wait_ge(S.dve_chain, t.up(S.dve_chain))
            v.scalar_tensor_tensor(turns, angle, float(np.pi / 2), turns, ALU.add, ALU.add).then_inc(S.dve_chain, 1)
            dve.wait_ge(S.dve_chain, t.up(S.dve_chain))
            v.tensor_scalar(turns, turns, PI, -PI, ALU.min, ALU.max).then_inc(S.setup_done, 1)
            dve.wait_ge(S.setup_done, t.up(S.setup_done))
            src = next_pair()
            dve.wait_ge(S.pair_full, n.q)
            v.tensor_copy(gaT[:], src[0:RANK, 0, :]).then_inc(pair_free[(n.q - 1) % 2], 1)
            dve.wait_ge(pair_free[(n.q - 1) % 2], (n.q - 1) // 2 + 1)
            for _ in range(4):
                next_pair()
            dve.wait_ge(S.trig_done, t.up(S.trig_done))
            for j in range(2):
                dve.wait_ge(S.soft_done, t.up(S.soft_done))
                for i in range(2):
                    c = 2 * j + i
                    v.tensor_scalar(tmp[2 * j + 1][:, i, :], X[c], vec[:, V_GLAB + c:V_GLAB + c + 1], 0.0,
                                           ALU.add, ALU.min).then_inc(S.dve_chain, 1)
                    dve.wait_ge(S.dve_chain, t.up(S.dve_chain))
                signal = S.lg_ready if j else S.dve_chain
                v.tensor_tensor(lg[:, 2 * j:2 * j + 2, :], tmp[2 * j + 1][:], tmp[2 * j][:], ALU.subtract).then_inc(signal, 1)
                dve.wait_ge(signal, t.up(signal))
            core(1.0 / GLA_TAU, side_core_1(), SIDE_CORE_1)
            side = merge_two()
            core_post(V_GLAN, False, side, SIDE_POST_1)
            attention(lambda m: (max(m - 1, 0), m + 1), True, side, SIDE_WINDOW)
            finish(merge(late, last=True))
            residual()
            norm(V_GFFN)
            ffn(True)
            norm(V_GFIN, split=False)

            v.tensor_scalar(small[:, 1:5], small[:, 1:5], 2.0 ** -60, None, ALU.max).then_inc(S.dve_chain, 1)
            dve.wait_ge(S.dve_chain, t.up(S.dve_chain))
            for l in range(LAYERS):
                norm(V_NMIX + DC * l)
                for j in range(2):
                    src = next_pair()
                    dve.wait_ge(S.pair_full, n.q)
                    ta, tb = tmp[2 * j], tmp[2 * j + 1]
                    if l == 0:
                        dve.wait_ge(S.soft_done, t.up(S.soft_done))
                        v.tensor_scalar(tb[:], src, 0.0, None, ALU.min).then_inc(S.dve_chain, 1)
                        dve.wait_ge(S.dve_chain, t.up(S.dve_chain))
                        v.tensor_tensor(lg[:, 2 * j:2 * j + 2, :], tb[:], ta[:], ALU.subtract).then_inc(pair_free[(n.q - 1) % 2], 1)
                        dve.wait_ge(pair_free[(n.q - 1) % 2], (n.q - 1) // 2 + 1)
                    else:
                        dve.wait_ge(S.soft_done, t.up(S.soft_done))
                        for i in range(2):
                            c = 2 * j + i
                            lo, span = small[:, 1 + c:2 + c], small[:, 5 + c:6 + c]
                            signal = S.decay_up if i else S.dve_chain
                            v.tensor_scalar(ta[:, i, :], ta[:, i, :], span, lo, ALU.mult, ALU.add).then_inc(signal, 1)
                            dve.wait_ge(signal, t.up(signal))
                        for i in range(2):
                            c = 2 * j + i
                            span = small[:, 5 + c:6 + c]
                            ins = v.tensor_scalar(gk[:, c, :], tb[:, i, :], span, None, ALU.mult)
                            if i == 0:
                                ins.then_inc(S.dve_chain, 1)
                                dve.wait_ge(S.dve_chain, t.up(S.dve_chain))
                        ins.then_inc(pair_free[(n.q - 1) % 2], 1)
                        dve.wait_ge(pair_free[(n.q - 1) % 2], (n.q - 1) // 2 + 1)
                    next_pair()
                v.memset(small[:, 31:32], 0.0).then_inc(S.lg_ready, 1)
                dve.wait_ge(S.lg_ready, t.up(S.lg_ready))
                for _ in range(2):
                    next_pair()
                core(1.0, side_core_2(l), SIDE_CORE_2)
                side = merge(early, first=True)
                v.tensor_scalar(hidden[:], causal, -1.0, None, ALU.mult).then_inc(S.dve_chain, 1)
                dve.wait_ge(S.dve_chain, t.up(S.dve_chain))
                score_keys(1)
                score_keys(2)
                selection = select_all()
                core_post(V_HN + l, True, side, SIDE_POST_2, selection)
                attention(lambda m: (0, m + 1), False, side, SIDE_SPARSE, selection)
                finish(merge(late, last=True))
                residual()
                norm(V_NFFN + DC * l)
                ffn(False, l + 1 == LAYERS)

            for i in range(2 * NT):
                m, half = i // 2, i % 2
                dve.wait_ge(S.y_T, t.up(S.y_T))
                v.tensor_copy(xtok[:, m, MIX * half:MIX * (half + 1)], X[i % 4]).then_inc(S.y_out, 1)
                dve.wait_ge(S.y_out, t.up(S.y_out))


N_LOADS = 17
MAGIC = 1.5 * 2.0 ** 23
TWO_PI = (6.28125, 0.0019350051879882812, 3.0199159819304e-07)
PI = 3.1415925


def shape_constants():
    f = np.float32
    c = np.zeros((P, N_CONST), f)
    i = np.arange(P)
    c[:, K_ID:K_ID + P] = np.eye(P)
    c[:, K_BLK:K_BLK + P] = i[:, None] // HD == i[None, :] // HD
    half = HD // 2
    for o in range(P):
        if o % HD < half:
            c[o + half, K_ROT + o] = -1.0
        else:
            c[o - half, K_ROT + o] = 1.0
    c[:, K_CAUS:K_CAUS + P] = np.where(i[None, :] <= i[:, None], 0.0, NEG)
    d = P + i[:, None] - np.arange(2 * P)[None, :]
    c[:, K_DIST:K_DIST + 2 * P] = np.where((d >= 0) & (d < P), d, FAR)
    c[:, K_INV] = (10000.0 ** (-(2.0 * (i % half)) / HD)).astype(f)
    j, t = i[:, None], i[None, :]
    sums, pairs = [], []
    for l in range(LEVELS):
        w = P >> (l + 1)
        odd = (t // w) % 2 == 1
        start = (t // w) * w
        sums.append(np.where(odd, (j >= start) & (j <= t), (j > t) & (j < start + w)))
        pairs.append(((j // w) % 2 == 0) & (t // w == j // w + 1))
    sums += [j <= t, j > t]
    pairs.append(j == t)
    return c, np.concatenate(sums + pairs, 1).astype(f)


_INS = ['x', 'g_mix', 'w_in', 'gla_w_alpha', 'gla_b_alpha', 'gla_norm_g', 'conv_w', 'swa_sinks', 'w_gla_o',
        'w_conv_o', 'w_swa_o', 'w_o', 'g_ffn', 'w_up', 'ffn_conv_w', 'w_down', 'g_final', 'positions_2', 'w_in_2',
        'w_proj_attn_2', 'w_proj_hgrn_2', 'w_out_2', 'norm_mix_2', 'norm_ffn_2', 'q_norm_2', 'k_norm_2',
        'hgrn_norm_2', 'hgrn_lower_bound_2', 'w_ffn_in_2', 'w_ffn_out_2']


def kernel(**inputs):
    import concourse.bacc as bacc
    from concourse.bass_utils import run_bass_kernel_spmd

    nc = bacc.Bacc("TRN2", target_bir_lowering=False, num_devices=1)
    arrays, aps = {}, {}
    given = {name: np.ascontiguousarray(inputs[name]) for name in _INS}
    given.update(zip(("c_const", "c_masks"), shape_constants()))
    for name, x in given.items():
        arrays[f"in_{name}"] = x
        aps[name] = nc.dram_tensor(f"in_{name}", x.shape, mybir.dt.from_np(x.dtype), kind="ExternalInput").ap()
    out = nc.dram_tensor("out_0", (1, T, D), F32, kind="ExternalOutput").ap()
    build_program(nc, aps, out)
    r = run_bass_kernel_spmd(nc, [arrays], core_ids=[0])
    return r.results[0]["out_0"]
```
